# Optimizing a Trainium2 kernel written in Bass

```python
import functools
import jax, jax.numpy as jnp
from jax import lax
import numpy as np

D_MODEL = 1024
BATCH = 1
SEQ = 512
DEPTH = 1

DN_HEADS = 8
DN_HEAD_DIM = 128
DN_DIM = DN_HEADS * DN_HEAD_DIM
DN_CHUNK = 64
CONV_WIDTH = 4
SGU_GROUPS = 8
SGU_GROUP_DIM = 128
SGU_DIM = SGU_GROUPS * SGU_GROUP_DIM
SGU_CHUNK = 128
N_GROUPS = 4
EXPERTS_PER_GROUP = 4
N_EXPERTS = N_GROUPS * EXPERTS_PER_GROUP
TOP_K_IN_GROUP = 2
EXPERT_FF = 256
DEEPNORM_ALPHA = (2.0 * DEPTH) ** 0.25
DEEPNORM_BETA = (8.0 * DEPTH) ** -0.25
LN_EPS = 1e-5
NORM_EPS = 1e-6
PROJ_SIZES = (3 * DN_DIM, DN_DIM, DN_HEADS, DN_HEADS, 2 * SGU_DIM, D_MODEL, D_MODEL)
PROJ_DIM = sum(PROJ_SIZES)


def layer_norm(x, g, b):
    xf = x.astype(jnp.float32)
    xc = xf - jnp.mean(xf, axis=-1, keepdims=True)
    var = jnp.mean(xc * xc, axis=-1, keepdims=True)
    return (xc * lax.rsqrt(var + LN_EPS) * g + b).astype(x.dtype)

def l2_normalize(x):
    return x * lax.rsqrt(jnp.sum(x * x, axis=-1, keepdims=True) + NORM_EPS)

def causal_depthwise_conv(x, w):
    k = w.shape[0]
    return lax.conv_general_dilated(
        x, w[:, None, :], window_strides=(1,), padding=[(k - 1, 0)],
        dimension_numbers=("NWC", "WIO", "NWC"), feature_group_count=x.shape[-1])

def gated_delta_rule(q, k, v, g, beta):
    bsz, seq, heads, dk = q.shape
    dv = v.shape[-1]
    n = seq // DN_CHUNK

    def to_chunks(t):
        return jnp.swapaxes(t.reshape(bsz, n, DN_CHUNK, heads, *t.shape[3:]), 2, 3)

    q, k, v, g, beta = (to_chunks(t) for t in (q, k, v, g, beta))
    g_cum = jnp.cumsum(g, axis=-1)
    idx = jnp.arange(DN_CHUNK)
    causal = idx[:, None] >= idx[None, :]
    strict = idx[:, None] > idx[None, :]
    diff = g_cum[..., :, None] - g_cum[..., None, :]
    decay = jnp.where(causal, jnp.exp(jnp.where(causal, diff, 0.0)), 0.0)
    k_beta = k * beta[..., None]
    v_beta = v * beta[..., None]
    a_mat = jnp.where(strict, jnp.einsum("bnhtk,bnhsk->bnhts", k_beta, k) * decay, 0.0) \
        + jnp.eye(DN_CHUNK, dtype=q.dtype)
    solve = functools.partial(lax.linalg.triangular_solve, left_side=True, lower=True,
                              unit_diagonal=True)
    u = solve(a_mat, v_beta)
    w = solve(a_mat, k_beta * jnp.exp(g_cum)[..., None])
    qk = jnp.einsum("bnhtk,bnhsk->bnhts", q, k) * decay
    q_dec = q * jnp.exp(g_cum)[..., None]
    k_dec = k * jnp.exp(g_cum[..., -1:] - g_cum)[..., None]
    g_last = jnp.exp(g_cum[..., -1])

    def step(state, inp):
        qk_c, u_c, w_c, q_c, k_c, gl_c = inp
        v_new = u_c - jnp.einsum("bhtk,bhkv->bhtv", w_c, state)
        out = jnp.einsum("bhtk,bhkv->bhtv", q_c, state) + jnp.einsum("bhts,bhsv->bhtv", qk_c, v_new)
        state = state * gl_c[..., None, None] + jnp.einsum("bhsk,bhsv->bhkv", k_c, v_new)
        return state, out

    xs = tuple(jnp.moveaxis(t, 1, 0) for t in (qk, u, w, q_dec, k_dec, g_last))
    state0 = jnp.zeros((bsz, heads, dk, dv), jnp.float32)
    _, out = lax.scan(step, state0, xs)
    return jnp.transpose(out, (1, 0, 3, 2, 4)).reshape(bsz, seq, heads, dv)

def spatial_gating(uv, ln_g, ln_b, spatial_w, spatial_b, w_sgu_out):
    bsz, seq, _ = uv.shape
    n = seq // SGU_CHUNK
    u, v = jnp.split(jax.nn.gelu(uv, approximate=False), 2, axis=-1)
    v = layer_norm(v, ln_g, ln_b)
    v = v.reshape(bsz, n, SGU_CHUNK, SGU_GROUPS, SGU_GROUP_DIM)
    idx = jnp.arange(SGU_CHUNK)
    causal = idx[:, None] >= idx[None, :]
    w_causal = jnp.where(causal, spatial_w, 0)
    v = jnp.einsum("gts,bnsgc->bntgc", w_causal, v) + spatial_b.T[:, :, None]
    gated = u * v.reshape(bsz, seq, SGU_DIM)
    return jnp.einsum("blc,cd->bld", gated, w_sgu_out)

def hybrid_mixer(x, w_in, conv_w, a_log, dt_bias, dn_norm_g, w_dn_out,
                 sgu_ln_g, sgu_ln_b, spatial_w, spatial_b, w_sgu_out, w_out):
    bsz, seq, _ = x.shape
    f32 = jnp.float32
    proj = jnp.einsum("bld,dp->blp", x, w_in)
    offsets = np.cumsum(PROJ_SIZES)[:-1].tolist()
    qkv, z, a, b, uv, gate_dn, gate_sgu = jnp.split(proj, offsets, axis=-1)

    qkv = jax.nn.silu(causal_depthwise_conv(qkv, conv_w)).astype(f32)
    q, k, v = jnp.split(qkv, 3, axis=-1)
    to_heads = lambda t: t.reshape(bsz, seq, DN_HEADS, DN_HEAD_DIM)
    q = l2_normalize(to_heads(q)) * (DN_HEAD_DIM ** -0.5)
    k = l2_normalize(to_heads(k))
    v = to_heads(v)
    beta = jax.nn.sigmoid(b.astype(f32))
    g = -jnp.exp(a_log.astype(f32)) * jax.nn.softplus(a.astype(f32) + dt_bias.astype(f32))
    o = gated_delta_rule(q, k, v, g, beta)
    o = o * lax.rsqrt(jnp.mean(o * o, axis=-1, keepdims=True) + NORM_EPS) * dn_norm_g.astype(f32)
    o = o * jax.nn.silu(to_heads(z).astype(f32))
    y_dn = jnp.einsum("blc,cd->bld", o.reshape(bsz, seq, DN_DIM).astype(x.dtype), w_dn_out)

    y_sgu = spatial_gating(uv, sgu_ln_g, sgu_ln_b, spatial_w, spatial_b, w_sgu_out)

    y = jax.nn.sigmoid(gate_dn) * y_dn + jax.nn.sigmoid(gate_sgu) * y_sgu
    return jnp.einsum("bld,de->ble", y, w_out)

def hierarchical_moe(x, router_group_w, router_group_b, router_expert_w, router_expert_b,
                     expert_w_gate, expert_w_up, expert_w_down):
    bsz, seq, d = x.shape
    f32 = jnp.float32
    t = x.reshape(bsz * seq, d)
    n_tok = t.shape[0]
    group_logits = (t @ router_group_w + router_group_b).astype(f32)
    group_p, group_idx = lax.top_k(jax.nn.softmax(group_logits, axis=-1), 1)
    group_p, group_idx = group_p[:, 0], group_idx[:, 0]
    expert_logits = (t @ router_expert_w + router_expert_b).astype(f32)
    expert_logits = expert_logits.reshape(n_tok, N_GROUPS, EXPERTS_PER_GROUP)
    in_group = expert_logits[jnp.arange(n_tok), group_idx]
    exp_p, exp_idx = lax.top_k(jax.nn.softmax(in_group, axis=-1), TOP_K_IN_GROUP)
    exp_p = exp_p / jnp.sum(exp_p, axis=-1, keepdims=True)
    gate = group_p[:, None] * exp_p
    expert_id = group_idx[:, None] * EXPERTS_PER_GROUP + exp_idx
    combine = jnp.sum(jax.nn.one_hot(expert_id, N_EXPERTS, dtype=f32) * gate[..., None], axis=1)
    h = jax.nn.silu(jnp.einsum("td,edf->tef", t, expert_w_gate)) \
        * jnp.einsum("td,edf->tef", t, expert_w_up)
    h = h * combine[:, :, None].astype(h.dtype)
    y = jnp.einsum("tef,efd->td", h, expert_w_down)
    return y.reshape(bsz, seq, d)

def first_inputs(seed: int = 0) -> dict:
    key = jax.random.key(seed)
    ks = jax.random.split(key, 24)
    f32 = jnp.float32
    nrm = lambda k, shape, scale: jax.random.normal(k, shape, f32) * scale
    dt = jnp.exp(jax.random.uniform(ks[4], (DEPTH, DN_HEADS), f32,
                                    minval=float(np.log(1e-3)), maxval=float(np.log(1e-1))))
    return {
        "x": nrm(ks[0], (BATCH, SEQ, D_MODEL), 1.0),
        "w_in": nrm(ks[1], (DEPTH, D_MODEL, PROJ_DIM), D_MODEL ** -0.5),
        "conv_w": nrm(ks[2], (DEPTH, CONV_WIDTH, 3 * DN_DIM), CONV_WIDTH ** -0.5),
        "a_log": jnp.log(jax.random.uniform(ks[3], (DEPTH, DN_HEADS), f32, minval=1.0, maxval=16.0)),
        "dt_bias": dt + jnp.log(-jnp.expm1(-dt)),
        "dn_norm_g": 1.0 + nrm(ks[5], (DEPTH, DN_HEAD_DIM), 0.1),
        "w_dn_out": nrm(ks[6], (DEPTH, DN_DIM, D_MODEL), DN_DIM ** -0.5),
        "sgu_ln_g": 1.0 + nrm(ks[7], (DEPTH, SGU_DIM), 0.1),
        "sgu_ln_b": nrm(ks[8], (DEPTH, SGU_DIM), 0.02),
        "spatial_w": nrm(ks[9], (DEPTH, SGU_GROUPS, SGU_CHUNK, SGU_CHUNK), 0.05),
        "spatial_b": 1.0 + nrm(ks[10], (DEPTH, SGU_GROUPS, SGU_CHUNK), 0.1),
        "w_sgu_out": nrm(ks[11], (DEPTH, SGU_DIM, D_MODEL), SGU_DIM ** -0.5),
        "w_out": nrm(ks[12], (DEPTH, D_MODEL, D_MODEL), D_MODEL ** -0.5 * DEEPNORM_BETA),
        "ln1_g": 1.0 + nrm(ks[13], (DEPTH, D_MODEL), 0.1),
        "ln1_b": nrm(ks[14], (DEPTH, D_MODEL), 0.02),
        "router_group_w": nrm(ks[15], (DEPTH, D_MODEL, N_GROUPS), D_MODEL ** -0.5),
        "router_group_b": nrm(ks[16], (DEPTH, N_GROUPS), 0.01),
        "router_expert_w": nrm(ks[17], (DEPTH, D_MODEL, N_EXPERTS), D_MODEL ** -0.5),
        "router_expert_b": nrm(ks[18], (DEPTH, N_EXPERTS), 0.01),
        "expert_w_gate": nrm(ks[19], (DEPTH, N_EXPERTS, D_MODEL, EXPERT_FF), D_MODEL ** -0.5),
        "expert_w_up": nrm(ks[20], (DEPTH, N_EXPERTS, D_MODEL, EXPERT_FF), D_MODEL ** -0.5),
        "expert_w_down": nrm(ks[21], (DEPTH, N_EXPERTS, EXPERT_FF, D_MODEL), EXPERT_FF ** -0.5 * DEEPNORM_BETA),
        "ln2_g": 1.0 + nrm(ks[22], (DEPTH, D_MODEL), 0.1),
        "ln2_b": nrm(ks[23], (DEPTH, D_MODEL), 0.02),
    }

def first_block(x, w_in, conv_w, a_log, dt_bias, dn_norm_g, w_dn_out, sgu_ln_g, sgu_ln_b,
              spatial_w, spatial_b, w_sgu_out, w_out, ln1_g, ln1_b,
              router_group_w, router_group_b, router_expert_w, router_expert_b,
              expert_w_gate, expert_w_up, expert_w_down, ln2_g, ln2_b):
    h = x
    for l in range(DEPTH):
        mix = hybrid_mixer(h, w_in[l], conv_w[l], a_log[l], dt_bias[l], dn_norm_g[l], w_dn_out[l],
                           sgu_ln_g[l], sgu_ln_b[l], spatial_w[l], spatial_b[l], w_sgu_out[l], w_out[l])
        h = layer_norm(DEEPNORM_ALPHA * h + mix, ln1_g[l], ln1_b[l])
        ffn = hierarchical_moe(h, router_group_w[l], router_group_b[l], router_expert_w[l],
                               router_expert_b[l], expert_w_gate[l], expert_w_up[l], expert_w_down[l])
        h = layer_norm(DEEPNORM_ALPHA * h + ffn, ln2_g[l], ln2_b[l])
    return h


DEPTH_2 = 2

N_MIXERS = 2
BLOCK_Q = 128
EPS = 1e-6
FOX_HEADS = 16
FOX_HEAD_DIM = D_MODEL // FOX_HEADS
FOX_IN = 3 * D_MODEL + FOX_HEADS
FORGET_BIAS_INIT = 3.0
MLA_HEADS = 16
MLA_Q_RANK = 384
MLA_KV_RANK = 256
MLA_NOPE_DIM = 64
MLA_ROPE_DIM = 32
MLA_V_DIM = 64
MLA_QK_DIM = MLA_NOPE_DIM + MLA_ROPE_DIM
MLA_IN = MLA_Q_RANK + MLA_KV_RANK + MLA_ROPE_DIM
ROPE_THETA = 10000.0
N_EXPERTS_2 = N_GROUPS * EXPERTS_PER_GROUP
D_EXPERT = 256

N_FOX_LAYERS = (DEPTH_2 + 1) // 2
N_MLA_LAYERS = DEPTH_2 // 2


def rmsnorm(x, g):
    xf = x.astype(jnp.float32)
    y = xf * lax.rsqrt(jnp.mean(xf * xf, axis=-1, keepdims=True) + EPS)
    return (y * g.astype(jnp.float32)).astype(x.dtype)

def rope(x, positions):
    half = MLA_ROPE_DIM // 2
    inv_freq = ROPE_THETA ** (-jnp.arange(0, half, dtype=jnp.float32) / half)
    ang = positions.astype(jnp.float32)[..., None] * inv_freq
    cos = jnp.cos(ang)[:, :, None, :]
    sin = jnp.sin(ang)[:, :, None, :]
    xf = x.astype(jnp.float32)
    x1, x2 = xf[..., :half], xf[..., half:]
    out = jnp.concatenate([x1 * cos - x2 * sin, x1 * sin + x2 * cos], axis=-1)
    return out.astype(x.dtype)

def causal_block_attention(q, k, v, scale, cum=None):
    B, H, S, dk = q.shape
    nb = S // BLOCK_Q
    qb = q.reshape(B, H, nb, BLOCK_Q, dk).transpose(2, 0, 1, 3, 4)
    kpos = jnp.arange(S)

    def one_block(args):
        i, qi = args
        s = jnp.einsum('bhqd,bhkd->bhqk', qi, k).astype(jnp.float32) * scale
        if cum is not None:
            ci = lax.dynamic_slice_in_dim(cum, i * BLOCK_Q, BLOCK_Q, axis=2)
            s = s + ci[..., :, None] - cum[..., None, :]
        qpos = i * BLOCK_Q + jnp.arange(BLOCK_Q)
        mask = kpos[None, :] <= qpos[:, None]
        s = jnp.where(mask, s, -jnp.inf)
        p = jax.nn.softmax(s, axis=-1)
        return jnp.einsum('bhqk,bhkd->bhqd', p.astype(v.dtype), v)

    o = lax.map(one_block, (jnp.arange(nb), qb))
    return o.transpose(1, 2, 0, 3, 4).reshape(B, H, S, v.shape[-1])

def fox_mixer(h, w_in, b_f, q_norm, k_norm, w_out):
    B, S, D = h.shape
    proj = h @ w_in
    q = proj[..., :D].reshape(B, S, FOX_HEADS, FOX_HEAD_DIM)
    k = proj[..., D:2 * D].reshape(B, S, FOX_HEADS, FOX_HEAD_DIM)
    v = proj[..., 2 * D:3 * D].reshape(B, S, FOX_HEADS, FOX_HEAD_DIM)
    f_logit = proj[..., 3 * D:]
    q = rmsnorm(q, q_norm)
    k = rmsnorm(k, k_norm)
    log_f = jax.nn.log_sigmoid((f_logit + b_f).astype(jnp.float32))
    cum = jnp.cumsum(log_f, axis=1).transpose(0, 2, 1)
    o = causal_block_attention(q.transpose(0, 2, 1, 3), k.transpose(0, 2, 1, 3),
                               v.transpose(0, 2, 1, 3), FOX_HEAD_DIM ** -0.5, cum)
    o = o.transpose(0, 2, 1, 3).reshape(B, S, D)
    return o @ w_out

def mla_mixer(h, positions, w_in, q_lat_norm, kv_lat_norm, w_uq, w_ukv, q_norm, k_norm, w_out):
    B, S, D = h.shape
    proj = h @ w_in
    cq = rmsnorm(proj[..., :MLA_Q_RANK], q_lat_norm)
    ckv = rmsnorm(proj[..., MLA_Q_RANK:MLA_Q_RANK + MLA_KV_RANK], kv_lat_norm)
    k_rope = proj[..., MLA_Q_RANK + MLA_KV_RANK:]
    q = (cq @ w_uq).reshape(B, S, MLA_HEADS, MLA_QK_DIM)
    kv = (ckv @ w_ukv).reshape(B, S, MLA_HEADS, MLA_NOPE_DIM + MLA_V_DIM)
    k_nope, v = kv[..., :MLA_NOPE_DIM], kv[..., MLA_NOPE_DIM:]
    k = jnp.concatenate(
        [k_nope, jnp.broadcast_to(k_rope[:, :, None, :], (B, S, MLA_HEADS, MLA_ROPE_DIM))], axis=-1)
    q = rmsnorm(q, q_norm)
    k = rmsnorm(k, k_norm)
    q = jnp.concatenate([q[..., :MLA_NOPE_DIM], rope(q[..., MLA_NOPE_DIM:], positions)], axis=-1)
    k = jnp.concatenate([k[..., :MLA_NOPE_DIM], rope(k[..., MLA_NOPE_DIM:], positions)], axis=-1)
    o = causal_block_attention(q.transpose(0, 2, 1, 3), k.transpose(0, 2, 1, 3),
                               v.transpose(0, 2, 1, 3), MLA_QK_DIM ** -0.5)
    o = o.transpose(0, 2, 1, 3).reshape(B, S, MLA_HEADS * MLA_V_DIM)
    return o @ w_out

def hier_moe(h, w_grp, b_grp, w_rt, b_rt, w_gate, w_up, w_down):
    B, S, D = h.shape
    T = B * S
    t = h.reshape(T, D)
    g_logits = (t @ w_grp).astype(jnp.float32) + b_grp.astype(jnp.float32)
    g_prob = jax.nn.softmax(g_logits, axis=-1)
    g_top, g_idx = lax.top_k(g_prob, 1)
    e_logits = ((t @ w_rt).astype(jnp.float32) + b_rt.astype(jnp.float32)).reshape(
        T, N_GROUPS, EXPERTS_PER_GROUP)
    sel = jnp.broadcast_to(g_idx[:, :, None], (T, 1, EXPERTS_PER_GROUP))
    in_group = jnp.take_along_axis(e_logits, sel, axis=1)[:, 0]
    e_top, e_idx = lax.top_k(in_group, TOP_K_IN_GROUP)
    w = jax.nn.softmax(e_top, axis=-1) * g_top
    expert_id = g_idx * EXPERTS_PER_GROUP + e_idx
    combine = jnp.sum(jax.nn.one_hot(expert_id, N_EXPERTS_2, dtype=jnp.float32) * w[..., None], axis=1)
    a = jnp.einsum('td,edf->tef', t, w_gate)
    u = jnp.einsum('td,edf->tef', t, w_up)
    hidden = jax.nn.silu(a) * u * combine[..., None].astype(t.dtype)
    out = jnp.einsum('tef,efd->td', hidden, w_down)
    return out.reshape(B, S, D)

def second_inputs(seed: int = 0) -> dict:
    key = jax.random.key(seed)
    ks = jax.random.split(key, 32)
    D = D_MODEL
    nrm = lambda k, shape, scale: jax.random.normal(k, shape, jnp.float32) * scale
    gain = lambda k, shape: 1.0 + 0.02 * jax.random.normal(k, shape, jnp.float32)
    offsets = jax.random.randint(ks[2], (BATCH, 1), 0, 1024, dtype=jnp.int32)
    return {
        "x": nrm(ks[0], (BATCH, SEQ, D), 1.0),
        "c": nrm(ks[1], (BATCH, D), 1.0),
        "positions": offsets + jnp.arange(SEQ, dtype=jnp.int32)[None, :],
        "w_ada": nrm(ks[3], (DEPTH_2, D, 6 * D), 0.5 * D ** -0.5),
        "b_ada": nrm(ks[4], (DEPTH_2, 6 * D), 0.01),
        "mix_norm": gain(ks[5], (DEPTH_2, D)),
        "ffn_norm": gain(ks[6], (DEPTH_2, D)),
        "fox_w_in": nrm(ks[7], (N_FOX_LAYERS, D, FOX_IN), D ** -0.5),
        "fox_b_f": FORGET_BIAS_INIT + nrm(ks[8], (N_FOX_LAYERS, FOX_HEADS), 0.5),
        "fox_q_norm": gain(ks[9], (N_FOX_LAYERS, FOX_HEAD_DIM)),
        "fox_k_norm": gain(ks[10], (N_FOX_LAYERS, FOX_HEAD_DIM)),
        "fox_w_out": nrm(ks[11], (N_FOX_LAYERS, D, D), D ** -0.5),
        "mla_w_in": nrm(ks[12], (N_MLA_LAYERS, D, MLA_IN), D ** -0.5),
        "mla_q_lat_norm": gain(ks[13], (N_MLA_LAYERS, MLA_Q_RANK)),
        "mla_kv_lat_norm": gain(ks[14], (N_MLA_LAYERS, MLA_KV_RANK)),
        "mla_w_uq": nrm(ks[15], (N_MLA_LAYERS, MLA_Q_RANK, MLA_HEADS * MLA_QK_DIM), MLA_Q_RANK ** -0.5),
        "mla_w_ukv": nrm(ks[16], (N_MLA_LAYERS, MLA_KV_RANK, MLA_HEADS * (MLA_NOPE_DIM + MLA_V_DIM)),
                         MLA_KV_RANK ** -0.5),
        "mla_q_norm": gain(ks[17], (N_MLA_LAYERS, MLA_QK_DIM)),
        "mla_k_norm": gain(ks[18], (N_MLA_LAYERS, MLA_QK_DIM)),
        "mla_w_out": nrm(ks[19], (N_MLA_LAYERS, MLA_HEADS * MLA_V_DIM, D), (MLA_HEADS * MLA_V_DIM) ** -0.5),
        "moe_w_grp": nrm(ks[20], (DEPTH_2, D, N_GROUPS), D ** -0.5),
        "moe_b_grp": nrm(ks[21], (DEPTH_2, N_GROUPS), 0.01),
        "moe_w_rt": nrm(ks[22], (DEPTH_2, D, N_EXPERTS_2), D ** -0.5),
        "moe_b_rt": nrm(ks[23], (DEPTH_2, N_EXPERTS_2), 0.01),
        "moe_w_gate": nrm(ks[24], (DEPTH_2, N_EXPERTS_2, D, D_EXPERT), D ** -0.5),
        "moe_w_up": nrm(ks[25], (DEPTH_2, N_EXPERTS_2, D, D_EXPERT), D ** -0.5),
        "moe_w_down": nrm(ks[26], (DEPTH_2, N_EXPERTS_2, D_EXPERT, D), D_EXPERT ** -0.5),
    }

def second_block(x, c, positions, w_ada, b_ada, mix_norm, ffn_norm,
              fox_w_in, fox_b_f, fox_q_norm, fox_k_norm, fox_w_out,
              mla_w_in, mla_q_lat_norm, mla_kv_lat_norm, mla_w_uq, mla_w_ukv, mla_q_norm, mla_k_norm,
              mla_w_out,
              moe_w_grp, moe_b_grp, moe_w_rt, moe_b_rt, moe_w_gate, moe_w_up, moe_w_down):
    c_act = jax.nn.silu(c)
    for i in range(DEPTH_2):
        mod = c_act @ w_ada[i] + b_ada[i]
        sh1, sc1, g1, sh2, sc2, g2 = [m[:, None, :] for m in jnp.split(mod, 6, axis=-1)]
        h = rmsnorm(x, mix_norm[i]) * (1.0 + sc1) + sh1
        j = i // N_MIXERS
        if i % N_MIXERS == 0:
            y = fox_mixer(h, fox_w_in[j], fox_b_f[j], fox_q_norm[j], fox_k_norm[j], fox_w_out[j])
        else:
            y = mla_mixer(h, positions, mla_w_in[j], mla_q_lat_norm[j], mla_kv_lat_norm[j],
                          mla_w_uq[j], mla_w_ukv[j], mla_q_norm[j], mla_k_norm[j], mla_w_out[j])
        x = x + g1 * y
        h = rmsnorm(x, ffn_norm[i]) * (1.0 + sc2) + sh2
        x = x + g2 * hier_moe(h, moe_w_grp[i], moe_b_grp[i], moe_w_rt[i], moe_b_rt[i],
                              moe_w_gate[i], moe_w_up[i], moe_w_down[i])
    return x


def setup_inputs(seed=0):
    out = dict(first_inputs(seed))
    for name, value in second_inputs(seed + 1).items():
        if name != "x":
            out[name + "_2"] = value
    return out


def reference(
    x, w_in, conv_w, a_log, dt_bias, dn_norm_g, w_dn_out, sgu_ln_g, sgu_ln_b, spatial_w,
    spatial_b, w_sgu_out, w_out, ln1_g, ln1_b, router_group_w, router_group_b, router_expert_w,
    router_expert_b, expert_w_gate, expert_w_up, expert_w_down, ln2_g, ln2_b, c_2, positions_2,
    w_ada_2, b_ada_2, mix_norm_2, ffn_norm_2, fox_w_in_2, fox_b_f_2, fox_q_norm_2, fox_k_norm_2,
    fox_w_out_2, mla_w_in_2, mla_q_lat_norm_2, mla_kv_lat_norm_2, mla_w_uq_2, mla_w_ukv_2,
    mla_q_norm_2, mla_k_norm_2, mla_w_out_2, moe_w_grp_2, moe_b_grp_2, moe_w_rt_2, moe_b_rt_2,
    moe_w_gate_2, moe_w_up_2, moe_w_down_2,
):
    x = first_block(
        x, w_in, conv_w, a_log, dt_bias, dn_norm_g, w_dn_out, sgu_ln_g, sgu_ln_b, spatial_w,
        spatial_b, w_sgu_out, w_out, ln1_g, ln1_b, router_group_w, router_group_b,
        router_expert_w, router_expert_b, expert_w_gate, expert_w_up, expert_w_down, ln2_g,
        ln2_b,
    )
    return second_block(
        x, c_2, positions_2, w_ada_2, b_ada_2, mix_norm_2, ffn_norm_2, fox_w_in_2, fox_b_f_2,
        fox_q_norm_2, fox_k_norm_2, fox_w_out_2, mla_w_in_2, mla_q_lat_norm_2,
        mla_kv_lat_norm_2, mla_w_uq_2, mla_w_ukv_2, mla_q_norm_2, mla_k_norm_2, mla_w_out_2,
        moe_w_grp_2, moe_b_grp_2, moe_w_rt_2, moe_b_rt_2, moe_w_gate_2, moe_w_up_2,
        moe_w_down_2,
    )


_drawn_inputs = setup_inputs


def setup_inputs(seed=0):
    import zlib

    import numpy as np

    out = dict(_drawn_inputs(seed))
    spreads = {}
    factors = {'sgu_ln_g': 3.916,
     'sgu_ln_b': 8.0,
     'router_group_b': 8.0,
     'router_expert_b': 8.0,
     'b_ada_2': 3.686,
     'mix_norm_2': 8.0,
     'ffn_norm_2': 3.396,
     'fox_q_norm_2': 8.0,
     'fox_k_norm_2': 8.0,
     'mla_q_lat_norm_2': 8.0,
     'mla_kv_lat_norm_2': 8.0,
     'mla_q_norm_2': 8.0,
     'mla_k_norm_2': 8.0,
     'moe_b_grp_2': 7.414,
     'moe_b_rt_2': 8.0}
    for name, (base, spread) in spreads.items():
        noise = np.random.default_rng([zlib.crc32(name.encode()), seed]).standard_normal(out[name].shape)
        drawn = base * np.exp(spread * noise) if base else spread * noise
        out[name] = __import__('jax').numpy.asarray(drawn.astype(out[name].dtype))
    for name, factor in factors.items():
        out[name] = (out[name] * factor).astype(out[name].dtype)
    return out
```

```python
from contextlib import ExitStack

import concourse.bass as bass
from concourse import mybir

ALU = mybir.AluOpType
ACT = mybir.ActivationFunctionType
F32 = mybir.dt.float32
I32 = mybir.dt.int32
X_AXIS = mybir.AxisListType.X

P = 128
BANK = 512
N_BANKS = 8
RING = 4
SLOT = 4096


class Steps:

    def __init__(self, sem):
        self.sem, self.made, self.at, self.due = sem, 0, 0, 0

    def begin(self, names, rounds=1):
        assert self.at == self.due, "a stage's steps have all been made"
        self.names, self.rounds, self.base, self.at = list(names), rounds, self.made, 0
        assert len(set(self.names)) == len(self.names)
        self.made += len(self.names) * rounds
        self.due = len(self.names) * rounds

    def value(self, name, i=0):
        return i * len(self.names) + (self.base + self.names.index(name) + 1)

    def done(self, ins, name):
        assert self.names[self.at % len(self.names)] == name, (name, self.names[self.at % len(self.names)])
        self.at += 1
        ins.then_inc(self.sem, 1)

    def wait(self, eng, name, i=0):
        eng.wait_ge(self.sem, self.value(name, i))


class Weights:

    def __init__(self, ring, landed):
        self.ring, self.landed = ring, landed
        self.chunks, self.slots, self.ready, self.used = [], [], [], {}
        self.count = [0] * RING
        self.issued = self.taken = 0
        self.turn = 1

    def plan(self, parts, slot=None, by_loop=False):
        if slot is None:
            self.turn = 1 - self.turn
            slot = self.turn
        self.chunks.append(parts)
        self.slots.append(slot)
        self.count[slot] += 16 * len(parts)
        if by_loop:
            self.chunks[-1] = None
        self.ready.append(self.count[slot])

    def take(self, n):
        first = self.taken
        self.taken += n
        return range(first, first + n)

    def slot(self, chunk):
        return self.ring[self.slots[chunk]]

    def wait_landed(self, eng, chunk):
        eng.wait_ge(self.landed[self.slots[chunk]], self.ready[chunk])

    def mark_used(self, chunk, sem, value):
        self.used[chunk] = (sem, value)

    def before(self, chunk):
        older = [c for c in range(chunk) if self.slots[c] == self.slots[chunk]]
        return older[-1] if older else None

    def issue(self, sp):
        while self.issued < len(self.chunks) and self.chunks[self.issued] is not None:
            old = self.before(self.issued)
            if old is not None:
                if old not in self.used:
                    return
                sp.wait_ge(*self.used[old])
            for dst, src in self.chunks[self.issued]:
                sp.dma_start(dst(self.slot(self.issued)), src).then_inc(self.landed[self.slots[self.issued]], 16)
            self.issued += 1


def build(nc, D, OUT, stop=None):
    S, DM = D["x"].shape[1], D["x"].shape[2]
    T = S // P
    KD = DM // P
    H = D["a_log"].shape[1]
    CONV = D["conv_w"].shape[1]
    DN = H * D["dn_norm_g"].shape[1]
    SG = D["spatial_w"].shape[1]
    GD_OFF = 4 * DN + 2 * H + 2 * SG * P
    UV_OFF = 4 * DN + 2 * H
    NG = D["router_group_w"].shape[2]
    NE = D["router_expert_w"].shape[2]
    PER = NE // NG
    FF = D["expert_w_gate"].shape[3]
    KF = FF // P
    LN_EPS, EPS = 1e-5, 1e-6
    ALPHA = 2.0 ** 0.25

    ctx = ExitStack()
    with ctx:
        def sb(name, shape, dt=F32):
            return ctx.enter_context(nc.sbuf_tensor(name, shape, dt))

        def sem(name):
            return ctx.enter_context(nc.semaphore(name))

        bank = [ctx.enter_context(nc.psum_tensor(f"bank{i}", [P, BANK], F32)) for i in range(N_BANKS)]
        ident = sb("ident", [P, P])
        tri = sb("tri", [P, P])
        strict = sb("strict", [P, P])
        ones = sb("ones", [P, P])
        level_mask = sb("level_mask", [P, 7, P])
        resid = sb("resid", [P, T, DM])
        featT = sb("featT", [P, KD, S])
        ring = [sb(f"ring{i}", [P, SLOT if i < 2 else SLOT // 2]) for i in range(RING)]
        work = sb("work", [P, 7 * 4096])
        buf = [work[:, i * 4096:(i + 1) * 4096] for i in range(7)]
        state = sb("state", [P, H * P])
        ada_w = [state, sb("ada_w", [P, KD * P])]
        small = sb("small", [P, 512])
        ismall = sb("ismall", [P, 64], I32)

        def tok(b):
            return b[:, :].rearrange("p (t n) -> p t n", t=T)

        def cols(a, n):
            return a

        def bcast(ap, *shape):
            return ap.to_broadcast(list(shape))

        N_MAIN, N_EXTRA = NE, (2 * S - NE) // P
        ROWS = (N_MAIN + N_EXTRA) * P
        x_rows = nc.dram_tensor("x_rows", [ROWS, DM], F32, kind="Internal").ap()
        y_rows = nc.dram_tensor("y_rows", [ROWS, DM], F32, kind="Internal").ap()
        ada_part = nc.dram_tensor("ada_part", [2, P, 6 * DM], F32, kind="Internal").ap()

        PE, AC, DV, PO = (Steps(sem(n)) for n in ("pe_steps", "act_steps", "dve_steps", "pool_steps"))
        loaded = sem("loaded")
        loads = [0]
        W = Weights(ring, [sem(f"slot{i}_landed") for i in range(RING)])

        def load(eng, dst, src):
            eng.dma_start(dst, src).then_inc(loaded, 16)
            loads[0] += 16

        def wait_loads(eng):
            eng.wait_ge(loaded, loads[0])

        def rows(w):
            return w.rearrange("(k p) n -> p k n", p=P)

        def plan_cols(w, lo, hi, step=BANK):
            k = w.shape[0] // P
            for c in range(lo, hi, step):
                n = min(step, hi - c)
                W.plan([(lambda s, k=k, n=n: s[:, 0:k * n].rearrange("p (k n) -> p k n", k=k), rows(w)[:, :, c:c + n])])  

        def plan_experts(gate, up, down):
            for e in range(NE):
                gu = [(lambda s, i=i: s[:, :].rearrange("p (k g n) -> p k g n", k=KD, g=2)[:, :, i, :], rows(w[e]))
                      for i, w in enumerate((gate, up))]
                dn = [(lambda s: s[:, 0:KF * DM].rearrange("p (k n) -> p k n", k=KF), rows(down[e]))]
                W.plan(gu, e % 2, by_loop=e >= 2)
                W.plan(dn, 2 + e % 2, by_loop=e >= 2)

        w_in = D["w_in"][0]
        plan_cols(w_in, UV_OFF, UV_OFF + 2 * SG * P)
        plan_cols(w_in, GD_OFF + DM, GD_OFF + 2 * DM)
        plan_cols(D["w_sgu_out"][0], 0, DM)
        plan_cols(w_in, 0, 3 * DN)
        plan_cols(w_in, 3 * DN, 4 * DN)
        plan_cols(w_in, GD_OFF, GD_OFF + DM)
        plan_cols(D["w_dn_out"][0], 0, DM)
        plan_cols(D["w_out"][0], 0, DM)
        plan_experts(D["expert_w_gate"][0], D["expert_w_up"][0], D["expert_w_down"][0])
        plan_cols(D["fox_w_in_2"][0], 0, 3 * DM)
        plan_cols(D["fox_w_out_2"][0], 0, DM)
        plan_experts(D["moe_w_gate_2"][0], D["moe_w_up_2"][0], D["moe_w_down_2"][0])
        plan_cols(D["mla_w_in_2"][0], 0, D["mla_w_in_2"].shape[2])
        plan_cols(D["mla_w_uq_2"][0], 0, D["mla_w_uq_2"].shape[2])
        plan_cols(D["mla_w_ukv_2"][0], 0, D["mla_w_ukv_2"].shape[2])
        plan_cols(D["mla_w_out_2"][0], 0, DM)
        plan_experts(D["moe_w_gate_2"][1], D["moe_w_up_2"][1], D["moe_w_down_2"][1])

        def stage(pe=(), act=(), dve=(), pool=(), rounds=1):
            for s, names in ((PE, pe), (AC, act), (DV, dve), (PO, pool)):
                s.begin(names, rounds)

        def transpose_stage(src, dst, prep_names=(), prep=None, ready=None, dma=None, blocks=KD):
            names = prep_names or {}
            tiles = range(T)
            pe_n = [("turned", t, h) for t in tiles for h in range(2)]
            ac_n = [n + (t,) for t in tiles for n in names.get("act", [])] + [("kept", t, 0) for t in tiles]
            dv_n = [n + (t,) for t in tiles for n in names.get("dve", [])] + [("kept", t, 1) for t in tiles]
            po_n = [n + (t,) for t in tiles for n in names.get("pool", [])]
            stage(pe_n, ac_n, dv_n, po_n)
            with nc.Block() as block:
                @block.tensor
                def _(pe):
                    for t in tiles:
                        if ready:
                            ready[0].wait(pe, ready[1] + (t,))
                        for h in range(2):
                            b = bank[2 * t + h]
                            for j in range(min(4, blocks - 4 * h)):
                                k = 4 * h + j
                                last = nc.tensor.transpose(b[:, j * P:(j + 1) * P], src[:, t, k * P:(k + 1) * P], ident[:, :])
                            PE.done(last, ("turned", t, h))

                def keep(eng, S_, copy, h):
                    for t in tiles:
                        PE.wait(eng, ("turned", t, h))
                        m = min(4, blocks - 4 * h)
                        S_.done(copy(dst[:, 4 * h:4 * h + m, t * P:(t + 1) * P],
                                     bank[2 * t + h][:, 0:m * P].rearrange("p (j n) -> p j n", j=m)), ("kept", t, h))

                @block.scalar
                def _(act):
                    if prep:
                        for t in tiles:
                            prep("act", act, t)
                    keep(act, AC, lambda o, i: nc.scalar.activation(o, i, ACT.Copy), 0)

                @block.vector
                def _(dve):
                    if prep:
                        for t in tiles:
                            prep("dve", dve, t)
                    keep(dve, DV, lambda o, i: nc.vector.tensor_copy(o, i), 1)

                @block.gpsimd
                def _(pool):
                    if prep:
                        for t in tiles:
                            prep("pool", pool, t)

                @block.sync
                def _(sp):
                    if dma:
                        dma(sp)
                    W.issue(sp)

        ada_landed, ada_stored = ([sem(f"ada_{what}{i}") for i in range(2)] for what in ("landed", "stored"))
        PIECES = 6 * DM // P
        ada_done = [0]

        def load_piece(eng, i):
            w = rows(D["w_ada_2"][i // PIECES])[:, :, (i % PIECES) * P:(i % PIECES + 1) * P]
            eng.dma_start(ada_w[i % 2][:, :].rearrange("p (k n) -> p k n", k=KD), w).then_inc(ada_landed[i % 2], 16)

        def store_piece(eng, i):
            q = i % PIECES
            eng.dma_start(ada_part[i // PIECES, :, q * P:(q + 1) * P], ada_w[i % 2][:, 0:P]).then_inc(ada_stored[i % 2], 16)

        def project(srcT, kblocks, widths, by, drain, mids=0, pieces=0):
            ids = W.take(len(widths))
            jobs = [(n, t) for n in range(len(widths)) for t in range(T)]
            drains = [(kind, n, t) for n, t in jobs for kind in ["mid%d" % m for m in range(mids)] + ["drained"]]
            beside = range(ada_done[0], ada_done[0] + pieces)
            ada_done[0] += pieces
            stage([("sum", n, t) for n, t in jobs], drains if by == "act" else (),
                  drains if by == "dve" else [("piece", i, m) for i in beside for m in range(4)])
            taker = AC if by == "act" else DV
            with nc.Block() as block:
                @block.tensor
                def _(pe):
                    for n, width in enumerate(widths):
                        W.wait_landed(pe, ids[n])
                        w = W.slot(ids[n])[:, 0:kblocks * width].rearrange("p (k n) -> p k n", k=kblocks)
                        for t in range(T):
                            j = n * T + t
                            if j >= N_BANKS:
                                taker.wait(pe, ("drained",) + jobs[j - N_BANKS])
                            b = bank[j % N_BANKS]
                            for k in range(kblocks):
                                last = nc.tensor.matmul(b[:, 0:width], srcT[:, k, t * P:(t + 1) * P], w[:, k, :],
                                                        start=(k == 0), stop=(k == kblocks - 1))
                            PE.done(last, ("sum", n, t))
                        W.mark_used(ids[n], PE.sem, PE.value(("sum", n, T - 1)))

                def take_away(eng):
                    moved = 0

                    def move_piece(k):
                        i = beside[0] + k
                        if k < pieces:
                            if i >= 2:
                                eng.wait_ge(ada_stored[i % 2], 16 * (i // 2))
                            load_piece(eng, i)
                        if k:
                            DV.wait(eng, ("piece", i - 1, 3))
                            store_piece(eng, i - 1)
                    for j, (n, t) in enumerate(jobs):
                        m = [0]

                        def mid(ins):
                            taker.done(ins, ("mid%d" % m[0], n, t))
                            taker.wait(eng, ("mid%d" % m[0], n, t))
                            m[0] += 1
                        while pieces and moved <= pieces and moved * len(jobs) <= (pieces + 1) * j:
                            move_piece(moved)
                            moved += 1
                        if mids and j:
                            taker.wait(eng, ("drained",) + jobs[j - 1])
                        PE.wait(eng, ("sum", n, t))
                        taker.done(drain(n, t, bank[j % N_BANKS], mid), ("drained", n, t))
                    while pieces and moved <= pieces:
                        move_piece(moved)
                        moved += 1
                    if pieces:
                        for i in beside[-2:]:
                            eng.wait_ge(ada_stored[i % 2], 16 * (i // 2 + 1))

                @block.scalar
                def _(act):
                    if by == "act":
                        take_away(act)

                @block.vector
                def _(dve):
                    if by == "dve":
                        take_away(dve)
                    for i in beside if by == "act" else ():
                        w = ada_w[i % 2][:, :].rearrange("p (k n) -> p k n", k=KD)
                        dve.wait_ge(ada_landed[i % 2], 16 * (i // 2 + 1))
                        DV.done(nc.vector.tensor_tensor(w, w, bcast(c_cols.unsqueeze(2), P, KD, P), ALU.mult), ("piece", i, 0))
                        for m in range(1, 4):
                            DV.wait(dve, ("piece", i, m - 1))
                            n = KD >> m
                            DV.done(nc.vector.tensor_tensor(w[:, 0:n, :], w[:, 0:n, :], w[:, n:2 * n, :], ALU.add), ("piece", i, m))

                @block.sync
                def _(sp):
                    W.issue(sp)

        def chain(steps, eng, name):
            n = [0]

            def link(ins):
                steps.done(ins, (name, n[0]))
                steps.wait(eng, (name, n[0]))
                n[0] += 1
            return link

        def links(name, n):
            return [(name, i) for i in range(n)]

        def span(t, half=BANK):
            return slice(t * half, (t + 1) * half)

        x_tok = D["x"][0].rearrange("(t p) n -> p t n", p=P)
        NCR = CONV * 3 * DN // P
        conv_rows = buf[5][0:NCR + SG, 0:P]
        sp_nat = buf[2][:, 2048:3072].rearrange("p (g s) -> p g s", g=SG)
        spT = buf[2][:, 3072:4096].rearrange("p (g t) -> p g t", g=SG)
        sp_bias = small[:, 16 + NCR:16 + NCR + SG]
        conv_cols = small[:, 16:16 + CONV * 3 * DN // P].rearrange("p (w b) -> p w b", w=CONV)
        ab_w = buf[6][:, 0:KD * 2 * H].rearrange("p (k n) -> p k n", k=KD)
        NL = 7
        c_rows = buf[5][0:KD, P:2 * P]
        c_cols = ismall[:, 48:48 + KD].bitcast(F32)
        stage(dve=links("zero", 1), pool=links("const", 6 + 3 * NL))
        with nc.Block() as block:
            @block.sync
            def _(sp):
                load(sp, resid[:, :, :], x_tok)
                load(sp, c_rows, D["c_2"][0].rearrange("(k p) -> k p", p=P))
                load(sp, sp_nat, D["spatial_w"][0].rearrange("g t s -> t g s"))
                load(sp, buf[2][:, 0:DM], D["sgu_ln_g"].partition_broadcast(P))
                load(sp, buf[2][:, DM:2 * DM], D["sgu_ln_b"].partition_broadcast(P))
                load(sp, conv_rows[NCR:NCR + SG, :], D["spatial_b"][0])
                load(sp, conv_rows[0:NCR, :], D["conv_w"][0].rearrange("w (b p) -> (w b) p", p=P))
                wait_loads(sp)
                W.issue(sp)

            @block.vector
            def _(dve):
                chain(DV, dve, "zero")(nc.vector.memset(buf[6][:, 3 * DM:4 * DM], 0.0))

            @block.gpsimd
            def _(pool):
                link = chain(PO, pool, "const")
                keep_where = dict(in_=ones[:, :], pattern=[[1, P]], channel_multiplier=-1)
                link(nc.gpsimd.memset(ones[:, :], 1.0))
                link(nc.gpsimd.affine_select(out=ident[:, :], compare_op=ALU.is_equal, fill=0.0, base=0, **keep_where))
                link(nc.gpsimd.affine_select(out=tri[:, :], compare_op=ALU.is_ge, fill=0.0, base=0, **keep_where))
                link(nc.gpsimd.affine_select(out=strict[:, :], compare_op=ALU.is_ge, fill=0.0, base=-1, **keep_where))
                for i in range(NL):
                    b = 1 << i
                    m = level_mask[:, i, :].rearrange("p (m c) -> p m c", c=2 * b)
                    o = ones[:, :].rearrange("p (m c) -> p m c", c=2 * b)
                    pairs = P // (2 * b)
                    link(nc.gpsimd.affine_select(out=m, in_=o, compare_op=ALU.is_ge, fill=0.0, base=0,
                                                 pattern=[[-2 * b, pairs], [0, 2 * b]], channel_multiplier=1))
                    link(nc.gpsimd.affine_select(out=m, in_=m, compare_op=ALU.is_ge, fill=0.0, base=b - 1,
                                                 pattern=[[2 * b, pairs], [0, 2 * b]], channel_multiplier=-1))
                    link(nc.gpsimd.memset(m[:, :, 0:b], 0.0))
                link(nc.gpsimd.iota(ismall[:, 0:16], pattern=[[1, 16]], base=0, channel_multiplier=0))
                link(nc.gpsimd.tensor_copy(small[:, 496:512], ismall[:, 0:16]))

        stage([("spT", 0), ("spT", 1), "conv", "c"], ["conv", "c"], [("spT", 0), ("spT", 1)], [])
        with nc.Block() as block:
            @block.tensor
            def _(pe):
                for h in range(2):
                    for j in range(4):
                        last = nc.tensor.transpose(bank[h][:, j * P:(j + 1) * P], sp_nat[:, 4 * h + j, :], ident[:, :])
                    PE.done(last, ("spT", h))
                n = conv_rows.shape[0]
                PE.done(nc.tensor.transpose(bank[2][:, 0:n], conv_rows, ident[0:n, 0:n]), "conv")
                PE.done(nc.tensor.transpose(bank[3][:, 0:KD], c_rows, ident[0:KD, 0:KD]), "c")

            @block.vector
            def _(dve):
                for h in range(2):
                    PE.wait(dve, ("spT", h))
                    DV.done(nc.vector.tensor_tensor(spT[:, 4 * h:4 * h + 4, :], bank[h][:, :].rearrange("p (j n) -> p j n", j=4),
                                                    bcast(tri[:, :].unsqueeze(1), P, 4, P), ALU.mult), ("spT", h))

            @block.scalar
            def _(act):
                PE.wait(act, "conv")
                AC.done(nc.scalar.activation(small[:, 16:16 + conv_rows.shape[0]], bank[2][:, 0:conv_rows.shape[0]], ACT.Copy), "conv")
                PE.wait(act, "c")
                AC.done(nc.scalar.activation(c_cols, bank[3][:, 0:KD], ACT.Silu), "c")

        zero_filled = sem("rows_zeroed")

        transpose_stage(resid, featT)

        u_tok, v_tok, y_tok, gate = tok(buf[0]), tok(buf[1]), tok(buf[4]), tok(buf[5])
        uv = [u_tok, v_tok]
        project(featT, KD, [BANK] * 4, "act",
                lambda n, t, b, mid: nc.scalar.activation(uv[n // 2][:, t, span(n % 2)], b[:, :], ACT.Gelu), pieces=24)
        project(featT, KD, [BANK] * 2, "act",
                lambda n, t, b, mid: nc.scalar.activation(gate[:, t, span(n)], b[:, :], ACT.Sigmoid), pieces=12)

        def layer_norm(x, gain, bias, eps, at, then=None):
            n_t = x.shape[1]
            dv, ac = [], []
            for t in range(n_t):
                dv += [("stat", t, 0), ("stat", t, 1), ("mean", t), ("eps", t), ("norm", t), ("gain", t), ("bias", t)]
                ac += [("log", t), ("rstd", t)]
            stage((), ac, dv)
            with nc.Block() as block:
                def st(t, lo, hi):
                    return small[:, at + 16 * t + lo:at + 16 * t + hi]

                @block.vector
                def _(dve):
                    for t in range(n_t):
                        for h in range(2):
                            DV.done(nc.vector.bn_stats(st(t, 6 * h, 6 * h + 6), x[:, t, span(h)]), ("stat", t, h))
                        DV.wait(dve, ("stat", t, 1))
                        DV.done(nc.vector.bn_aggr(st(t, 12, 14), st(t, 0, 12).rearrange("p (a b) -> p a b", a=2)), ("mean", t))
                        DV.wait(dve, ("mean", t))
                        DV.done(nc.vector.tensor_scalar_add(st(t, 14, 15), st(t, 13, 14), eps), ("eps", t))
                        AC.wait(dve, ("rstd", t))
                        DV.done(nc.vector.tensor_scalar(x[:, t, :], x[:, t, :], st(t, 12, 13), st(t, 15, 16),
                                                        ALU.subtract, ALU.mult), ("norm", t))
                        DV.wait(dve, ("norm", t))
                        DV.done(nc.vector.tensor_tensor(x[:, t, :], x[:, t, :], gain, ALU.mult), ("gain", t))
                        DV.wait(dve, ("gain", t))
                        DV.done(nc.vector.tensor_tensor(x[:, t, :], x[:, t, :], bias, ALU.add), ("bias", t))

                @block.scalar
                def _(act):
                    for t in range(n_t):
                        DV.wait(act, ("eps", t))
                        AC.done(nc.scalar.activation(st(t, 14, 15), st(t, 14, 15), ACT.Ln), ("log", t))
                        AC.wait(act, ("log", t))
                        AC.done(nc.scalar.activation(st(t, 15, 16), st(t, 14, 15), ACT.Exp, scale=-0.5), ("rstd", t))

                @block.sync
                def _(sp):
                    if then:
                        then(sp)
                    W.issue(sp)

        layer_norm(v_tok, buf[2][:, 0:DM], buf[2][:, DM:2 * DM], LN_EPS, 128)

        jobs = [(t, h) for t in range(T) for h in range(2)]
        stage([("mix",) + j for j in jobs], (), [("bias",) + j + (g,) for j in jobs for g in range(4)] )
        with nc.Block() as block:
            @block.tensor
            def _(pe):
                for t, h in jobs:
                    for g in range(4):
                        last = nc.tensor.matmul(bank[2 * t + h][:, g * P:(g + 1) * P], spT[:, 4 * h + g, :],
                                                v_tok[:, t, (4 * h + g) * P:(4 * h + g + 1) * P], start=True, stop=True)
                    PE.done(last, ("mix", t, h))

            @block.vector
            def _(dve):
                for t, h in jobs:
                    PE.wait(dve, ("mix", t, h))
                    for g in range(4):
                        c = slice((4 * h + g) * P, (4 * h + g + 1) * P)
                        DV.done(nc.vector.scalar_tensor_tensor(
                            out=u_tok[:, t, c], in0=bank[2 * t + h][:, g * P:(g + 1) * P], scalar=sp_bias[:, 4 * h + g:4 * h + g + 1],
                            in1=u_tok[:, t, c], op0=ALU.add, op1=ALU.mult), ("bias", t, h, g))
        gatedT = buf[1][:, :].rearrange("p (k s) -> p k s", k=KD)
        transpose_stage(u_tok, gatedT)
        project(gatedT, KD, [BANK] * 2, "dve",
                lambda n, t, b, mid: nc.vector.tensor_tensor(y_tok[:, t, span(n)], b[:, :], gate[:, t, span(n)], ALU.mult))

        q_tok, k_tok, vd_tok = tok(buf[0]), tok(buf[1]), tok(buf[2])
        NB = 3 * DN // P
        ids = W.take(NB // 4)
        dve_names = [(s, b) for b in range(NB) for s in ("tap0", "tap1", "tap2", "tap3")]
        stage([x for b in range(NB + 1) for x in ([("block", b)] if b < NB else []) + ([("turned", b - 1)] if b else [])],
              [(s, b) for b in range(NB) for s in ("silu", "kept")], dve_names)
        conv_acc = [buf[3][:, i * S:(i + 1) * S] for i in range(2)]
        conv_out = [buf[3][:, (2 + i) * S:(3 + i) * S] for i in range(2)]
        with nc.Block() as block:
            @block.tensor
            def _(pe):
                def turn(b):
                    AC.wait(pe, ("silu", b))
                    if b >= 4:
                        AC.wait(pe, ("kept", b - 4))
                    for t in range(T):
                        last = nc.tensor.transpose(bank[4 + b % 4][:, t * P:(t + 1) * P], conv_out[b % 2][:, t * P:(t + 1) * P], ident[:, :])
                    PE.done(last, ("turned", b))
                for b in range(NB):
                    chunk = ids[b // 4]
                    if b % 4 == 0:
                        W.wait_landed(pe, chunk)
                    if b >= 4:
                        DV.wait(pe, ("tap3", b - 4))
                    w = W.slot(chunk)[:, :].rearrange("p (k n) -> p k n", k=KD)
                    for k in range(KD):
                        last = nc.tensor.matmul(bank[b % 4][:, :], w[:, k, (b % 4) * P:(b % 4 + 1) * P], featT[:, k, :],
                                                start=(k == 0), stop=(k == KD - 1))
                    PE.done(last, ("block", b))
                    if b % 4 == 3:
                        W.mark_used(chunk, PE.sem, PE.value(("block", b)))
                    if b:
                        turn(b - 1)
                turn(NB - 1)

            @block.vector
            def _(dve):
                for b in range(NB):
                    acc, src = conv_acc[b % 2], bank[b % 4]
                    PE.wait(dve, ("block", b))
                    if b >= 2:
                        AC.wait(dve, ("silu", b - 2))
                    DV.done(nc.vector.tensor_scalar(acc, src[:, :], conv_cols[:, CONV - 1, b:b + 1], None, ALU.mult), ("tap0", b))
                    for back in range(1, CONV):
                        DV.wait(dve, ("tap%d" % (back - 1), b))
                        DV.done(nc.vector.scalar_tensor_tensor(
                            out=acc[:, back:S], in0=src[:, 0:S - back], scalar=conv_cols[:, CONV - 1 - back, b:b + 1],
                            in1=acc[:, back:S], op0=ALU.mult, op1=ALU.add), ("tap%d" % back, b))

            @block.scalar
            def _(act):
                for b in range(NB):
                    DV.wait(act, ("tap3", b))
                    if b >= 2:
                        PE.wait(act, ("turned", b - 2))
                    AC.done(nc.scalar.activation(conv_out[b % 2], conv_acc[b % 2], ACT.Silu), ("silu", b))
                    PE.wait(act, ("turned", b))
                    dst = (q_tok, k_tok, vd_tok)[b // 8][:, :, (b % 8) * P:(b % 8 + 1) * P]
                    AC.done(nc.scalar.activation(dst, bank[4 + b % 4][:, :].rearrange("p (t n) -> p t n", t=T), ACT.Copy), ("kept", b))

            @block.gpsimd
            def _(pool):
                fills = [r_[i * P:(i + 1) * P, :] for r_ in (x_rows, y_rows) for i in range(N_MAIN + N_EXTRA)]
                for i, rows_ in enumerate(fills):
                    if i % 2 == 0:
                        PE.wait(pool, ("block", i // 2))
                    pool.dma_start(rows_, buf[6][:, 3 * DM:4 * DM]).then_inc(zero_filled, 16)

            @block.sync
            def _(sp):
                load(sp, ab_w, rows(w_in)[:, :, 4 * DN:UV_OFF])
                load(sp, small[:, 256:256 + H], D["a_log"].partition_broadcast(P))
                load(sp, small[:, 264:264 + H], D["dt_bias"].partition_broadcast(P))
                wait_loads(sp)
                W.issue(sp)

        sc = small
        decay_rate, dt_bias = sc[:, 256:256 + H], sc[:, 264:264 + H]
        TH = T * H
        a_in, g_all, beta_all, tmp_a, tmp_b = (sc[:, 288 + 32 * i:288 + 32 * (i + 1)] for i in range(5))
        ssq = [buf[6][:, 2048 + 32 * i:2048 + 32 * (i + 1)] for i in range(2)]
        square = [buf[3][:, 0:DM], buf[3][:, DM:2 * DM]]
        def th(a):
            return a.rearrange("p (t h) -> p t h", t=T)
        dv_names = (["dt", "neg", "low", "high", "rate", "g"] +
                    [(s, i, t) for t in range(T) for i in range(2) for s in ("square", "ssq")] +
                    [("eps", i) for i in range(2)] + [("unit", i, t) for t in range(T) for i in range(2)])
        ac_names = ["beta", "exp", "rate", "log"] + [(s, i) for i in range(2) for s in ("log", "inv")]
        stage(["ab"], ac_names, dv_names)
        with nc.Block() as block:
            @block.tensor
            def _(pe):
                for t in range(T):
                    for k in range(KD):
                        last = nc.tensor.matmul(bank[0][:, t * 2 * H:(t + 1) * 2 * H], featT[:, k, t * P:(t + 1) * P],
                                                ab_w[:, k, :], start=(k == 0), stop=(k == KD - 1))
                PE.done(last, "ab")

            @block.vector
            def _(dve):
                ab = bank[0][:, 0:T * 2 * H].rearrange("p (t n) -> p t n", t=T)
                PE.wait(dve, "ab")
                DV.done(nc.vector.tensor_tensor(th(a_in), ab[:, :, 0:H], bcast(dt_bias.unsqueeze(1), P, T, H), ALU.add), "dt")
                DV.wait(dve, "dt")
                DV.done(nc.vector.tensor_scalar(tmp_a, a_in, -1.0, None, ALU.mult), "neg")
                DV.wait(dve, "neg")
                DV.done(nc.vector.tensor_tensor(tmp_a, tmp_a, a_in, ALU.min), "low")
                DV.done(nc.vector.tensor_scalar(a_in, a_in, 0.0, None, ALU.max), "high")
                AC.wait(dve, "log")
                DV.wait(dve, "high")
                DV.done(nc.vector.tensor_tensor(tmp_b, tmp_b, a_in, ALU.add), "rate")
                DV.wait(dve, "rate")
                DV.done(nc.vector.scalar_tensor_tensor(out=th(g_all), in0=th(tmp_b), scalar=-1.0, in1=bcast(decay_rate.unsqueeze(1), P, T, H),
                                                       op0=ALU.mult, op1=ALU.mult), "g")
                for t in range(T):
                    for i, x in enumerate((q_tok, k_tok)):
                        if t:
                            DV.wait(dve, ("ssq", i, t - 1))
                        DV.done(nc.vector.tensor_tensor(square[i], x[:, t, :], x[:, t, :], ALU.mult), ("square", i, t))
                        DV.wait(dve, ("square", i, t))
                        DV.done(nc.vector.reduce_sum(ssq[i][:, t * H:(t + 1) * H], square[i].rearrange("p (h n) -> p h n", h=H), X_AXIS), ("ssq", i, t))
                for i in range(2):
                    DV.wait(dve, ("ssq", i, T - 1))
                    DV.done(nc.vector.tensor_scalar_add(ssq[i], ssq[i], EPS), ("eps", i))
                for t in range(T):
                    for i, x in enumerate((q_tok, k_tok)):
                        AC.wait(dve, ("inv", i))
                        v = x[:, t, :].rearrange("p (h n) -> p h n", h=H)
                        r = bcast(ssq[i][:, t * H:(t + 1) * H].unsqueeze(2), P, H, P)
                        if i == 0:
                            DV.done(nc.vector.scalar_tensor_tensor(out=v, in0=v, scalar=float(P) ** -0.5, in1=r, op0=ALU.mult, op1=ALU.mult), ("unit", i, t))
                        else:
                            DV.done(nc.vector.tensor_tensor(v, v, r, ALU.mult), ("unit", i, t))

            @block.scalar
            def _(act):
                ab = bank[0][:, 0:T * 2 * H].rearrange("p (t n) -> p t n", t=T)
                PE.wait(act, "ab")
                DV.wait(act, "dt")
                AC.done(nc.scalar.activation(th(beta_all), ab[:, :, H:2 * H], ACT.Sigmoid), "beta")
                DV.wait(act, "low")
                AC.done(nc.scalar.activation(tmp_b, tmp_a, ACT.Exp), "exp")
                AC.done(nc.scalar.activation(decay_rate, decay_rate, ACT.Exp), "rate")
                AC.wait(act, "rate")
                AC.done(nc.scalar.activation(tmp_b, tmp_b, ACT.Ln, bias=1.0), "log")
                for i in range(2):
                    DV.wait(act, ("eps", i))
                    AC.done(nc.scalar.activation(ssq[i], ssq[i], ACT.Ln), ("log", i))
                    AC.wait(act, ("log", i))
                    AC.done(nc.scalar.activation(ssq[i], ssq[i], ACT.Exp, scale=-0.5), ("inv", i))

            @block.gpsimd
            def _(pool):
                nc.gpsimd.memset(state[:, :], 0.0)

            @block.sync
            def _(sp):
                W.issue(sp)

        HH = H // 2
        heads = lambda a: a.rearrange("p (h n) -> p h n", h=H)
        qkbT = buf[3][:, 0:2048].rearrange("p (h i n) -> p h i n", h=H, i=2)
        kT, decT = heads(buf[3][:, 2048:3072]), heads(buf[3][:, 3072:4096])
        qk, negT, inv_t, inv = (heads(buf[5][:, i * DM:(i + 1) * DM]) for i in range(4))
        lev, kb, kd, vnew = (heads(buf[6][:, i * DM:(i + 1) * DM]) for i in range(4))
        gcol, gtot = sc[:, 448:456], sc[:, 456:464]
        e_g, e_tot, e_rest, b_eg = (sc[:, 464 + 8 * i:472 + 8 * i] for i in range(4))
        st_h = heads(state[:, :])
        LV = range(1, NL)
        halves = range(2)
        HU = 2
        units = range(H // HU)
        pe_n = (["sums", "qT", "kT", "kbT", "scores"] + [("t0", u) for u in units] +
                [(s, l, h) for l in LV for s in ("lev", "dinv") + (("turn",) if l < NL - 1 else ()) for h in units] +
                [(s, h) for s in ("ks", "qs") for h in halves] + [("vn", h) for h in halves] + [(s, h) for s in ("o", "s") for h in halves])
        ac_n = (["g", "e", "rest", "decay", ("qT", 0), ("qT", 1), ("kbT", 0), ("kbT", 1)] + [("t0", u) for u in units] +
                [(s, l, h) for l in LV for s in ("lev",) + (("turn",) if l < NL - 1 else ()) for h in units] + [("vn", h) for h in halves])
        dv_n = (["tg", "rest", "beg", ("diff", 0), ("diff", 1), "clip", ("kT", 0), ("kT", 1)] + [(s, i) for i in range(4) for s in ("qk", "neg")] +
                ["strict", "first", "eye"] + [("add", l, h) for l in LV for h in units] +
                [(s, h) for h in halves for s in ("rk", "r")] + [(s, h) for h in halves for s in ("oq", "o", "sg", "s")])
        po_n = ["kb", "vb", "kd", "causal"]
        stage(pe_n, ac_n, dv_n, po_n, rounds=T)
        b4 = lambda i: bank[i][:, :].rearrange("p (h n) -> p h n", h=HH)
        hs = lambda h: slice(HH * h, HH * h + HH)
        per_head = lambda a, n=H: bcast(a.unsqueeze(2), P, n, P)
        with nc.Block() as block:
            @block.tensor
            def _(pe):
                for c in range(T):
                    g_c = g_all[:, c * H:(c + 1) * H]
                    DV.wait(pe, "tg", c)
                    if c:
                        DV.wait(pe, ("s", 1), c - 1)
                    for h in halves:
                        nc.tensor.matmul(bank[h][:, :], ones[:, :], lev[:, hs(h), :], start=True, stop=True)
                    nc.tensor.matmul(bank[2][:, 0:H], tri[:, :], g_c, start=True, stop=True)
                    PE.done(nc.tensor.matmul(bank[2][:, H:2 * H], ones[:, :], g_c, start=True, stop=True), "sums")
                    for h in range(H):
                        last = nc.tensor.transpose(bank[3 + h // HH][:, (h % HH) * P:(h % HH + 1) * P], heads(q_tok[:, c, :])[:, h, :], ident[:, :])
                    PE.done(last, "qT")
                    for h in range(H):
                        last = nc.tensor.transpose(bank[5 + h // HH][:, (h % HH) * P:(h % HH + 1) * P], heads(k_tok[:, c, :])[:, h, :], ident[:, :])
                    PE.done(last, "kT")
                    PO.wait(pe, "kb", c)
                    DV.wait(pe, ("diff", 1), c)
                    for h in range(H):
                        last = nc.tensor.transpose(bank[h // HH][:, (h % HH) * P:(h % HH + 1) * P], kb[:, h, :], ident[:, :])
                    PE.done(last, "kbT")
                    AC.wait(pe, ("kbT", 1), c)
                    DV.wait(pe, ("kT", 1), c)
                    for h in range(H):
                        last = nc.tensor.matmul(bank[2 + h // 2][:, (h % 2) * 2 * P:(h % 2 + 1) * 2 * P], kT[:, h, :],
                                                qkbT[:, h, :, :], start=True, stop=True)
                    PE.done(last, "scores")
                    DV.wait(pe, "eye", c)
                    def unit(u, out, f, name):
                        for j in range(HU):
                            last = f(bank[out + u][:, j * P:(j + 1) * P], HU * u + j)
                        PE.done(last, name)
                    turn = lambda o, h: nc.tensor.transpose(o, inv_t[:, h, :], ident[:, :])
                    for u in units:
                        unit(u, 4, turn, ("t0", u))
                    for l in LV:
                        for u in units:
                            AC.wait(pe, ("turn", l - 1, u) if l > 1 else ("t0", u), c)
                            unit(u, 0, lambda o, h: nc.tensor.matmul(o, negT[:, h, :], inv[:, h, :], start=True, stop=True), ("lev", l, u))
                        for u in units:
                            AC.wait(pe, ("lev", l, u), c)
                            unit(u, 4, lambda o, h: nc.tensor.matmul(o, lev[:, h, :], inv_t[:, h, :], start=True, stop=True), ("dinv", l, u))
                        if l < NL - 1:
                            for u in units:
                                DV.wait(pe, ("add", l, u), c)
                                unit(u, 0, turn, ("turn", l, u))
                    DV.wait(pe, ("add", NL - 1, units[-1]), c)
                    for h in halves:
                        for j in range(HH):
                            last = nc.tensor.matmul(bank[h][:, j * P:(j + 1) * P], kT[:, HH * h + j, :], st_h[:, HH * h + j, :], start=True, stop=True)
                        PE.done(last, ("ks", h))
                    for h in halves:
                        for j in range(HH):
                            last = nc.tensor.matmul(bank[6 + h][:, j * P:(j + 1) * P], qkbT[:, HH * h + j, 0, :], st_h[:, HH * h + j, :], start=True, stop=True)
                        PE.done(last, ("qs", h))
                    for h in halves:
                        DV.wait(pe, ("r", h), c)
                        for j in range(HH):
                            last = nc.tensor.matmul(bank[2 + h][:, j * P:(j + 1) * P], inv_t[:, HH * h + j, :], kb[:, HH * h + j, :], start=True, stop=True)
                        PE.done(last, ("vn", h))
                    AC.wait(pe, ("vn", 1), c)
                    PO.wait(pe, "kd", c)
                    for h in halves:
                        for j in range(HH):
                            last = nc.tensor.matmul(bank[4 + h][:, j * P:(j + 1) * P], qk[:, HH * h + j, :], vnew[:, HH * h + j, :], start=True, stop=True)
                        PE.done(last, ("o", h))
                    for h in halves:
                        for j in range(HH):
                            last = nc.tensor.matmul(bank[h][:, j * P:(j + 1) * P], kd[:, HH * h + j, :], vnew[:, HH * h + j, :], start=True, stop=True)
                        PE.done(last, ("s", h))

            @block.scalar
            def _(act):
                for c in range(T):
                    PE.wait(act, "sums", c)
                    AC.done(nc.scalar.activation(sc[:, 448:464], bank[2][:, 0:2 * H], ACT.Copy), "g")
                    AC.wait(act, "g", c)
                    AC.done(nc.scalar.activation(sc[:, 464:480], sc[:, 448:464], ACT.Exp), "e")
                    DV.wait(act, "rest", c)
                    AC.done(nc.scalar.activation(e_rest, e_rest, ACT.Exp), "rest")
                    DV.wait(act, "clip", c)
                    AC.done(nc.scalar.activation(decT, decT, ACT.Exp), "decay")
                    PE.wait(act, "qT", c)
                    for h in halves:
                        AC.done(nc.scalar.activation(qkbT[:, hs(h), 0, :], b4(3 + h), ACT.Copy), ("qT", h))
                    PE.wait(act, "kbT", c)
                    for h in halves:
                        AC.done(nc.scalar.activation(qkbT[:, hs(h), 1, :], b4(h), ACT.Copy), ("kbT", h))
                    two = lambda i: bank[i][:, 0:HU * P].rearrange("p (h n) -> p h n", h=HU)
                    us = lambda u: slice(HU * u, HU * u + HU)
                    for u in units:
                        PE.wait(act, ("t0", u), c)
                        AC.done(nc.scalar.activation(inv[:, us(u), :], two(4 + u), ACT.Copy), ("t0", u))
                    for l in LV:
                        for u in units:
                            PE.wait(act, ("lev", l, u), c)
                            AC.done(nc.scalar.activation(lev[:, us(u), :], two(u), ACT.Copy), ("lev", l, u))
                        if l < NL - 1:
                            for u in units:
                                PE.wait(act, ("turn", l, u), c)
                                AC.done(nc.scalar.activation(inv[:, us(u), :], two(u), ACT.Copy), ("turn", l, u))
                    for h in halves:
                        PE.wait(act, ("vn", h), c)
                        AC.done(nc.scalar.activation(vnew[:, hs(h), :], b4(2 + h), ACT.Copy), ("vn", h))

            @block.vector
            def _(dve):
                for c in range(T):
                    g_c, be_c = g_all[:, c * H:(c + 1) * H], beta_all[:, c * H:(c + 1) * H]
                    o_c = heads(vd_tok[:, c, :])
                    DV.done(nc.vector.tensor_tensor(lev, bcast(tri[:, :].unsqueeze(1), P, H, P), per_head(g_c), ALU.mult), "tg")
                    AC.wait(dve, "e", c)
                    DV.done(nc.vector.tensor_tensor(e_rest, gtot, gcol, ALU.subtract), "rest")
                    DV.done(nc.vector.tensor_tensor(b_eg, e_g, be_c, ALU.mult), "beg")
                    for h in halves:
                        DV.done(nc.vector.tensor_tensor(decT[:, hs(h), :], b4(h), per_head(gcol[:, hs(h)], HH), ALU.subtract), ("diff", h))
                    DV.wait(dve, ("diff", 1), c)
                    DV.done(nc.vector.tensor_scalar(decT, decT, 0.0, None, ALU.min), "clip")
                    PE.wait(dve, "kT", c)
                    for h in halves:
                        DV.done(nc.vector.tensor_copy(kT[:, hs(h), :], b4(5 + h)), ("kT", h))
                    PE.wait(dve, "scores", c)
                    PO.wait(dve, "causal", c)
                    for i in range(4):
                        s4 = bank[2 + i][:, :].rearrange("p (h i n) -> p h i n", h=2, i=2)
                        two = slice(2 * i, 2 * i + 2)
                        DV.done(nc.vector.tensor_tensor(qk[:, two, :], s4[:, :, 0, :], decT[:, two, :], ALU.mult), ("qk", i))
                        DV.done(nc.vector.tensor_tensor(negT[:, two, :], s4[:, :, 1, :], decT[:, two, :], ALU.mult), ("neg", i))
                    DV.wait(dve, ("neg", 3), c)
                    DV.done(nc.vector.scalar_tensor_tensor(out=negT, in0=negT, scalar=-1.0, in1=bcast(strict[:, :].unsqueeze(1), P, H, P),
                                                           op0=ALU.mult, op1=ALU.mult), "strict")
                    DV.wait(dve, "strict", c)
                    DV.done(nc.vector.tensor_tensor(inv_t, negT, bcast(level_mask[:, 0, :].unsqueeze(1), P, H, P), ALU.mult), "first")
                    DV.wait(dve, "first", c)
                    DV.done(nc.vector.tensor_tensor(inv_t, inv_t, bcast(ident[:, :].unsqueeze(1), P, H, P), ALU.add), "eye")
                    for l in LV:
                        for u in units:
                            PE.wait(dve, ("dinv", l, u), c)
                            DV.done(nc.vector.copy_predicated(
                                inv_t[:, HU * u:HU * u + HU, :], bcast(level_mask[:, l, :].bitcast(I32).unsqueeze(1), P, HU, P),
                                bank[4 + u][:, 0:HU * P].rearrange("p (h n) -> p h n", h=HU)), ("add", l, u))
                    for h in halves:
                        PE.wait(dve, ("ks", h), c)
                        DV.done(nc.vector.tensor_tensor(kb[:, hs(h), :], b4(h), per_head(b_eg[:, hs(h)], HH), ALU.mult), ("rk", h))
                        DV.wait(dve, ("rk", h), c)
                        PO.wait(dve, "vb", c)
                        DV.done(nc.vector.tensor_tensor(kb[:, hs(h), :], o_c[:, hs(h), :], kb[:, hs(h), :], ALU.subtract), ("r", h))
                    for h in halves:
                        PE.wait(dve, ("qs", h), c)
                        DV.wait(dve, ("r", h), c)
                        DV.done(nc.vector.tensor_tensor(o_c[:, hs(h), :], b4(6 + h), per_head(e_g[:, hs(h)], HH), ALU.mult), ("oq", h))
                        PE.wait(dve, ("o", h), c)
                        DV.wait(dve, ("oq", h), c)
                        DV.done(nc.vector.tensor_tensor(o_c[:, hs(h), :], o_c[:, hs(h), :], b4(4 + h), ALU.add), ("o", h))
                        PE.wait(dve, ("s", h), c)
                        DV.done(nc.vector.tensor_tensor(st_h[:, hs(h), :], st_h[:, hs(h), :], per_head(e_tot[:, hs(h)], HH), ALU.mult), ("sg", h))
                        DV.wait(dve, ("sg", h), c)
                        DV.done(nc.vector.tensor_tensor(st_h[:, hs(h), :], st_h[:, hs(h), :], b4(h), ALU.add), ("s", h))

            @block.gpsimd
            def _(pool):
                for c in range(T):
                    be_c = beta_all[:, c * H:(c + 1) * H]
                    k_c, v_c = heads(k_tok[:, c, :]), heads(vd_tok[:, c, :])
                    if c:
                        PE.wait(pool, ("s", 1), c - 1)
                    PO.done(nc.gpsimd.tensor_tensor(kb, k_c, per_head(be_c), ALU.mult), "kb")
                    PO.done(nc.gpsimd.tensor_tensor(v_c, v_c, per_head(be_c), ALU.mult), "vb")
                    AC.wait(pool, "rest", c)
                    PO.done(nc.gpsimd.tensor_tensor(kd, k_c, per_head(e_rest), ALU.mult), "kd")
                    AC.wait(pool, "decay", c)
                    PO.done(nc.gpsimd.affine_select(out=decT, in_=decT, compare_op=ALU.is_ge, fill=0.0, base=0,
                                                    pattern=[[0, H], [1, P]], channel_multiplier=-1), "causal")

            @block.sync
            def _(sp):
                load(sp, sc[:, 128:256], D["dn_norm_g"].partition_broadcast(P))
                wait_loads(sp)
                W.issue(sp)

        def rms_stage(x, n, w, eps, gain=None, after=None, then=None, scratch=None, at=0):
            extra = len(after(0, dry=True)) if after else 0
            dv = [(s, t) for t in range(T) for s in ["square", "ssq", "eps"]]
            dv += [(s, t) for t in range(T) for s in ["unit"] + (["gain"] if gain is not None else []) + ["after%d" % i for i in range(extra)]]
            ac = [(s, t) for t in range(T) for s in ("log", "inv")]
            stage((), ac, dv)
            st = [small[:, at + n * t:at + n * t + n] for t in range(T)]
            sq = scratch.rearrange("p (n w) -> p n w", n=n)
            with nc.Block() as block:
                @block.vector
                def _(dve):
                    for t in range(T):
                        if t:
                            DV.wait(dve, ("ssq", t - 1))
                        DV.done(nc.vector.tensor_tensor(sq, x(t), x(t), ALU.mult), ("square", t))
                        DV.wait(dve, ("square", t))
                        DV.done(nc.vector.reduce_sum(st[t], sq, X_AXIS), ("ssq", t))
                        DV.wait(dve, ("ssq", t))
                        DV.done(nc.vector.tensor_scalar(st[t], st[t], 1.0 / w, eps, ALU.mult, ALU.add), ("eps", t))
                    for t in range(T):
                        AC.wait(dve, ("inv", t))
                        DV.done(nc.vector.tensor_tensor(x(t), x(t), bcast(st[t].unsqueeze(2), P, n, w), ALU.mult), ("unit", t))
                        DV.wait(dve, ("unit", t))
                        if gain is not None:
                            DV.done(nc.vector.tensor_tensor(x(t), x(t), bcast(gain.unsqueeze(1), P, n, w), ALU.mult), ("gain", t))
                            DV.wait(dve, ("gain", t))
                        if after:
                            for i, f in enumerate(after(t)):
                                if i:
                                    DV.wait(dve, ("after%d" % (i - 1), t))
                                DV.done(f(), ("after%d" % i, t))

                @block.scalar
                def _(act):
                    for t in range(T):
                        DV.wait(act, ("eps", t))
                        AC.done(nc.scalar.activation(st[t], st[t], ACT.Ln), ("log", t))
                        AC.wait(act, ("log", t))
                        AC.done(nc.scalar.activation(st[t], st[t], ACT.Exp, scale=-0.5), ("inv", t))

                @block.sync
                def _(sp):
                    if then:
                        then(sp)
                        wait_loads(sp)
                    W.issue(sp)

        z_tok = q_tok
        project(featT, KD, [BANK] * 2, "act",
                lambda n, t, b, mid: nc.scalar.activation(z_tok[:, t, span(n)], b[:, :], ACT.Silu), pieces=12)

        def times_z(t, dry=False):
            return [lambda: nc.vector.tensor_tensor(vd_tok[:, t, :], vd_tok[:, t, :], z_tok[:, t, :], ALU.mult)]

        def ln1_loads(sp):
            load(sp, buf[6][:, 0:DM], D["ln1_g"].partition_broadcast(P))
            load(sp, buf[6][:, DM:2 * DM], D["ln1_b"].partition_broadcast(P))
        rms_stage(lambda t: heads(vd_tok[:, t, :]), H, P, EPS, gain=sc[:, 128:256], after=times_z, then=ln1_loads,
                  scratch=buf[3][:, 0:DM])
        oT = buf[1][:, :].rearrange("p (k s) -> p k s", k=KD)
        transpose_stage(vd_tok, oT)
        project(featT, KD, [BANK] * 2, "act",
                lambda n, t, b, mid: nc.scalar.activation(gate[:, t, span(n)], b[:, :], ACT.Sigmoid), pieces=12)

        def add_gated(n, t, b, mid):
            mid(nc.vector.tensor_tensor(buf[3][:, 0:BANK], b[:, :], gate[:, t, span(n)], ALU.mult))
            return nc.vector.tensor_tensor(y_tok[:, t, span(n)], y_tok[:, t, span(n)], buf[3][:, 0:BANK], ALU.add)
        project(oT, KD, [BANK] * 2, "dve", add_gated, mids=1)
        yT = buf[0][:, :].rearrange("p (k s) -> p k s", k=KD)
        transpose_stage(y_tok, yT)

        def add_resid(n, t, b, mid):
            return nc.vector.scalar_tensor_tensor(out=resid[:, t, span(n)], in0=resid[:, t, span(n)], scalar=ALPHA, in1=b[:, :],
                                                  op0=ALU.mult, op1=ALU.add)
        project(yT, KD, [BANK] * 2, "dve", add_resid)
        layer_norm(resid, buf[6][:, 0:DM], buf[6][:, DM:2 * DM], LN_EPS, 128)

        step1 = lambda name: Steps(sem(name))
        M_xT, M_gu, M_hT, M_down = (step1("moe_" + n) for n in ("x_turned", "gate_up_sum", "h_turned", "down_sum"))
        M_keep = {"act": step1("moe_x_kept_act"), "dve": step1("moe_x_kept_dve")}
        M_silu, M_h, M_hkept = step1("moe_silu"), step1("moe_h"), step1("moe_h_kept")
        M_y = {"act": step1("moe_y_kept_act"), "dve": step1("moe_y_kept_dve")}
        M_all = [M_xT, M_gu, M_hT, M_down, *M_keep.values(), M_silu, M_h, M_hkept, *M_y.values()]
        x_landed, y_stored = [sem(f"moe_x_landed{i}") for i in range(2)], [sem(f"moe_y_stored{i}") for i in range(2)]
        scattered, gathered = sem("rows_scattered"), [sem(f"rows_gathered{i}") for i in range(4)]
        E_in, E_pe, E_act, E_dve, E_out = (sem("extra_" + n) for n in ("landed", "pe", "act", "dve", "stored"))
        moe_n = [0]
        e_idx = small[:, 496:512]

        def moe(gate_w, up_w, down_w, group_w, group_b, expert_w, expert_b, x_tok, xT, finish, then=None):
            nth = moe_n[0]
            moe_n[0] += 1
            r = buf[3]
            rw = r[:, 0:KD * (NG + NE)].rearrange("p (k n) -> p k n", k=KD)
            nrt = NG + NE
            rb = r[:, 160:160 + nrt]
            def f(at, n):
                return r[:, at:at + n]
            lg = f(192, T * nrt).rearrange("p (t n) -> p t n", t=T)
            gm, gsum, gp, mx1, mx2, low1, dif, w1, w2 = (f(272 + T * i, T) for i in range(9))
            eq, val, goh, gexp, ing, oh1, oh2, masked = (f(320 + 16 * i, 16).rearrange("p (t n) -> p t n", t=T) for i in range(8))
            O1, O2, O, prod, rowf, big = (f(448 + 64 * i, 64) for i in range(6))
            t16 = lambda a: a.rearrange("p (t n) -> p t n", t=T)
            t44 = lambda a: a.rearrange("p (t g j) -> p t g j", t=T, g=NG)
            cnt, nx, incl, xbase, tabA, tabB = (f(832 + 16 * i, 16) for i in range(6))
            rowsf, cmpx, eidf = f(928, 2 * T), f(944, N_EXTRA * NE), f(1072, N_EXTRA + 1)
            rows_i = ismall[:, 0:2 * T]
            ctl = ismall[:, 2 * T:2 * T + N_EXTRA + 1]
            per_tile = lambda a, n=NG: bcast(a.unsqueeze(2), P, T, n)
            idx4 = bcast(e_idx[:, 0:PER].unsqueeze(1), P, T, PER)
            N_DVE = 52
            stage(["logits", "ranks"], ["gexp", "r"], links("route", N_DVE))
            with nc.Block() as block:
                @block.sync
                def _(sp):
                    sp.wait_ge(zero_filled, 16 * 2 * (N_MAIN + N_EXTRA))
                    load(sp, rw[:, :, 0:NG], rows(group_w))
                    load(sp, rw[:, :, NG:nrt], rows(expert_w))
                    load(sp, rb[:, 0:NG], group_b.partition_broadcast(P))
                    load(sp, rb[:, NG:nrt], expert_b.partition_broadcast(P))
                all_loads = loads[0]

                @block.tensor
                def _(pe):
                    pe.wait_ge(loaded, all_loads)
                    for t in range(T):
                        for k in range(KD):
                            last = nc.tensor.matmul(bank[0][:, t * nrt:(t + 1) * nrt], xT[:, k, t * P:(t + 1) * P], rw[:, k, :],
                                                    start=(k == 0), stop=(k == KD - 1))
                    PE.done(last, "logits")
                    DV.wait(pe, ("route", 29))
                    for t in range(T):
                        for s in range(t + 1):
                            nc.tensor.matmul(bank[1][:, t * NE:(t + 1) * NE], (strict if s == t else ones)[:, :], O[:, s * NE:(s + 1) * NE],
                                             start=(s == 0), stop=(s == t))
                    for s in range(T):
                        last = nc.tensor.matmul(bank[1][:, T * NE:(T + 1) * NE], ones[:, :], O[:, s * NE:(s + 1) * NE], start=(s == 0), stop=(s == T - 1))
                    PE.done(last, "ranks")

                @block.scalar
                def _(act):
                    DV.wait(act, ("route", 6))
                    AC.done(nc.scalar.activation(gexp, gexp, ACT.Exp), "gexp")
                    DV.wait(act, ("route", 22))
                    AC.done(nc.scalar.activation(dif, dif, ACT.Exp), "r")

                @block.vector
                def _(dve):
                    link = chain(DV, dve, "route")
                    V = nc.vector

                    def first_of(x, m):
                        link(V.reduce_max(m, x, X_AXIS))
                        link(V.tensor_tensor(eq, x, per_tile(m), ALU.is_equal))
                        link(V.scalar_tensor_tensor(out=val, in0=eq, scalar=-64.0, in1=idx4, op0=ALU.mult, op1=ALU.add))
                        link(V.tensor_reduce(low1, val, X_AXIS, ALU.min))
                    dve.wait_ge(loaded, all_loads)
                    PE.wait(dve, "logits")
                    link(V.tensor_tensor(lg, bank[0][:, 0:T * nrt].rearrange("p (t n) -> p t n", t=T), bcast(rb.unsqueeze(1), P, T, nrt), ALU.add))
                    first_of(lg[:, :, 0:NG], gm)
                    link(V.tensor_tensor(goh, val, per_tile(low1), ALU.is_equal))
                    link(V.tensor_tensor(gexp, lg[:, :, 0:NG], per_tile(gm), ALU.subtract))
                    link(V.tensor_tensor(t44(prod), lg[:, :, NG:nrt].rearrange("p t (g j) -> p t g j", g=NG),
                                         bcast(goh.unsqueeze(3), P, T, NG, PER), ALU.mult))
                    link(V.reduce_sum(ing, prod.rearrange("p (t g j) -> p t j g", t=T, g=NG), X_AXIS))
                    AC.wait(dve, "gexp")
                    link(V.reduce_sum(gsum, gexp, X_AXIS))
                    link(V.reciprocal(gp, gsum))
                    first_of(ing, mx1)
                    link(V.tensor_tensor(oh1, val, per_tile(low1), ALU.is_equal))
                    link(V.scalar_tensor_tensor(out=masked, in0=oh1, scalar=-1e30, in1=ing, op0=ALU.mult, op1=ALU.add))
                    first_of(masked, mx2)
                    link(V.tensor_tensor(oh2, val, per_tile(low1), ALU.is_equal))
                    link(V.tensor_tensor(dif, mx2, mx1, ALU.subtract))
                    AC.wait(dve, "r")
                    link(V.tensor_scalar_add(mx1, dif, 1.0))
                    link(V.reciprocal(mx1, mx1))
                    link(V.tensor_tensor(w1, gp, mx1, ALU.mult))
                    link(V.tensor_tensor(w2, w1, dif, ALU.mult))
                    g4, j4 = bcast(goh.unsqueeze(3), P, T, NG, PER), lambda a: bcast(a.unsqueeze(2), P, T, NG, PER)
                    link(V.tensor_tensor(t44(O1), g4, j4(oh1), ALU.mult))
                    link(V.tensor_tensor(t44(O2), g4, j4(oh2), ALU.mult))
                    link(V.tensor_tensor(O, O1, O2, ALU.add))
                    PE.wait(dve, "ranks")
                    link(V.tensor_copy(cnt, bank[1][:, T * NE:(T + 1) * NE]))
                    link(V.tensor_scalar(nx, cnt, float(P), None, ALU.is_gt))
                    for m in range(2, T):
                        link(V.scalar_tensor_tensor(out=nx, in0=cnt, scalar=float(P * m), in1=nx, op0=ALU.is_gt, op1=ALU.add))
                    link(V.tensor_tensor_scan(incl, ones[:, 0:NE], nx, 0.0, ALU.mult, ALU.add))
                    link(V.tensor_tensor(xbase, incl, nx, ALU.subtract))
                    link(V.tensor_scalar(tabA, e_idx, float(P), None, ALU.mult))
                    link(V.tensor_scalar(tabB, xbase, float(P), float(P * (N_MAIN - 1)), ALU.mult, ALU.add))
                    link(V.tensor_tensor(tabB, tabB, tabA, ALU.subtract))
                    ranks = t16(bank[1][:, 0:T * NE])
                    link(V.tensor_scalar(t16(big), ranks, float(P), None, ALU.is_ge))
                    link(V.tensor_tensor(t16(big), t16(big), bcast(tabB.unsqueeze(1), P, T, NE), ALU.mult))
                    link(V.tensor_tensor(t16(big), t16(big), bcast(tabA.unsqueeze(1), P, T, NE), ALU.add))
                    link(V.tensor_tensor(t16(rowf), t16(big), ranks, ALU.add))
                    for i, oo in enumerate((O1, O2)):
                        link(V.tensor_tensor(prod, oo, rowf, ALU.mult))
                        link(V.reduce_sum(rowsf[:, i * T:(i + 1) * T], t16(prod), X_AXIS))
                    link(V.tensor_copy(rows_i, rowsf))
                    c3 = cmpx.rearrange("p (x n) -> p x n", x=N_EXTRA)
                    link(V.tensor_tensor(c3, bcast(incl.unsqueeze(1), P, N_EXTRA, NE), bcast(e_idx[:, 0:N_EXTRA].unsqueeze(2), P, N_EXTRA, NE), ALU.is_le))
                    link(V.reduce_sum(eidf[:, 0:N_EXTRA], c3, X_AXIS))
                    link(V.tensor_copy(eidf[:, N_EXTRA:N_EXTRA + 1], incl[:, NE - 1:NE]))
                    link(V.tensor_copy(ctl, eidf))

                @block.gpsimd
                def _(pool):
                    DV.wait(pool, ("route", N_DVE - 5))
                    for t in range(T):
                        for i in range(2):
                            nc.gpsimd.indirect_dma_start(
                                out=x_rows[:, :], out_offset=bass.IndirectOffsetOnAxis(ap=rows_i[:, i * T + t:i * T + t + 1], axis=0),
                                in_=x_tok[:, t, :], in_offset=None).then_inc(scattered, 16)
                    pool.wait_ge(scattered, 16 * 2 * T * (nth + 1))

            half = lambda a, n: [a[:, i * n:(i + 1) * n] for i in range(2)]
            xg, xgT = half(r[:, 2048:4096], DM), [a.rearrange("p (k n) -> p k n", k=KD) for a in half(buf[1][:, 0:2048], DM)]
            act_g, h_tok = half(buf[1][:, 2048:2560], FF), half(buf[1][:, 2560:3072], FF)
            hT = [a.rearrange("p (k n) -> p k n", k=KF) for a in half(buf[1][:, 3072:3072 + 2 * KF * P], KF * P)]
            yg = half(buf[2][:, 0:2048], DM)
            w_gu = [ring[i][:, :].rearrange("p (k n) -> p k n", k=KD) for i in range(2)]
            w_dn = [ring[2 + i][:, 0:KF * DM].rearrange("p (k n) -> p k n", k=KF) for i in range(2)]
            ids = W.take(2 * NE)
            stage()
            for m in M_all:
                m.begin(["e"], NE)
                m.at = m.due
            v = lambda m, e: m.value("e", 0) + e
            land = lambda chunk, pair: W.ready[chunk] + (W.ready[chunk + 4] - W.ready[chunk]) * pair
            xl = 16 * NE // 2 * nth
            gr, ur, dr = (w.rearrange("e (k p) n -> p e k n", p=P) for w in (gate_w, up_w, down_w))

            def rounds(eng, body, lo, hi):
                with eng.Fori(lo // 2, hi // 2) as pair:
                    for par in range(2):
                        body(2 * pair + par, par, pair)

            def turn_x(eng, e, par, pair):
                eng.wait_ge(x_landed[par], 16 * (pair + 1) + xl)
                for h in range(2):
                    for j in range(4):
                        k = 4 * h + j
                        last = nc.tensor.transpose(bank[h][:, j * P:(j + 1) * P], xg[par][:, k * P:(k + 1) * P], ident[:, :])
                last.then_inc(M_xT.sem, 1)

            def gate_up(e, par):
                for k in range(KD):
                    last = nc.tensor.matmul(bank[2 + par][:, :], xgT[par][:, k, :], w_gu[par][:, k, :], start=(k == 0), stop=(k == KD - 1))
                last.then_inc(M_gu.sem, 1)

            def turn_h(e, par):
                for k in range(KF):
                    last = nc.tensor.transpose(bank[4][:, k * P:(k + 1) * P], h_tok[par][:, k * P:(k + 1) * P], ident[:, :])
                last.then_inc(M_hT.sem, 1)

            def down(e, par):
                for h in range(2):
                    for k in range(KF):
                        last = nc.tensor.matmul(bank[5 + h][:, :], hT[par][:, k, :], w_dn[par][:, k, span(h)], start=(k == 0), stop=(k == KF - 1))
                last.then_inc(M_down.sem, 1)

            def keep_x(par, h):
                out, src = xgT[par][:, 4 * h:4 * h + 4, :], bank[h][:, :].rearrange("p (j n) -> p j n", j=4)
                return nc.vector.tensor_copy(out, src) if h else nc.scalar.activation(out, src, ACT.Copy)

            def silu(par):
                return nc.scalar.activation(act_g[par], bank[2 + par][:, 0:FF], ACT.Silu)

            def times_up(par):
                return nc.vector.tensor_tensor(h_tok[par], act_g[par], bank[2 + par][:, FF:2 * FF], ALU.mult)

            def keep_h(par):
                return nc.vector.tensor_copy(hT[par], bank[4][:, 0:KF * P].rearrange("p (k n) -> p k n", k=KF))

            def keep_y(par, h):
                out = yg[par][:, span(h)]
                return nc.vector.tensor_copy(out, bank[5 + h][:, :]) if h else nc.scalar.activation(out, bank[5][:, :], ACT.Copy)

            with nc.Block() as block:
                @block.tensor
                def _(pe):
                    def body(e, par, pair, first=False, second=False, last=False):
                        before = pair if par else pair - 1
                        pe.wait_ge(W.landed[par], land(ids[2 * par], pair))
                        for m in M_keep.values():
                            pe.wait_ge(m.sem, v(m, e))
                        gate_up(e, par)
                        if not last:
                            turn_x(pe, e + 1, 1 - par, pair + 1 if par else pair)
                        if not first:
                            pe.wait_ge(W.landed[2 + 1 - par], land(ids[2 * (1 - par) + 1], before))
                            pe.wait_ge(M_hkept.sem, v(M_hkept, e - 1))
                            if not second:
                                for m in M_y.values():
                                    pe.wait_ge(m.sem, v(m, e - 2))
                            down(e - 1, 1 - par)
                        pe.wait_ge(M_h.sem, v(M_h, e))
                        turn_h(e, par)
                    turn_x(pe, 0, 0, 0)
                    body(0, 0, 0, first=True)
                    body(1, 1, 0, second=True)
                    rounds(pe, body, 2, NE - 2)
                    body(NE - 2, 0, NE // 2 - 1)
                    body(NE - 1, 1, NE // 2 - 1, last=True)
                    W.wait_landed(pe, ids[2 * NE - 1])
                    pe.wait_ge(M_hkept.sem, v(M_hkept, NE - 1))
                    for m in M_y.values():
                        pe.wait_ge(m.sem, v(m, NE - 2))
                    down(NE - 1, 1)
                    for i in range(2 * NE):
                        m = M_down if i % 2 else M_gu
                        W.mark_used(ids[i], m.sem, v(m, i // 2))

                @block.scalar
                def _(act):
                    def keep_y_act(e, par, pair, early=False):
                        act.wait_ge(M_down.sem, v(M_down, e))
                        if not early:
                            act.wait_ge(y_stored[par], 16 * pair + xl)
                        keep_y(par, 0).then_inc(M_y["act"].sem, 1)

                    def store_y(e, par):
                        for m in M_y.values():
                            act.wait_ge(m.sem, v(m, e))
                        act.dma_start(y_rows[bass.ds(e * P, P), :], yg[par]).then_inc(y_stored[par], 16)

                    def keep_x_act(e, par):
                        act.wait_ge(M_xT.sem, v(M_xT, e))
                        keep_x(par, 0).then_inc(M_keep["act"].sem, 1)

                    def load_gate_up(e, par):
                        for i, w in enumerate((gr, ur)):
                            act.dma_start(ring[par][:, :].rearrange("p (k g n) -> p k g n", k=KD, g=2)[:, :, i, :],
                                          w[:, bass.ds(e, 1), :, :].rearrange("p e k n -> p (e k) n")).then_inc(W.landed[par], 16)

                    def load_down(e, par):
                        act.dma_start(w_dn[par], dr[:, bass.ds(e, 1), :, :].rearrange("p e k n -> p (e k) n")).then_inc(W.landed[2 + par], 16)

                    def body(e, par, pair, first=False, free=False, no_y=False, tail=False, last=False):
                        act.wait_ge(M_gu.sem, v(M_gu, e))
                        if not free:
                            act.wait_ge(M_h.sem, v(M_h, e - 2))
                        silu(par).then_inc(M_silu.sem, 1)
                        if not tail:
                            load_gate_up(e + 2, par)
                        if not last:
                            keep_x_act(e + 1, 1 - par)
                        if not first:
                            keep_y_act(e - 1, 1 - par, pair if par else pair - 1, early=no_y)
                            if not last:
                                load_down(e + 1, 1 - par)
                        if not first:
                            store_y(e - 1, 1 - par)
                    keep_x_act(0, 0)
                    body(0, 0, 0, first=True, free=True)
                    body(1, 1, 0, free=True, no_y=True)
                    body(2, 0, 1, no_y=True)
                    body(3, 1, 1)
                    rounds(act, body, 4, NE - 2)
                    body(NE - 2, 0, NE // 2 - 1, tail=True)
                    body(NE - 1, 1, NE // 2 - 1, tail=True, last=True)
                    keep_y_act(NE - 1, 1, NE // 2 - 1)
                    store_y(NE - 1, 1)
                    for i in range(2):
                        act.wait_ge(y_stored[i], 16 * NE // 2 * (nth + 1))

                @block.vector
                def _(dve):
                    def keep_y_dve(e, par, pair, early=False):
                        dve.wait_ge(M_down.sem, v(M_down, e))
                        if not early:
                            dve.wait_ge(y_stored[par], 16 * pair + xl)
                        keep_y(par, 1).then_inc(M_y["dve"].sem, 1)

                    def keep_x_dve(e, par):
                        dve.wait_ge(M_xT.sem, v(M_xT, e))
                        keep_x(par, 1).then_inc(M_keep["dve"].sem, 1)

                    def body(e, par, pair, first=False, early=False, last=False):
                        dve.wait_ge(M_silu.sem, v(M_silu, e))
                        times_up(par).then_inc(M_h.sem, 1)
                        if not last:
                            keep_x_dve(e + 1, 1 - par)
                        if not first:
                            keep_y_dve(e - 1, 1 - par, pair if par else pair - 1, early=early)
                        dve.wait_ge(M_hT.sem, v(M_hT, e))
                        keep_h(par).then_inc(M_hkept.sem, 1)
                    keep_x_dve(0, 0)
                    body(0, 0, 0, first=True)
                    body(1, 1, 0, early=True)
                    body(2, 0, 1, early=True)
                    body(3, 1, 1)
                    rounds(dve, body, 4, NE - 2)
                    body(NE - 2, 0, NE // 2 - 1)
                    body(NE - 1, 1, NE // 2 - 1, last=True)
                    keep_y_dve(NE - 1, 1, NE // 2 - 1)

                @block.gpsimd
                def _(pool):
                    def load_x(e, par):
                        pool.dma_start(xg[par], x_rows[bass.ds(e * P, P), :]).then_inc(x_landed[par], 16)

                    load_x(0, 0)
                    load_x(1, 1)

                    def body(e, par, pair):
                        pool.wait_ge(M_xT.sem, v(M_xT, e - 2))
                        load_x(e, par)
                    rounds(pool, body, 2, NE)

                @block.sync
                def _(sp):
                    W.issue(sp)
                    assert W.issued == ids[4]

                    W.issued += 2 * NE - 4

            stage()
            with nc.Block() as block:
                def extra(eng, body):
                    n = eng.value_load(ctl[0:1, N_EXTRA:N_EXTRA + 1], min_val=0, max_val=N_EXTRA)
                    with eng.If(n > 0):
                        with eng.Fori(0, n) as x:
                            body(x)
                    with eng.Else():
                        eng.nop()

                @block.tensor
                def _(pe):
                    def body(x):
                        pe.wait_ge(E_in, 64 * x + 64)
                        for h in range(2):
                            for j in range(4):
                                k = 4 * h + j
                                last = nc.tensor.transpose(bank[h][:, j * P:(j + 1) * P], xg[0][:, k * P:(k + 1) * P], ident[:, :])
                        last.then_inc(E_pe, 1)
                        pe.wait_ge(E_act, 3 * x + 1)
                        pe.wait_ge(E_dve, 4 * x + 1)
                        for k in range(KD):
                            last = nc.tensor.matmul(bank[2][:, :], xgT[0][:, k, :], w_gu[0][:, k, :], start=(k == 0), stop=(k == KD - 1))
                        last.then_inc(E_pe, 1)
                        pe.wait_ge(E_dve, 4 * x + 2)
                        for k in range(KF):
                            last = nc.tensor.transpose(bank[4][:, k * P:(k + 1) * P], h_tok[0][:, k * P:(k + 1) * P], ident[:, :])
                        last.then_inc(E_pe, 1)
                        pe.wait_ge(E_dve, 4 * x + 3)
                        for h in range(2):
                            for k in range(KF):
                                last = nc.tensor.matmul(bank[5 + h][:, :], hT[0][:, k, :], w_dn[0][:, k, span(h)], start=(k == 0), stop=(k == KF - 1))
                        last.then_inc(E_pe, 1)
                    extra(pe, body)

                @block.scalar
                def _(act):
                    def body(x):
                        e = act.value_load(ctl[0:1, bass.ds(x, 1)], min_val=0, max_val=NE - 1)
                        row = bass.ds(x * P + N_MAIN * P, P)
                        act.dma_start(xg[0], x_rows[row, :]).then_inc(E_in, 16)
                        for i, w in enumerate((gr, ur)):
                            act.dma_start(ring[0][:, :].rearrange("p (k g n) -> p k g n", k=KD, g=2)[:, :, i, :],
                                          w[:, bass.ds(e, 1), :, :].rearrange("p e k n -> p (e k) n")).then_inc(E_in, 16)
                        act.dma_start(w_dn[0], dr[:, bass.ds(e, 1), :, :].rearrange("p e k n -> p (e k) n")).then_inc(E_in, 16)
                        act.wait_ge(E_pe, 4 * x + 1)
                        keep_x(0, 0).then_inc(E_act, 1)
                        act.wait_ge(E_pe, 4 * x + 2)
                        silu(0).then_inc(E_act, 1)
                        act.wait_ge(E_pe, 4 * x + 4)
                        keep_y(0, 0).then_inc(E_act, 1)
                        act.wait_ge(E_act, 3 * x + 3)
                        act.wait_ge(E_dve, 4 * x + 4)
                        act.dma_start(y_rows[row, :], yg[0]).then_inc(E_out, 16)
                        act.wait_ge(E_out, 16 * x + 16)
                    extra(act, body)

                @block.vector
                def _(dve):
                    def body(x):
                        dve.wait_ge(E_pe, 4 * x + 1)
                        keep_x(0, 1).then_inc(E_dve, 1)
                        dve.wait_ge(E_act, 3 * x + 2)
                        times_up(0).then_inc(E_dve, 1)
                        dve.wait_ge(E_pe, 4 * x + 3)
                        keep_h(0).then_inc(E_dve, 1)
                        dve.wait_ge(E_pe, 4 * x + 4)
                        keep_y(0, 1).then_inc(E_dve, 1)
                    extra(dve, body)

            g_buf = [buf[2][:, 2048:3072], buf[2][:, 3072:4096], buf[1][:, 0:1024], buf[1][:, 1024:2048]]
            fin = finish(0, g_buf[0], g_buf[1], w1[:, 0:1], w2[:, 0:1])
            stage((), (), [("f", t, i) for t in range(T) for i in range(len(fin))])
            with nc.Block() as block:
                @block.gpsimd
                def _(pool):
                    for s in (E_in, E_pe, E_act, E_dve, E_out):
                        pool.sem_clear(s)
                    for t in range(T):
                        if t >= 2:
                            DV.wait(pool, ("f", t - 2, len(fin) - 1))
                        for i in range(2):
                            g = 2 * (t % 2) + i
                            nc.gpsimd.indirect_dma_start(
                                out=g_buf[g], out_offset=None, in_=y_rows[:, :],
                                in_offset=bass.IndirectOffsetOnAxis(ap=rows_i[:, i * T + t:i * T + t + 1], axis=0)).then_inc(gathered[g], 16)

                @block.vector
                def _(dve):
                    for t in range(T):
                        g = 2 * (t % 2)
                        for i in range(2):
                            dve.wait_ge(gathered[g + i], 16 * (T // 2 * nth + t // 2 + 1))
                        for i, ins in enumerate(finish(t, g_buf[g], g_buf[g + 1], w1[:, t:t + 1], w2[:, t:t + 1])):
                            if i:
                                DV.wait(dve, ("f", t, i - 1))
                            DV.done(ins(), ("f", t, i))

                @block.sync
                def _(sp):
                    if then:
                        then(sp)
                        wait_loads(sp)
                    W.issue(sp)

        def ln2_loads(sp):
            load(sp, buf[6][:, 0:DM], D["ln2_g"].partition_broadcast(P))
            load(sp, buf[6][:, DM:2 * DM], D["ln2_b"].partition_broadcast(P))

        def finish_a(t, g1, g2, a, b):
            x = resid[:, t, :]
            return [lambda: nc.vector.tensor_scalar(x, x, ALPHA, None, ALU.mult),
                    lambda: nc.vector.scalar_tensor_tensor(out=x, in0=g1, scalar=a, in1=x, op0=ALU.mult, op1=ALU.add),
                    lambda: nc.vector.scalar_tensor_tensor(out=x, in0=g2, scalar=b, in1=x, op0=ALU.mult, op1=ALU.add)]

        transpose_stage(resid, featT)
        moe(D["expert_w_gate"][0], D["expert_w_up"][0], D["expert_w_down"][0], D["router_group_w"][0], D["router_group_b"],
            D["router_expert_w"][0], D["router_expert_b"], resid, featT, finish_a, then=ln2_loads)
        layer_norm(resid, buf[6][:, 0:DM], buf[6][:, DM:2 * DM], LN_EPS, 128)

        NHB = D["fox_b_f_2"].shape[1]
        WORK = 7 * 4096
        MOD = WORK - 6 * DM
        sh1, sc1, g1row, sh2, sc2, g2row = (work[:, MOD + i * DM:MOD + (i + 1) * DM] for i in range(6))
        T4 = lambda a, n: a.rearrange("p (t n) -> p t n", t=T)

        def modulation(l):
            n_ch = 6 * DM // BANK
            part = work[:, MOD:WORK]
            b_row = work[0:1, 0:6 * DM]
            norm = [work[:, 6 * DM:7 * DM], work[:, 7 * DM:8 * DM]]
            stage([("sum", n) for n in range(n_ch)], (), [("kept", n) for n in range(n_ch)] + [("scale", 0), ("scale", 1)])
            with nc.Block() as block:
                @block.sync
                def _(sp):
                    load(sp, b_row, D["b_ada_2"][l:l + 1, :])
                    load(sp, norm[0], D["mix_norm_2"][l:l + 1, :].partition_broadcast(P))
                    load(sp, norm[1], D["ffn_norm_2"][l:l + 1, :].partition_broadcast(P))
                    load(sp, part, ada_part[l])
                    W.issue(sp)
                row_loads = loads[0]

                @block.tensor
                def _(pe):
                    pe.wait_ge(loaded, row_loads)
                    for n in range(n_ch):
                        if n >= N_BANKS:
                            DV.wait(pe, ("kept", n - N_BANKS))
                        nc.tensor.matmul(bank[n % N_BANKS][:, :], ones[:, :], part[:, span(n)], start=True, stop=False)
                        PE.done(nc.tensor.matmul(bank[n % N_BANKS][:, :], ones[0:1, :], b_row[:, span(n)], start=False, stop=True), ("sum", n))

                @block.vector
                def _(dve):
                    for n in range(n_ch):
                        PE.wait(dve, ("sum", n))
                        DV.done(nc.vector.tensor_copy(part[:, span(n)], bank[n % N_BANKS][:, :]), ("kept", n))
                    DV.wait(dve, ("kept", n_ch - 1))
                    for i, s in enumerate((sc1, sc2)):
                        DV.done(nc.vector.scalar_tensor_tensor(out=s, in0=s, scalar=1.0, in1=norm[i],
                                                               op0=ALU.add, op1=ALU.mult), ("scale", i))

        h_tok2 = T4(work[:, 0:T * DM], DM)

        def modulated(scale, shift, dma=None):
            st = [small[:, 4 * t:4 * t + 2] for t in range(T)]

            def prep(eng_name, eng, t):
                ssq, inv = st[t][:, 0:1], st[t][:, 1:2]
                if eng_name == "act":
                    if t:
                        AC.wait(eng, ("square", t - 1))
                    AC.done(nc.scalar.activation(work[:, 4 * DM:5 * DM], resid[:, t, :], ACT.Square, accum_out=ssq), ("square", t))
                    DV.wait(eng, ("eps", t))
                    AC.done(nc.scalar.activation(inv, inv, ACT.Ln), ("log", t))
                    AC.wait(eng, ("log", t))
                    AC.done(nc.scalar.activation(inv, inv, ACT.Exp, scale=-0.5), ("inv", t))
                elif eng_name == "dve":
                    AC.wait(eng, ("square", t))
                    DV.done(nc.vector.tensor_scalar(inv, ssq, 1.0 / DM, EPS, ALU.mult, ALU.add), ("eps", t))
                    AC.wait(eng, ("inv", t))
                    DV.done(nc.vector.scalar_tensor_tensor(out=h_tok2[:, t, :], in0=resid[:, t, :], scalar=inv, in1=scale, op0=ALU.mult, op1=ALU.mult), ("scaled", t))
                else:
                    DV.wait(eng, ("scaled", t))
                    PO.done(nc.gpsimd.tensor_tensor(h_tok2[:, t, :], h_tok2[:, t, :], shift, ALU.add), ("shifted", t))
            transpose_stage(h_tok2, featT, dict(act=[("square",), ("log",), ("inv",)], dve=[("eps",), ("scaled",)], pool=[("shifted",)]),
                            prep, ready=(PO, ("shifted",)), dma=dma)

        def attention(dk, q_at, k_at, v_at, qT_at, scale, cumT=None):
            wq = NHB * dk
            q, k = (T4(work[:, a:a + T * wq], wq) for a in (q_at, k_at))
            v = T4(work[:, v_at:v_at + T * DM], DM)
            G = NHB // 2
            dkp = max(dk, 96)
            DVH = DM // NHB
            scr = featT[:, :, :].rearrange("p k s -> p (k s)")
            sx = [scr[:, i * BANK:(i + 1) * BANK] for i in range(3)]
            pT = [scr[:, (3 + i) * BANK:(4 + i) * BANK].rearrange("p (s n) -> p s n", s=T) for i in range(2)]
            cb = [scr[:, (5 + i) * BANK:(6 + i) * BANK] for i in range(2)]
            mx, rs = small[:, 64:128], small[:, 128:192]
            for grp in range(2):
                hd = range(G)
                turned = [work[0:dkp, qT_at + i * G * S:qT_at + (i + 1) * G * S].rearrange("p (h s) -> p h s", h=G) for i in range(2)]
                stage([("turn", i, h) for h in hd for i in range(2)], [("kept", 0, h) for h in hd], [("kept", 1, h) for h in hd])
                with nc.Block() as block:
                    @block.tensor
                    def _(pe):
                        for h in hd:
                            for i, x in enumerate((q, k)):
                                if h >= 4:
                                    (AC, DV)[i].wait(pe, ("kept", i, h - 4))
                                c = (grp * G + h) * dk
                                for t in range(T):
                                    last = nc.tensor.transpose(bank[2 * (h % 4) + i][0:dk, t * P:(t + 1) * P], x[:, t, c:c + dk], ident[:, :])
                                PE.done(last, ("turn", i, h))

                    @block.scalar
                    def _(act):
                        for h in hd:
                            PE.wait(act, ("turn", 0, h))
                            AC.done(nc.scalar.activation(turned[0][0:dk, h, :], bank[2 * (h % 4)][0:dk, :], ACT.Copy), ("kept", 0, h))

                    @block.vector
                    def _(dve):
                        for h in hd:
                            PE.wait(dve, ("turn", 1, h))
                            DV.done(nc.vector.tensor_copy(turned[1][0:dk, h, :], bank[2 * (h % 4) + 1][0:dk, :]), ("kept", 1, h))

                    @block.gpsimd
                    def _(pool):
                        if dkp > dk and grp == 0:
                            for i in range(2):
                                nc.gpsimd.memset(turned[i][dk:dkp, :, :], 0.0)

                units = [(h, t) for h in hd for t in range(T)]
                N = len(units)
                pe_n, cum = [], cumT is not None
                for i in range(N + 3):
                    if i < N:
                        pe_n += [("C", units[i][0])] if cum and units[i][1] == 0 else []
                        pe_n += [("S", i)]
                    pe_n += [("turn", i - 2)] if 2 <= i < N + 2 else []
                    pe_n += [("pv", i - 3)] if i >= 3 else []
                ac_n, dv_n = [], []
                for i in range(N + 1):
                    if i < N:
                        ac_n += [("C", units[i][0])] if cum and units[i][1] == 0 else []
                        ac_n += [("exp", i)]
                    if i:
                        ac_n += [("pT", i - 1)]
                for i in range(N + 2):
                    if i < N:
                        dv_n += [("scaled", i), ("max", i), ("neg", i)]
                    if i >= 2:
                        dv_n += [("inv", i - 2), ("o", i - 2)]
                stage(pe_n, ac_n, dv_n, [("masked", i) for i in range(N)])
                with nc.Block() as block:
                    @block.tensor
                    def _(pe):
                        for i in range(N + 3):
                            if i < N:
                                h, t = units[i]
                                if cum and t == 0:
                                    if h >= 2:
                                        AC.wait(pe, ("C", h - 2))
                                    hg = grp * G + h
                                    PE.done(nc.tensor.matmul(bank[6 + h % 2][:, :], bcast(ident[:, hg:hg + 1], P, P), cumT, start=True, stop=True), ("C", h))
                                if i >= 2:
                                    DV.wait(pe, ("scaled", i - 2))
                                PE.done(nc.tensor.matmul(bank[i % 2][:, 0:(t + 1) * P], turned[0][:, h, t * P:(t + 1) * P],
                                                         turned[1][:, h, 0:(t + 1) * P], start=True, stop=True), ("S", i))
                            if 2 <= i < N + 2:
                                j = i - 2
                                AC.wait(pe, ("exp", j))
                                if j >= 2:
                                    AC.wait(pe, ("pT", j - 2))
                                for s in range(units[j][1] + 1):
                                    last = nc.tensor.transpose(bank[2 + j % 2][:, s * P:(s + 1) * P], sx[j % 3][:, s * P:(s + 1) * P], ident[:, :])
                                PE.done(last, ("turn", j))
                            if i >= 3:
                                j = i - 3
                                h, t = units[j]
                                AC.wait(pe, ("pT", j))
                                if j >= 2:
                                    DV.wait(pe, ("o", j - 2))
                                c = (grp * G + h) * DVH
                                for s in range(t + 1):
                                    last = nc.tensor.matmul(bank[4 + j % 2][:, 0:DVH], pT[j % 2][:, s, :], v[:, s, c:c + DVH], start=(s == 0), stop=(s == t))
                                PE.done(last, ("pv", j))

                    @block.scalar
                    def _(act):
                        for i in range(N + 1):
                            if i < N:
                                h, t = units[i]
                                if cum and t == 0:
                                    PE.wait(act, ("C", h))
                                    if h >= 2:
                                        DV.wait(act, ("scaled", 4 * (h - 2) + 3))
                                    AC.done(nc.scalar.activation(cb[h % 2], bank[6 + h % 2][:, :], ACT.Copy), ("C", h))
                                DV.wait(act, ("neg", i))
                                e = sx[i % 3][:, 0:(t + 1) * P]
                                AC.done(nc.scalar.activation(e, e, ACT.Exp, bias=mx[:, i:i + 1], accum_out=rs[:, i:i + 1]), ("exp", i))
                            if i:
                                j = i - 1
                                n = units[j][1] + 1
                                PE.wait(act, ("turn", j))
                                if j >= 2:
                                    PE.wait(act, ("pv", j - 2))
                                AC.done(nc.scalar.activation(pT[j % 2][:, 0:n, :], bank[2 + j % 2][:, 0:n * P].rearrange("p (s n) -> p s n", s=n), ACT.Copy), ("pT", j))

                    @block.vector
                    def _(dve):
                        for i in range(N + 2):
                            if i < N:
                                h, t = units[i]
                                n = (t + 1) * P
                                PE.wait(dve, ("S", i))
                                if i >= 3:
                                    PE.wait(dve, ("turn", i - 3))
                                if cum:
                                    AC.wait(dve, ("C", h))
                                    DV.done(nc.vector.scalar_tensor_tensor(out=sx[i % 3][:, 0:n], in0=bank[i % 2][:, 0:n], scalar=scale, in1=cb[h % 2][:, 0:n],
                                                                           op0=ALU.mult, op1=ALU.subtract), ("scaled", i))
                                else:
                                    DV.done(nc.vector.tensor_scalar(sx[i % 3][:, 0:n], bank[i % 2][:, 0:n], scale, None, ALU.mult), ("scaled", i))
                                PO.wait(dve, ("masked", i))
                                DV.done(nc.vector.reduce_max(mx[:, i:i + 1], sx[i % 3][:, 0:n], X_AXIS), ("max", i))
                                DV.wait(dve, ("max", i))
                                DV.done(nc.vector.tensor_scalar(mx[:, i:i + 1], mx[:, i:i + 1], -1.0, None, ALU.mult), ("neg", i))
                            if i >= 2:
                                j = i - 2
                                h, t = units[j]
                                AC.wait(dve, ("exp", j))
                                DV.done(nc.vector.reciprocal(rs[:, j:j + 1], rs[:, j:j + 1]), ("inv", j))
                                PE.wait(dve, ("pv", j))
                                DV.wait(dve, ("inv", j))
                                c = (grp * G + h) * DVH
                                DV.done(nc.vector.tensor_scalar(k[:, t, c:c + DVH], bank[4 + j % 2][:, 0:DVH], rs[:, j:j + 1], None, ALU.mult), ("o", j))

                    @block.gpsimd
                    def _(pool):
                        for i, (h, t) in enumerate(units):
                            DV.wait(pool, ("scaled", i))
                            d = sx[i % 3][:, t * P:(t + 1) * P]
                            PO.done(nc.gpsimd.affine_select(out=d, in_=d, compare_op=ALU.is_ge, fill=-3.0e38, base=0, pattern=[[-1, P]], channel_multiplier=1), ("masked", i))

            oT2 = work[:, qT_at:qT_at + KD * S].rearrange("p (k s) -> p k s", k=KD)
            transpose_stage(k[:, :, 0:DM], oT2)
            return oT2

        def add_mixed(n, t, b, mid):
            mid(nc.vector.tensor_tensor(work[:, 0:BANK], b[:, :], g1row[:, span(n)], ALU.mult))
            return nc.vector.tensor_tensor(resid[:, t, span(n)], resid[:, t, span(n)], work[:, 0:BANK], ALU.add)

        def finish_b(t, g1, g2, a, b):
            x = resid[:, t, :]
            return [lambda: nc.vector.tensor_scalar(g1, g1, a, None, ALU.mult),
                    lambda: nc.vector.scalar_tensor_tensor(out=g1, in0=g2, scalar=b, in1=g1, op0=ALU.mult, op1=ALU.add),
                    lambda: nc.vector.tensor_tensor(g1, g1, g2row, ALU.mult),
                    lambda: nc.vector.tensor_tensor(x, x, g1, ALU.add)]

        def experts_b(l):
            modulated(sc2, sh2)
            moe(D["moe_w_gate_2"][l], D["moe_w_up_2"][l], D["moe_w_down_2"][l], D["moe_w_grp_2"][l], D["moe_b_grp_2"][l:l + 1, :],
                D["moe_w_rt_2"][l], D["moe_b_rt_2"][l:l + 1, :], h_tok2, featT, finish_b)

        FD = DM // NHB
        modulation(0)
        modulated(sc1, sh1)
        qkv_f = [T4(work[:, i * 4096:(i + 1) * 4096], DM) for i in range(3)]
        project(featT, KD, [BANK] * 6, "act",
                lambda n, t, b, mid: nc.scalar.activation(qkv_f[n // 2][:, t, span(n % 2)], b[:, :], ACT.Copy), pieces=2 * PIECES - 60)
        F0 = 5 * 4096
        cumT = work[:, F0:F0 + S]
        wf = work[:, F0 + 512:F0 + 512 + KD * NHB].rearrange("p (k n) -> p k n", k=KD)
        bf = work[:, F0 + 640:F0 + 640 + NHB]
        f_in, f_abs, f_log, f_cum = (work[:, F0 + 672 + i * 64:F0 + 736 + i * 64] for i in range(4))
        stage(["f", "cum", "cumT"], ["exp", "log", "cum", "cumT"], ["in", "neg", "abs", "low", "f"], ["zero"])
        with nc.Block() as block:
            @block.sync
            def _(sp):
                load(sp, wf, rows(D["fox_w_in_2"][0])[:, :, 3 * DM:3 * DM + NHB])
                load(sp, bf, D["fox_b_f_2"].partition_broadcast(P))
                load(sp, small[:, 256:256 + FD], D["fox_q_norm_2"].partition_broadcast(P))
                load(sp, small[:, 320:320 + FD], D["fox_k_norm_2"].partition_broadcast(P))
                wait_loads(sp)
                W.issue(sp)
            f_loads = loads[0]

            @block.tensor
            def _(pe):
                pe.wait_ge(loaded, f_loads)
                for t in range(T):
                    for k in range(KD):
                        last = nc.tensor.matmul(bank[0][:, t * NHB:(t + 1) * NHB], featT[:, k, t * P:(t + 1) * P], wf[:, k, :], start=(k == 0), stop=(k == KD - 1))
                PE.done(last, "f")
                DV.wait(pe, "f")
                for t in range(T):
                    for s in range(t + 1):
                        last = nc.tensor.matmul(bank[1][:, t * NHB:(t + 1) * NHB], (tri if s == t else ones)[:, :], f_log[:, s * NHB:(s + 1) * NHB],
                                                start=(s == 0), stop=(s == t))
                PE.done(last, "cum")
                AC.wait(pe, "cum")
                for t in range(T):
                    last = nc.tensor.transpose(bank[2][0:NHB, t * P:(t + 1) * P], f_cum[:, t * NHB:(t + 1) * NHB], ident[:, :])
                PE.done(last, "cumT")

            @block.vector
            def _(dve):
                dve.wait_ge(loaded, f_loads)
                PE.wait(dve, "f")
                DV.done(nc.vector.tensor_tensor(T4(f_in, NHB), T4(bank[0][:, 0:T * NHB], NHB), bcast(bf.unsqueeze(1), P, T, NHB), ALU.add), "in")
                DV.wait(dve, "in")
                DV.done(nc.vector.tensor_scalar(f_abs, f_in, -1.0, None, ALU.mult), "neg")
                DV.wait(dve, "neg")
                DV.done(nc.vector.tensor_tensor(f_abs, f_abs, f_in, ALU.min), "abs")
                DV.done(nc.vector.tensor_scalar(f_in, f_in, 0.0, None, ALU.min), "low")
                AC.wait(dve, "log")
                DV.wait(dve, "low")
                DV.done(nc.vector.tensor_tensor(f_log, f_in, f_abs, ALU.subtract), "f")

            @block.scalar
            def _(act):
                DV.wait(act, "abs")
                AC.done(nc.scalar.activation(f_abs, f_abs, ACT.Exp), "exp")
                AC.wait(act, "exp")
                AC.done(nc.scalar.activation(f_abs, f_abs, ACT.Ln, bias=1.0), "log")
                PE.wait(act, "cum")
                AC.done(nc.scalar.activation(f_cum, bank[1][:, 0:T * NHB], ACT.Copy), "cum")
                PE.wait(act, "cumT")
                PO.wait(act, "zero")
                AC.done(nc.scalar.activation(cumT[0:NHB, :], bank[2][0:NHB, :], ACT.Copy), "cumT")

            @block.gpsimd
            def _(pool):
                PO.done(nc.gpsimd.memset(cumT, 0.0), "zero")

        hd_view = lambda x, w: (lambda t: x[:, t, 0:NHB * w].rearrange("p (h n) -> p h n", h=NHB))
        rms_stage(hd_view(qkv_f[0], FD), NHB, FD, EPS, gain=small[:, 256:256 + FD], scratch=work[:, 4 * 4096:4 * 4096 + DM])
        rms_stage(hd_view(qkv_f[1], FD), NHB, FD, EPS, gain=small[:, 320:320 + FD], scratch=work[:, 4 * 4096:4 * 4096 + DM])
        oT2 = attention(FD, 0, 4096, 8192, 3 * 4096, FD ** -0.5, cumT)
        project(oT2, KD, [BANK] * 2, "dve", add_mixed, mids=1)
        experts_b(0)

        QR, KR = D["mla_q_lat_norm_2"].shape[1], D["mla_kv_lat_norm_2"].shape[1]
        QK = D["mla_q_norm_2"].shape[1]
        LAT = D["mla_w_in_2"].shape[2]
        ROPE = LAT - QR - KR
        NOPE, HALF = QK - ROPE, ROPE // 2
        modulation(1)
        modulated(sc1, sh1)
        V0, QT0 = 2 * T * NHB * QK, 2 * T * NHB * QK + 4096
        lat = T4(work[:, QT0:QT0 + T * LAT], LAT)
        project(featT, KD, [BANK, LAT - BANK], "act",
                lambda n, t, b, mid: nc.scalar.activation(lat[:, t, n * BANK:min((n + 1) * BANK, LAT)], b[:, 0:min(BANK, LAT - n * BANK)], ACT.Copy))
        gq, gkv = work[:, V0:V0 + QR], work[:, V0 + QR:V0 + QR + KR]

        def lat_loads(sp):
            load(sp, gq, D["mla_q_lat_norm_2"].partition_broadcast(P))
            load(sp, gkv, D["mla_kv_lat_norm_2"].partition_broadcast(P))
            load(sp, small[:, 192:192 + QK], D["mla_q_norm_2"].partition_broadcast(P))
            load(sp, small[:, 288:288 + QK], D["mla_k_norm_2"].partition_broadcast(P))
            load(sp, pos_rows, D["positions_2"].rearrange("b (t p) -> (b t) p", p=P))

        pos_rows = work[0:T, 0:P].bitcast(I32)
        posf = work[0:T, P:2 * P]
        TR = T * HALF
        ang, turns, res, freq, cos, sin = (work[:, V0 + 704 + i * TR:V0 + 704 + (i + 1) * TR] for i in range(6))
        TWO_PI = 6.283185307179586
        C1 = 6.28125
        C2 = float(int((TWO_PI - C1) * 2 ** 21)) / 2 ** 21
        C3 = TWO_PI - C1 - C2
        PI_F = 3.1415925
        ROUND = 12582912.0
        stage(["pos"], ["sin"], links("rope", 13) + ["cos_in"], links("freq", HALF))
        with nc.Block() as block:
            @block.sync
            def _(sp):
                lat_loads(sp)
                wait_loads(sp)
                W.issue(sp)
            pos_loads = loads[0]

            @block.gpsimd
            def _(pool):
                link = chain(PO, pool, "freq")
                for i in range(HALF):
                    link(nc.gpsimd.memset(freq[:, i:i + 1], 10000.0 ** (-i / HALF)))

            @block.tensor
            def _(pe):
                DV.wait(pe, ("rope", 0))
                PE.done(nc.tensor.transpose(bank[0][:, 0:T], posf, ident[0:T, 0:T]), "pos")

            @block.vector
            def _(dve):
                link = chain(DV, dve, "rope")
                V = nc.vector
                dve.wait_ge(loaded, pos_loads)
                link(V.tensor_copy(posf, pos_rows))
                PE.wait(dve, "pos")
                link(V.tensor_copy(small[:, 0:T], bank[0][:, 0:T]))
                PO.wait(dve, ("freq", HALF - 1))
                link(V.tensor_tensor(T4(ang, HALF), bcast(small[:, 0:T].unsqueeze(2), P, T, HALF), bcast(freq[:, 0:HALF].unsqueeze(1), P, T, HALF), ALU.mult))
                link(V.tensor_scalar(turns, ang, 1.0 / TWO_PI, None, ALU.mult))
                link(V.tensor_scalar(turns, turns, ROUND, None, ALU.add))
                link(V.tensor_scalar(turns, turns, ROUND, None, ALU.subtract))
                for c in (C1, C2, C3):
                    link(V.scalar_tensor_tensor(out=ang, in0=turns, scalar=-c, in1=ang, op0=ALU.mult, op1=ALU.add))
                link(V.tensor_scalar(res, ang, TWO_PI / 4, None, ALU.add))
                link(V.tensor_scalar(turns, res, PI_F, -TWO_PI, ALU.is_gt, ALU.mult))
                link(V.tensor_tensor(res, res, turns, ALU.add))
                link(V.tensor_scalar(ang, ang, PI_F, -PI_F, ALU.min, ALU.max))
                DV.done(V.tensor_scalar(res, res, PI_F, -PI_F, ALU.min, ALU.max), "cos_in")

            @block.scalar
            def _(act):
                DV.wait(act, "cos_in")
                nc.scalar.activation(sin, ang, ACT.Sin)
                AC.done(nc.scalar.activation(cos, res, ACT.Sin), "sin")

        rms_stage(lambda t: lat[:, t, 0:QR].unsqueeze(1), 1, QR, EPS, gain=gq, scratch=work[:, 0:QR])
        rms_stage(lambda t: lat[:, t, QR:QR + KR].unsqueeze(1), 1, KR, EPS, gain=gkv, scratch=work[:, 0:KR])
        latT = featT
        transpose_stage(lat, latT, blocks=(QR + KR) // P)

        q_m, k_m = (T4(work[:, i * T * NHB * QK:(i + 1) * T * NHB * QK], NHB * QK) for i in range(2))
        v_m = T4(work[:, V0:V0 + 4096], DM)
        rt = [work[:, MOD + i * NHB * HALF:MOD + (i + 1) * NHB * HALF].rearrange("p (h n) -> p h n", h=NHB) for i in range(4)]
        trig = [work[:, MOD + 1024 + i * TR:MOD + 1024 + (i + 1) * TR] for i in range(2)]
        krope = work[:, MOD + 1152:MOD + 1152 + T * ROPE]
        stage((), (), ["cos", "sin", "krope"])
        with nc.Block() as block:
            @block.vector
            def _(dve):
                DV.done(nc.vector.tensor_copy(trig[0], cos), "cos")
                DV.done(nc.vector.tensor_copy(trig[1], sin), "sin")
                DV.done(nc.vector.tensor_copy(T4(krope, ROPE), lat[:, :, QR + KR:LAT]), "krope")

        def rope_of(x):
            def after(t, dry=False):
                v = x[:, t, :].rearrange("p (h n) -> p h n", h=NHB)
                x1, x2 = v[:, :, NOPE:NOPE + HALF], v[:, :, NOPE + HALF:QK]
                c, s = (bcast(T4(a, HALF)[:, t, :].unsqueeze(1), P, NHB, HALF) for a in trig)
                tt = lambda o, a, b, op: (lambda: nc.vector.tensor_tensor(o, a, b, op))
                return [tt(rt[0], x1, c, ALU.mult), tt(rt[1], x2, s, ALU.mult), tt(rt[2], x1, s, ALU.mult), tt(rt[3], x2, c, ALU.mult),
                        tt(x1, rt[0], rt[1], ALU.subtract), tt(x2, rt[2], rt[3], ALU.add)]
            return after
        project(latT, QR // P, [BANK] * (NHB * QK // BANK), "act",
                lambda n, t, b, mid: nc.scalar.activation(q_m[:, t, span(n)], b[:, :], ACT.Copy))

        HPB = BANK // P

        def keys_values(n, t, b, mid):
            kv = b[:, :].rearrange("p (h n) -> p h n", h=HPB)
            kd_ = k_m[:, t, :].rearrange("p (h n) -> p h n", h=NHB)[:, n * HPB:(n + 1) * HPB, 0:NOPE]
            mid(nc.scalar.activation(kd_, kv[:, :, 0:NOPE], ACT.Copy))
            vd_ = v_m[:, t, :].rearrange("p (h n) -> p h n", h=NHB)[:, n * HPB:(n + 1) * HPB, :]
            return nc.scalar.activation(vd_, kv[:, :, NOPE:P], ACT.Copy)
        project(latT[:, QR // P:(QR + KR) // P, :], KR // P, [BANK] * 4, "act", keys_values, mids=1)
        stage((), (), [("krope", t) for t in range(T)])
        with nc.Block() as block:
            @block.vector
            def _(dve):
                for t in range(T):
                    DV.done(nc.vector.tensor_copy(k_m[:, t, :].rearrange("p (h n) -> p h n", h=NHB)[:, :, NOPE:QK],
                                                  bcast(T4(krope, ROPE)[:, t, :].unsqueeze(1), P, NHB, ROPE)), ("krope", t))
        rms_stage(hd_view(q_m, QK), NHB, QK, EPS, gain=small[:, 192:192 + QK], after=rope_of(q_m), scratch=work[:, QT0:QT0 + NHB * QK])
        rms_stage(hd_view(k_m, QK), NHB, QK, EPS, gain=small[:, 288:288 + QK], after=rope_of(k_m), scratch=work[:, QT0:QT0 + NHB * QK])
        oT3 = attention(QK, 0, T * NHB * QK, V0, QT0, QK ** -0.5)
        project(oT3, KD, [BANK] * 2, "dve", add_mixed, mids=1)
        experts_b(1)

        stage()
        with nc.Block() as block:
            @block.sync
            def _(sp):
                stored = sem("stored")
                sp.dma_start(OUT[0].rearrange("(t p) n -> p t n", p=P), resid[:, :, :]).then_inc(stored, 16)
                sp.wait_ge(stored, 16)


def kernel(**inputs):
    import numpy as np
    import concourse.bacc as bacc
    from concourse.bass_utils import run_bass_kernel_spmd

    nc = bacc.Bacc("TRN2", target_bir_lowering=False, num_devices=1)
    arrays, dram = {}, {}
    for name, value in inputs.items():
        arrays["in_" + name] = np.ascontiguousarray(value)
        dram[name] = nc.dram_tensor("in_" + name, arrays["in_" + name].shape, mybir.dt.from_np(arrays["in_" + name].dtype),
                                    kind="ExternalInput").ap()
    out = nc.dram_tensor("out", inputs["x"].shape, F32, kind="ExternalOutput").ap()
    build(nc, dram, out)
    result = run_bass_kernel_spmd(nc, [arrays], core_ids=[0])
    return result.results[0]["out"]
```

```python
from contextlib import ExitStack

import concourse.bass as bass
from concourse import mybir

ALU = mybir.AluOpType
ACT = mybir.ActivationFunctionType
F32 = mybir.dt.float32
I32 = mybir.dt.int32
X_AXIS = mybir.AxisListType.X

P = 128
BANK = 512
N_BANKS = 8
RING = 4
SLOT = 4096


class Steps:

    def __init__(self, sem):
        self.sem, self.made, self.at, self.due = sem, 0, 0, 0

    def begin(self, names, rounds=1):
        assert self.at == self.due, "a stage's steps have all been made"
        self.names, self.rounds, self.base, self.at = list(names), rounds, self.made, 0
        assert len(set(self.names)) == len(self.names)
        self.made += len(self.names) * rounds
        self.due = len(self.names) * rounds

    def value(self, name, i=0):
        return i * len(self.names) + (self.base + self.names.index(name) + 1)

    def done(self, ins, name):
        assert self.names[self.at % len(self.names)] == name, (name, self.names[self.at % len(self.names)])
        self.at += 1
        ins.then_inc(self.sem, 1)

    def wait(self, eng, name, i=0):
        eng.wait_ge(self.sem, self.value(name, i))


class Weights:

    def __init__(self, ring, landed):
        self.ring, self.landed = ring, landed
        self.chunks, self.slots, self.ready, self.used = [], [], [], {}
        self.count = [0] * RING
        self.issued = self.taken = 0
        self.turn = 1

    def plan(self, parts, slot=None, by_loop=False):
        if slot is None:
            self.turn = 1 - self.turn
            slot = self.turn
        self.chunks.append(parts)
        self.slots.append(slot)
        self.count[slot] += 16 * len(parts)
        if by_loop:
            self.chunks[-1] = None
        self.ready.append(self.count[slot])

    def take(self, n):
        first = self.taken
        self.taken += n
        return range(first, first + n)

    def slot(self, chunk):
        return self.ring[self.slots[chunk]]

    def wait_landed(self, eng, chunk):
        eng.wait_ge(self.landed[self.slots[chunk]], self.ready[chunk])

    def mark_used(self, chunk, sem, value):
        self.used[chunk] = (sem, value)

    def before(self, chunk):
        older = [c for c in range(chunk) if self.slots[c] == self.slots[chunk]]
        return older[-1] if older else None

    def issue(self, sp, most=None):
        most = len(self.chunks) if most is None else most
        end = self.issued + most
        while self.issued < end and self.issued < len(self.chunks) and self.chunks[self.issued] is not None:
            old = self.before(self.issued)
            if old is not None:
                if old not in self.used:
                    return
                sp.wait_ge(*self.used[old])
            for dst, src in self.chunks[self.issued]:
                sp.dma_start(dst(self.slot(self.issued)), src).then_inc(self.landed[self.slots[self.issued]], 16)
            self.issued += 1


def build(nc, D, OUT, stop=None):
    S, DM = D["x"].shape[1], D["x"].shape[2]
    T = S // P
    KD = DM // P
    H = D["a_log"].shape[1]
    CONV = D["conv_w"].shape[1]
    DN = H * D["dn_norm_g"].shape[1]
    SG = D["spatial_w"].shape[1]
    GD_OFF = 4 * DN + 2 * H + 2 * SG * P
    UV_OFF = 4 * DN + 2 * H
    NG = D["router_group_w"].shape[2]
    NE = D["router_expert_w"].shape[2]
    PER = NE // NG
    FF = D["expert_w_gate"].shape[3]
    KF = FF // P
    LN_EPS, EPS = 1e-5, 1e-6
    ALPHA = 2.0 ** 0.25

    ctx = ExitStack()
    with ctx:
        def sb(name, shape, dt=F32):
            return ctx.enter_context(nc.sbuf_tensor(name, shape, dt))

        def sem(name):
            return ctx.enter_context(nc.semaphore(name))

        bank = [ctx.enter_context(nc.psum_tensor(f"bank{i}", [P, BANK], F32)) for i in range(N_BANKS)]
        ident = sb("ident", [P, P])
        tri = sb("tri", [P, P])
        strict = sb("strict", [P, P])
        ones = sb("ones", [P, P])
        level_mask = sb("level_mask", [P, 7, P])
        resid = sb("resid", [P, T, DM])
        featT = sb("featT", [P, KD, S])
        ring = [sb(f"ring{i}", [P, SLOT if i < 2 else SLOT // 2]) for i in range(RING)]
        work = sb("work", [P, 7 * 4096])
        buf = [work[:, i * 4096:(i + 1) * 4096] for i in range(7)]
        state = sb("state", [P, H * P])
        ada_w = [state, sb("ada_w", [P, KD * P])]
        small = sb("small", [P, 512])
        ismall = sb("ismall", [P, 64], I32)

        def tok(b):
            return b[:, :].rearrange("p (t n) -> p t n", t=T)

        def bcast(ap, *shape):
            return ap.to_broadcast(list(shape))

        N_MAIN, N_EXTRA = NE, (2 * S - NE) // P
        ROWS = (N_MAIN + N_EXTRA) * P
        x_rows = nc.dram_tensor("x_rows", [ROWS, DM], F32, kind="Internal").ap()
        y_rows = nc.dram_tensor("y_rows", [ROWS, DM], F32, kind="Internal").ap()
        ada_part = nc.dram_tensor("ada_part", [2, P, 6 * DM], F32, kind="Internal").ap()

        PE, AC, DV, PO = (Steps(sem(n)) for n in ("pe_steps", "act_steps", "dve_steps", "pool_steps"))
        loaded = sem("loaded")
        loads = [0]
        W = Weights(ring, [sem(f"slot{i}_landed") for i in range(RING)])

        def load(eng, dst, src):
            eng.dma_start(dst, src).then_inc(loaded, 16)
            loads[0] += 16

        def wait_loads(eng):
            eng.wait_ge(loaded, loads[0])

        def rows(w):
            return w.rearrange("(k p) n -> p k n", p=P)

        def plan_cols(w, lo, hi, step=BANK):
            k = w.shape[0] // P
            for c in range(lo, hi, step):
                n = min(step, hi - c)
                W.plan([(lambda s, k=k, n=n: s[:, 0:k * n].rearrange("p (k n) -> p k n", k=k), rows(w)[:, :, c:c + n])])  

        def plan_experts(gate, up, down):
            for e in range(NE):
                gu = [(lambda s, i=i: s[:, :].rearrange("p (k g n) -> p k g n", k=KD, g=2)[:, :, i, :], rows(w[e]))
                      for i, w in enumerate((gate, up))]
                dn = [(lambda s: s[:, 0:KF * DM].rearrange("p (k n) -> p k n", k=KF), rows(down[e]))]
                W.plan(gu, e % 2, by_loop=e >= 2)
                W.plan(dn, 2 + e % 2, by_loop=e >= 2)

        w_in = D["w_in"][0]
        plan_cols(w_in, UV_OFF, UV_OFF + 2 * SG * P)
        plan_cols(w_in, GD_OFF + DM, GD_OFF + 2 * DM)
        plan_cols(D["w_sgu_out"][0], 0, DM)
        plan_cols(w_in, 0, 3 * DN)
        plan_cols(w_in, 3 * DN, 4 * DN)
        plan_cols(w_in, GD_OFF, GD_OFF + DM)
        plan_cols(D["w_dn_out"][0], 0, DM)
        plan_cols(D["w_out"][0], 0, DM)
        plan_experts(D["expert_w_gate"][0], D["expert_w_up"][0], D["expert_w_down"][0])
        plan_cols(D["fox_w_in_2"][0], 0, 3 * DM)
        plan_cols(D["fox_w_out_2"][0], 0, DM)
        plan_experts(D["moe_w_gate_2"][0], D["moe_w_up_2"][0], D["moe_w_down_2"][0])
        plan_cols(D["mla_w_in_2"][0], 0, D["mla_w_in_2"].shape[2])
        plan_cols(D["mla_w_uq_2"][0], 0, D["mla_w_uq_2"].shape[2])
        plan_cols(D["mla_w_ukv_2"][0], 0, D["mla_w_ukv_2"].shape[2])
        plan_cols(D["mla_w_out_2"][0], 0, DM)
        plan_experts(D["moe_w_gate_2"][1], D["moe_w_up_2"][1], D["moe_w_down_2"][1])

        def stage(pe=(), act=(), dve=(), pool=(), rounds=1):
            for s, names in ((PE, pe), (AC, act), (DV, dve), (PO, pool)):
                s.begin(names, rounds)

        def transpose_stage(src, dst, prep_names=(), prep=None, ready=None, dma=None, blocks=KD):
            names = prep_names or {}
            tiles = range(T)
            pe_n = [("turned", t, h) for t in tiles for h in range(2)]
            ac_n = names.get("act", []) + [("kept", t, 0) for t in tiles]
            dv_n = names.get("dve", []) + [("kept", t, 1) for t in tiles]
            po_n = names.get("pool", [])
            stage(pe_n, ac_n, dv_n, po_n)
            with nc.Block() as block:
                @block.tensor
                def _(pe):
                    for t in tiles:
                        if ready:
                            ready[0].wait(pe, ready[1] + (t,))
                        for h in range(2):
                            b = bank[2 * t + h]
                            for j in range(min(4, blocks - 4 * h)):
                                k = 4 * h + j
                                last = nc.tensor.transpose(b[:, j * P:(j + 1) * P], src[:, t, k * P:(k + 1) * P], ident[:, :])
                            PE.done(last, ("turned", t, h))

                def keep(eng, S_, copy, h):
                    for t in tiles:
                        PE.wait(eng, ("turned", t, h))
                        m = min(4, blocks - 4 * h)
                        S_.done(copy(dst[:, 4 * h:4 * h + m, t * P:(t + 1) * P],
                                     bank[2 * t + h][:, 0:m * P].rearrange("p (j n) -> p j n", j=m)), ("kept", t, h))

                @block.scalar
                def _(act):
                    if prep:
                        prep("act", act)
                    keep(act, AC, lambda o, i: nc.scalar.activation(o, i, ACT.Copy), 0)

                @block.vector
                def _(dve):
                    if prep:
                        prep("dve", dve)
                    keep(dve, DV, lambda o, i: nc.vector.tensor_copy(o, i), 1)

                @block.gpsimd
                def _(pool):
                    if prep:
                        prep("pool", pool)

                @block.sync
                def _(sp):
                    if dma:
                        dma(sp)
                    W.issue(sp)

        ada_landed, ada_stored = ([sem(f"ada_{what}{i}") for i in range(2)] for what in ("landed", "stored"))
        PIECES = 6 * DM // P
        ada_done = [0]

        def load_piece(eng, i):
            w = rows(D["w_ada_2"][i // PIECES])[:, :, (i % PIECES) * P:(i % PIECES + 1) * P]
            eng.dma_start(ada_w[i % 2][:, :].rearrange("p (k n) -> p k n", k=KD), w).then_inc(ada_landed[i % 2], 16)

        piece_sum = [buf[3][:, 2048 + i * P:2048 + (i + 1) * P] for i in range(2)]

        def store_piece(eng, i):
            q = i % PIECES
            eng.dma_start(ada_part[i // PIECES, :, q * P:(q + 1) * P], piece_sum[i % 2]).then_inc(ada_stored[i % 2], 16)

        def project(srcT, kblocks, widths, by, drain, mids=0, pieces=0):
            ids = W.take(len(widths))
            jobs = [(n, t) for n in range(len(widths)) for t in range(T)]
            drains = [(kind, n, t) for n, t in jobs for kind in ["mid%d" % m for m in range(mids)] + ["drained"]]
            beside = range(ada_done[0], ada_done[0] + pieces)
            ada_done[0] += pieces
            stage([("sum", n, t) for n, t in jobs], drains if by == "act" else (),
                  drains if by == "dve" else [("piece", i, m) for i in beside for m in range(4)])
            taker = AC if by == "act" else DV
            with nc.Block() as block:
                @block.tensor
                def _(pe):
                    for n, width in enumerate(widths):
                        W.wait_landed(pe, ids[n])
                        w = W.slot(ids[n])[:, 0:kblocks * width].rearrange("p (k n) -> p k n", k=kblocks)
                        for t in range(T):
                            j = n * T + t
                            if j >= N_BANKS:
                                taker.wait(pe, ("drained",) + jobs[j - N_BANKS])
                            b = bank[j % N_BANKS]
                            for k in range(kblocks):
                                last = nc.tensor.matmul(b[:, 0:width], srcT[:, k, t * P:(t + 1) * P], w[:, k, :],
                                                        start=(k == 0), stop=(k == kblocks - 1))
                            PE.done(last, ("sum", n, t))
                        W.mark_used(ids[n], PE.sem, PE.value(("sum", n, T - 1)))

                def take_away(eng):
                    for j, (n, t) in enumerate(jobs):
                        m = [0]

                        def mid(ins):
                            taker.done(ins, ("mid%d" % m[0], n, t))
                            taker.wait(eng, ("mid%d" % m[0], n, t))
                            m[0] += 1
                        if mids and j:
                            taker.wait(eng, ("drained",) + jobs[j - 1])
                        PE.wait(eng, ("sum", n, t))
                        taker.done(drain(n, t, bank[j % N_BANKS], mid), ("drained", n, t))
                @block.scalar
                def _(act):
                    if by == "act":
                        take_away(act)

                @block.vector
                def _(dve):
                    if by == "dve":
                        take_away(dve)
                    for i in beside if by == "act" else ():
                        w = ada_w[i % 2][:, :].rearrange("p (k n) -> p k n", k=KD)
                        dve.wait_ge(ada_landed[i % 2], 16 * (i // 2 + 1))
                        DV.done(nc.vector.tensor_tensor(w, w, bcast(c_cols.unsqueeze(2), P, KD, P), ALU.mult), ("piece", i, 0))
                        for m in range(1, 4):
                            DV.wait(dve, ("piece", i, m - 1))
                            if m == 3 and i >= 2:
                                dve.wait_ge(ada_stored[i % 2], 16 * (i // 2))
                            n = KD >> m
                            out = w[:, 0:n, :] if m < 3 else piece_sum[i % 2].unsqueeze(1)
                            DV.done(nc.vector.tensor_tensor(out, w[:, 0:n, :], w[:, n:2 * n, :], ALU.add), ("piece", i, m))

                @block.sync
                def _(sp):
                    for k in range(pieces + 2 if pieces else 0):
                        if k < pieces:
                            if k >= 2:
                                DV.wait(sp, ("piece", beside[k - 2], 3))
                            load_piece(sp, beside[k])
                        if k >= 2:
                            DV.wait(sp, ("piece", beside[k - 2], 3))
                            store_piece(sp, beside[k - 2])
                        if (k + 1) * len(widths) % (pieces + 2) < len(widths):
                            W.issue(sp, 1)
                    for i in beside[-2:]:
                        sp.wait_ge(ada_stored[i % 2], 16 * (i // 2 + 1))
                    W.issue(sp)

        def chain(steps, eng, name):
            n = [0]

            def link(ins):
                steps.done(ins, (name, n[0]))
                steps.wait(eng, (name, n[0]))
                n[0] += 1
            return link

        def links(name, n):
            return [(name, i) for i in range(n)]

        def span(t, half=BANK):
            return slice(t * half, (t + 1) * half)

        x_tok = D["x"][0].rearrange("(t p) n -> p t n", p=P)
        NCR = CONV * 3 * DN // P
        conv_rows = buf[5][0:NCR + SG, 0:P]
        sp_nat = buf[2][:, 2048:3072].rearrange("p (g s) -> p g s", g=SG)
        spT = buf[2][:, 3072:4096].rearrange("p (g t) -> p g t", g=SG)
        sp_bias = small[:, 16 + NCR:16 + NCR + SG]
        conv_cols = small[:, 16:16 + CONV * 3 * DN // P].rearrange("p (w b) -> p w b", w=CONV)
        ab_w = buf[6][:, 0:KD * 2 * H].rearrange("p (k n) -> p k n", k=KD)
        NL = 7
        c_rows = buf[5][0:KD, P:2 * P]
        c_cols = ismall[:, 48:48 + KD].bitcast(F32)
        stage(dve=links("zero", 1), pool=links("const", 6 + 3 * NL))
        with nc.Block() as block:
            @block.sync
            def _(sp):
                load(sp, resid[:, :, :], x_tok)
                load(sp, c_rows, D["c_2"][0].rearrange("(k p) -> k p", p=P))
                load(sp, sp_nat, D["spatial_w"][0].rearrange("g t s -> t g s"))
                load(sp, buf[2][:, 0:DM], D["sgu_ln_g"].partition_broadcast(P))
                load(sp, buf[2][:, DM:2 * DM], D["sgu_ln_b"].partition_broadcast(P))
                load(sp, conv_rows[NCR:NCR + SG, :], D["spatial_b"][0])
                load(sp, conv_rows[0:NCR, :], D["conv_w"][0].rearrange("w (b p) -> (w b) p", p=P))
                wait_loads(sp)
                W.issue(sp)

            @block.vector
            def _(dve):
                chain(DV, dve, "zero")(nc.vector.memset(buf[6][:, 3 * DM:4 * DM], 0.0))

            @block.gpsimd
            def _(pool):
                link = chain(PO, pool, "const")
                keep_where = dict(in_=ones[:, :], pattern=[[1, P]], channel_multiplier=-1)
                link(nc.gpsimd.memset(ones[:, :], 1.0))
                link(nc.gpsimd.affine_select(out=ident[:, :], compare_op=ALU.is_equal, fill=0.0, base=0, **keep_where))
                link(nc.gpsimd.affine_select(out=tri[:, :], compare_op=ALU.is_ge, fill=0.0, base=0, **keep_where))
                link(nc.gpsimd.affine_select(out=strict[:, :], compare_op=ALU.is_ge, fill=0.0, base=-1, **keep_where))
                for i in range(NL):
                    b = 1 << i
                    m = level_mask[:, i, :].rearrange("p (m c) -> p m c", c=2 * b)
                    o = ones[:, :].rearrange("p (m c) -> p m c", c=2 * b)
                    pairs = P // (2 * b)
                    link(nc.gpsimd.affine_select(out=m, in_=o, compare_op=ALU.is_ge, fill=0.0, base=0,
                                                 pattern=[[-2 * b, pairs], [0, 2 * b]], channel_multiplier=1))
                    link(nc.gpsimd.affine_select(out=m, in_=m, compare_op=ALU.is_ge, fill=0.0, base=b - 1,
                                                 pattern=[[2 * b, pairs], [0, 2 * b]], channel_multiplier=-1))
                    link(nc.gpsimd.memset(m[:, :, 0:b], 0.0))
                link(nc.gpsimd.iota(ismall[:, 0:16], pattern=[[1, 16]], base=0, channel_multiplier=0))
                link(nc.gpsimd.tensor_copy(small[:, 496:512], ismall[:, 0:16]))

        stage([("spT", 0), ("spT", 1), "conv", "c"], ["conv", "c"], [("spT", 0), ("spT", 1)], [])
        with nc.Block() as block:
            @block.tensor
            def _(pe):
                for h in range(2):
                    for j in range(4):
                        last = nc.tensor.transpose(bank[h][:, j * P:(j + 1) * P], sp_nat[:, 4 * h + j, :], ident[:, :])
                    PE.done(last, ("spT", h))
                n = conv_rows.shape[0]
                PE.done(nc.tensor.transpose(bank[2][:, 0:n], conv_rows, ident[0:n, 0:n]), "conv")
                PE.done(nc.tensor.transpose(bank[3][:, 0:KD], c_rows, ident[0:KD, 0:KD]), "c")

            @block.vector
            def _(dve):
                for h in range(2):
                    PE.wait(dve, ("spT", h))
                    DV.done(nc.vector.tensor_tensor(spT[:, 4 * h:4 * h + 4, :], bank[h][:, :].rearrange("p (j n) -> p j n", j=4),
                                                    bcast(tri[:, :].unsqueeze(1), P, 4, P), ALU.mult), ("spT", h))

            @block.scalar
            def _(act):
                PE.wait(act, "conv")
                AC.done(nc.scalar.activation(small[:, 16:16 + conv_rows.shape[0]], bank[2][:, 0:conv_rows.shape[0]], ACT.Copy), "conv")
                PE.wait(act, "c")
                AC.done(nc.scalar.activation(c_cols, bank[3][:, 0:KD], ACT.Silu), "c")

        zero_filled = sem("rows_zeroed")

        transpose_stage(resid, featT)

        u_tok, v_tok, y_tok, gate = tok(buf[0]), tok(buf[1]), tok(buf[4]), tok(buf[5])
        uv = [u_tok, v_tok]
        project(featT, KD, [BANK] * 4, "act",
                lambda n, t, b, mid: nc.scalar.activation(uv[n // 2][:, t, span(n % 2)], b[:, :], ACT.Gelu), pieces=24)
        project(featT, KD, [BANK] * 2, "act",
                lambda n, t, b, mid: nc.scalar.activation(gate[:, t, span(n)], b[:, :], ACT.Sigmoid), pieces=12)

        def layer_norm(x, gain, bias, eps, at, then=None):
            n_t = x.shape[1]
            tiles = range(n_t)
            stage((), ["log", "rstd"], [(w, t) for t in tiles for w in ("half0", "half1")] + [("mean", t) for t in tiles] + ["eps"]
                  + [(w, t) for t in tiles for w in ("gain", "bias")])
            st = [small[:, at + 12 * t:at + 12 * t + 12] for t in tiles]
            mv = small[:, at + 12 * n_t:at + 14 * n_t].rearrange("p (t n) -> p t n", n=2)
            rstd = small[:, at + 14 * n_t:at + 15 * n_t]
            with nc.Block() as block:
                @block.vector
                def _(dve):
                    for t in tiles:
                        for h in range(2):
                            DV.done(nc.vector.bn_stats(st[t][:, 6 * h:6 * h + 6], x[:, t, span(h)]), ("half%d" % h, t))
                    for t in tiles:
                        DV.wait(dve, ("half1", t))
                        DV.done(nc.vector.bn_aggr(mv[:, t, :], st[t].rearrange("p (a b) -> p a b", a=2)), ("mean", t))
                    DV.wait(dve, ("mean", n_t - 1))
                    DV.done(nc.vector.tensor_scalar_add(rstd, mv[:, :, 1], eps), "eps")
                    AC.wait(dve, "rstd")
                    for t in tiles:
                        DV.done(nc.vector.scalar_tensor_tensor(out=x[:, t, :], in0=x[:, t, :], scalar=mv[:, t, 0:1], in1=gain,
                                                               op0=ALU.subtract, op1=ALU.mult), ("gain", t))
                        DV.wait(dve, ("gain", t))
                        DV.done(nc.vector.scalar_tensor_tensor(out=x[:, t, :], in0=x[:, t, :], scalar=rstd[:, t:t + 1], in1=bias,
                                                               op0=ALU.mult, op1=ALU.add), ("bias", t))

                @block.scalar
                def _(act):
                    DV.wait(act, "eps")
                    AC.done(nc.scalar.activation(rstd, rstd, ACT.Ln), "log")
                    AC.wait(act, "log")
                    AC.done(nc.scalar.activation(rstd, rstd, ACT.Exp, scale=-0.5), "rstd")

                @block.sync
                def _(sp):
                    if then:
                        then(sp)
                    W.issue(sp)

        layer_norm(v_tok, buf[2][:, 0:DM], buf[2][:, DM:2 * DM], LN_EPS, 128)

        jobs = [(t, h) for t in range(T) for h in range(2)]
        stage([("mix",) + j for j in jobs], (), [("bias",) + j + (g,) for j in jobs for g in range(4)] )
        with nc.Block() as block:
            @block.tensor
            def _(pe):
                for t, h in jobs:
                    for g in range(4):
                        last = nc.tensor.matmul(bank[2 * t + h][:, g * P:(g + 1) * P], spT[:, 4 * h + g, :],
                                                v_tok[:, t, (4 * h + g) * P:(4 * h + g + 1) * P], start=True, stop=True)
                    PE.done(last, ("mix", t, h))

            @block.vector
            def _(dve):
                for t, h in jobs:
                    PE.wait(dve, ("mix", t, h))
                    for g in range(4):
                        c = slice((4 * h + g) * P, (4 * h + g + 1) * P)
                        DV.done(nc.vector.scalar_tensor_tensor(
                            out=u_tok[:, t, c], in0=bank[2 * t + h][:, g * P:(g + 1) * P], scalar=sp_bias[:, 4 * h + g:4 * h + g + 1],
                            in1=u_tok[:, t, c], op0=ALU.add, op1=ALU.mult), ("bias", t, h, g))
        gatedT = buf[1][:, :].rearrange("p (k s) -> p k s", k=KD)
        transpose_stage(u_tok, gatedT)
        project(gatedT, KD, [BANK] * 2, "dve",
                lambda n, t, b, mid: nc.vector.tensor_tensor(y_tok[:, t, span(n)], b[:, :], gate[:, t, span(n)], ALU.mult))

        q_tok, k_tok, vd_tok = tok(buf[0]), tok(buf[1]), tok(buf[2])
        NB = 3 * DN // P
        ids = W.take(NB // 4)
        dve_names = [(s, b) for b in range(NB) for s in ("tap0", "tap1", "tap2", "tap3")]
        stage([x for b in range(NB + 1) for x in ([("block", b)] if b < NB else []) + ([("turned", b - 1)] if b else [])],
              [(s, b) for b in range(NB) for s in ("silu", "kept")], dve_names)
        conv_acc = [buf[3][:, i * S:(i + 1) * S] for i in range(2)]
        conv_out = [buf[3][:, (2 + i) * S:(3 + i) * S] for i in range(2)]
        with nc.Block() as block:
            @block.tensor
            def _(pe):
                def turn(b):
                    AC.wait(pe, ("silu", b))
                    if b >= 4:
                        AC.wait(pe, ("kept", b - 4))
                    for t in range(T):
                        last = nc.tensor.transpose(bank[4 + b % 4][:, t * P:(t + 1) * P], conv_out[b % 2][:, t * P:(t + 1) * P], ident[:, :])
                    PE.done(last, ("turned", b))
                for b in range(NB):
                    chunk = ids[b // 4]
                    if b % 4 == 0:
                        W.wait_landed(pe, chunk)
                    if b >= 4:
                        DV.wait(pe, ("tap3", b - 4))
                    w = W.slot(chunk)[:, :].rearrange("p (k n) -> p k n", k=KD)
                    for k in range(KD):
                        last = nc.tensor.matmul(bank[b % 4][:, :], w[:, k, (b % 4) * P:(b % 4 + 1) * P], featT[:, k, :],
                                                start=(k == 0), stop=(k == KD - 1))
                    PE.done(last, ("block", b))
                    if b % 4 == 3:
                        W.mark_used(chunk, PE.sem, PE.value(("block", b)))
                    if b:
                        turn(b - 1)
                turn(NB - 1)

            @block.vector
            def _(dve):
                for b in range(NB):
                    acc, src = conv_acc[b % 2], bank[b % 4]
                    PE.wait(dve, ("block", b))
                    if b >= 2:
                        AC.wait(dve, ("silu", b - 2))
                    DV.done(nc.vector.tensor_scalar(acc, src[:, :], conv_cols[:, CONV - 1, b:b + 1], None, ALU.mult), ("tap0", b))
                    for back in range(1, CONV):
                        DV.wait(dve, ("tap%d" % (back - 1), b))
                        DV.done(nc.vector.scalar_tensor_tensor(
                            out=acc[:, back:S], in0=src[:, 0:S - back], scalar=conv_cols[:, CONV - 1 - back, b:b + 1],
                            in1=acc[:, back:S], op0=ALU.mult, op1=ALU.add), ("tap%d" % back, b))

            @block.scalar
            def _(act):
                for b in range(NB):
                    DV.wait(act, ("tap3", b))
                    if b >= 2:
                        PE.wait(act, ("turned", b - 2))
                    AC.done(nc.scalar.activation(conv_out[b % 2], conv_acc[b % 2], ACT.Silu), ("silu", b))
                    PE.wait(act, ("turned", b))
                    dst = (q_tok, k_tok, vd_tok)[b // 8][:, :, (b % 8) * P:(b % 8 + 1) * P]
                    AC.done(nc.scalar.activation(dst, bank[4 + b % 4][:, :].rearrange("p (t n) -> p t n", t=T), ACT.Copy), ("kept", b))

            @block.gpsimd
            def _(pool):
                fills = [r_[i * P:(i + 1) * P, :] for r_ in (x_rows, y_rows) for i in range(N_MAIN + N_EXTRA)]
                for i, rows_ in enumerate(fills):
                    if i % 2 == 0:
                        PE.wait(pool, ("block", i // 2))
                    pool.dma_start(rows_, buf[6][:, 3 * DM:4 * DM]).then_inc(zero_filled, 16)

            @block.sync
            def _(sp):
                load(sp, ab_w, rows(w_in)[:, :, 4 * DN:UV_OFF])
                load(sp, small[:, 256:256 + H], D["a_log"].partition_broadcast(P))
                load(sp, small[:, 264:264 + H], D["dt_bias"].partition_broadcast(P))
                wait_loads(sp)
                W.issue(sp)

        sc = small
        decay_rate, dt_bias = sc[:, 256:256 + H], sc[:, 264:264 + H]
        TH = T * H
        a_in, g_all, beta_all, tmp_a, tmp_b = (sc[:, 288 + 32 * i:288 + 32 * (i + 1)] for i in range(5))
        ssq = [buf[6][:, 2048 + 32 * i:2048 + 32 * (i + 1)] for i in range(2)]
        square = [buf[3][:, 0:DM], buf[3][:, DM:2 * DM]]
        def th(a):
            return a.rearrange("p (t h) -> p t h", t=T)
        dv_names = (["dt", "neg", "low", "high", "rate", "g"] +
                    [(s, i, t) for t in range(T) for i in range(2) for s in ("square", "ssq")] +
                    [("eps", i) for i in range(2)] + [("unit", i, t) for t in range(T) for i in range(2)])
        ac_names = ["beta", "exp", "rate", "log"] + [(s, i) for i in range(2) for s in ("log", "inv")]
        stage(["ab"], ac_names, dv_names)
        with nc.Block() as block:
            @block.tensor
            def _(pe):
                for t in range(T):
                    for k in range(KD):
                        last = nc.tensor.matmul(bank[0][:, t * 2 * H:(t + 1) * 2 * H], featT[:, k, t * P:(t + 1) * P],
                                                ab_w[:, k, :], start=(k == 0), stop=(k == KD - 1))
                PE.done(last, "ab")

            @block.vector
            def _(dve):
                ab = bank[0][:, 0:T * 2 * H].rearrange("p (t n) -> p t n", t=T)
                PE.wait(dve, "ab")
                DV.done(nc.vector.tensor_tensor(th(a_in), ab[:, :, 0:H], bcast(dt_bias.unsqueeze(1), P, T, H), ALU.add), "dt")
                DV.wait(dve, "dt")
                DV.done(nc.vector.tensor_scalar(tmp_a, a_in, -1.0, None, ALU.mult), "neg")
                DV.wait(dve, "neg")
                DV.done(nc.vector.tensor_tensor(tmp_a, tmp_a, a_in, ALU.min), "low")
                DV.done(nc.vector.tensor_scalar(a_in, a_in, 0.0, None, ALU.max), "high")
                AC.wait(dve, "log")
                DV.wait(dve, "high")
                DV.done(nc.vector.tensor_tensor(tmp_b, tmp_b, a_in, ALU.add), "rate")
                DV.wait(dve, "rate")
                DV.done(nc.vector.scalar_tensor_tensor(out=th(g_all), in0=th(tmp_b), scalar=-1.0, in1=bcast(decay_rate.unsqueeze(1), P, T, H),
                                                       op0=ALU.mult, op1=ALU.mult), "g")
                for t in range(T):
                    for i, x in enumerate((q_tok, k_tok)):
                        if t:
                            DV.wait(dve, ("ssq", i, t - 1))
                        DV.done(nc.vector.tensor_tensor(square[i], x[:, t, :], x[:, t, :], ALU.mult), ("square", i, t))
                        DV.wait(dve, ("square", i, t))
                        DV.done(nc.vector.reduce_sum(ssq[i][:, t * H:(t + 1) * H], square[i].rearrange("p (h n) -> p h n", h=H), X_AXIS), ("ssq", i, t))
                for i in range(2):
                    DV.wait(dve, ("ssq", i, T - 1))
                    DV.done(nc.vector.tensor_scalar_add(ssq[i], ssq[i], EPS), ("eps", i))
                for t in range(T):
                    for i, x in enumerate((q_tok, k_tok)):
                        AC.wait(dve, ("inv", i))
                        v = x[:, t, :].rearrange("p (h n) -> p h n", h=H)
                        r = bcast(ssq[i][:, t * H:(t + 1) * H].unsqueeze(2), P, H, P)
                        if i == 0:
                            DV.done(nc.vector.scalar_tensor_tensor(out=v, in0=v, scalar=float(P) ** -0.5, in1=r, op0=ALU.mult, op1=ALU.mult), ("unit", i, t))
                        else:
                            DV.done(nc.vector.tensor_tensor(v, v, r, ALU.mult), ("unit", i, t))

            @block.scalar
            def _(act):
                ab = bank[0][:, 0:T * 2 * H].rearrange("p (t n) -> p t n", t=T)
                PE.wait(act, "ab")
                DV.wait(act, "dt")
                AC.done(nc.scalar.activation(th(beta_all), ab[:, :, H:2 * H], ACT.Sigmoid), "beta")
                DV.wait(act, "low")
                AC.done(nc.scalar.activation(tmp_b, tmp_a, ACT.Exp), "exp")
                AC.done(nc.scalar.activation(decay_rate, decay_rate, ACT.Exp), "rate")
                AC.wait(act, "rate")
                AC.done(nc.scalar.activation(tmp_b, tmp_b, ACT.Ln, bias=1.0), "log")
                for i in range(2):
                    DV.wait(act, ("eps", i))
                    AC.done(nc.scalar.activation(ssq[i], ssq[i], ACT.Ln), ("log", i))
                    AC.wait(act, ("log", i))
                    AC.done(nc.scalar.activation(ssq[i], ssq[i], ACT.Exp, scale=-0.5), ("inv", i))

            @block.gpsimd
            def _(pool):
                nc.gpsimd.memset(state[:, :], 0.0)

            @block.sync
            def _(sp):
                W.issue(sp)

        HH = H // 2
        heads = lambda a: a.rearrange("p (h n) -> p h n", h=H)
        qkbT = buf[3][:, 0:2048].rearrange("p (h i n) -> p h i n", h=H, i=2)
        kT, decT = heads(buf[3][:, 2048:3072]), heads(buf[3][:, 3072:4096])
        qk, negT, inv_t, inv = (heads(buf[5][:, i * DM:(i + 1) * DM]) for i in range(4))
        lev, kb, kd, vnew = (heads(buf[6][:, i * DM:(i + 1) * DM]) for i in range(4))
        gcol, gtot = sc[:, 448:456], sc[:, 456:464]
        e_g, e_tot, e_rest, b_eg = (sc[:, 464 + 8 * i:472 + 8 * i] for i in range(4))
        st_h = heads(state[:, :])
        LV = range(1, NL)
        halves = range(2)
        HU = 2
        units = range(H // HU)
        pe_n = (["sums", "qT", "kT", "kbT", "scores"] + [("t0", u) for u in units] +
                [(s, l, h) for l in LV for s in ("lev", "dinv") + (("turn",) if l < NL - 1 else ()) for h in units] +
                [(s, h) for s in ("ks", "qs") for h in halves] + [("vn", h) for h in halves] + [(s, h) for s in ("o", "s") for h in halves])
        ac_n = (["g", "e", "rest", "decay", ("qT", 0), ("qT", 1), ("kbT", 0), ("kbT", 1)] + [("t0", u) for u in units] +
                [(s, l, h) for l in LV for s in ("lev",) + (("turn",) if l < NL - 1 else ()) for h in units] + [("vn", h) for h in halves])
        dv_n = (["tg", "rest", "beg", ("diff", 0), ("diff", 1), "clip", ("kT", 0), ("kT", 1)] + [(s, i) for i in range(4) for s in ("qk", "neg")] +
                ["strict", "first", "eye"] + [("add", l, h) for l in LV for h in units] +
                [(s, h) for h in halves for s in ("rk", "r")] + [(s, h) for h in halves for s in ("oq", "o", "sg", "s")])
        po_n = ["kb", "vb", "kd", "causal"]
        stage(pe_n, ac_n, dv_n, po_n, rounds=T)
        b4 = lambda i: bank[i][:, :].rearrange("p (h n) -> p h n", h=HH)
        hs = lambda h: slice(HH * h, HH * h + HH)
        per_head = lambda a, n=H: bcast(a.unsqueeze(2), P, n, P)
        with nc.Block() as block:
            @block.tensor
            def _(pe):
                for c in range(T):
                    g_c = g_all[:, c * H:(c + 1) * H]
                    DV.wait(pe, "tg", c)
                    if c:
                        DV.wait(pe, ("s", 1), c - 1)
                    for h in halves:
                        nc.tensor.matmul(bank[h][:, :], ones[:, :], lev[:, hs(h), :], start=True, stop=True)
                    nc.tensor.matmul(bank[2][:, 0:H], tri[:, :], g_c, start=True, stop=True)
                    PE.done(nc.tensor.matmul(bank[2][:, H:2 * H], ones[:, :], g_c, start=True, stop=True), "sums")
                    for h in range(H):
                        last = nc.tensor.transpose(bank[3 + h // HH][:, (h % HH) * P:(h % HH + 1) * P], heads(q_tok[:, c, :])[:, h, :], ident[:, :])
                    PE.done(last, "qT")
                    for h in range(H):
                        last = nc.tensor.transpose(bank[5 + h // HH][:, (h % HH) * P:(h % HH + 1) * P], heads(k_tok[:, c, :])[:, h, :], ident[:, :])
                    PE.done(last, "kT")
                    PO.wait(pe, "kb", c)
                    DV.wait(pe, ("diff", 1), c)
                    for h in range(H):
                        last = nc.tensor.transpose(bank[h // HH][:, (h % HH) * P:(h % HH + 1) * P], kb[:, h, :], ident[:, :])
                    PE.done(last, "kbT")
                    AC.wait(pe, ("kbT", 1), c)
                    DV.wait(pe, ("kT", 1), c)
                    for h in range(H):
                        last = nc.tensor.matmul(bank[2 + h // 2][:, (h % 2) * 2 * P:(h % 2 + 1) * 2 * P], kT[:, h, :],
                                                qkbT[:, h, :, :], start=True, stop=True)
                    PE.done(last, "scores")
                    DV.wait(pe, "eye", c)
                    def unit(u, out, f, name):
                        for j in range(HU):
                            last = f(bank[out + u][:, j * P:(j + 1) * P], HU * u + j)
                        PE.done(last, name)
                    turn = lambda o, h: nc.tensor.transpose(o, inv_t[:, h, :], ident[:, :])
                    for u in units:
                        unit(u, 4, turn, ("t0", u))
                    for l in LV:
                        for u in units:
                            AC.wait(pe, ("turn", l - 1, u) if l > 1 else ("t0", u), c)
                            unit(u, 0, lambda o, h: nc.tensor.matmul(o, negT[:, h, :], inv[:, h, :], start=True, stop=True), ("lev", l, u))
                        for u in units:
                            AC.wait(pe, ("lev", l, u), c)
                            unit(u, 4, lambda o, h: nc.tensor.matmul(o, lev[:, h, :], inv_t[:, h, :], start=True, stop=True), ("dinv", l, u))
                        if l < NL - 1:
                            for u in units:
                                DV.wait(pe, ("add", l, u), c)
                                unit(u, 0, turn, ("turn", l, u))
                    DV.wait(pe, ("add", NL - 1, units[-1]), c)
                    for h in halves:
                        for j in range(HH):
                            last = nc.tensor.matmul(bank[h][:, j * P:(j + 1) * P], kT[:, HH * h + j, :], st_h[:, HH * h + j, :], start=True, stop=True)
                        PE.done(last, ("ks", h))
                    for h in halves:
                        for j in range(HH):
                            last = nc.tensor.matmul(bank[6 + h][:, j * P:(j + 1) * P], qkbT[:, HH * h + j, 0, :], st_h[:, HH * h + j, :], start=True, stop=True)
                        PE.done(last, ("qs", h))
                    for h in halves:
                        DV.wait(pe, ("r", h), c)
                        for j in range(HH):
                            last = nc.tensor.matmul(bank[2 + h][:, j * P:(j + 1) * P], inv_t[:, HH * h + j, :], kb[:, HH * h + j, :], start=True, stop=True)
                        PE.done(last, ("vn", h))
                    AC.wait(pe, ("vn", 1), c)
                    PO.wait(pe, "kd", c)
                    for h in halves:
                        for j in range(HH):
                            last = nc.tensor.matmul(bank[4 + h][:, j * P:(j + 1) * P], qk[:, HH * h + j, :], vnew[:, HH * h + j, :], start=True, stop=True)
                        PE.done(last, ("o", h))
                    for h in halves:
                        for j in range(HH):
                            last = nc.tensor.matmul(bank[h][:, j * P:(j + 1) * P], kd[:, HH * h + j, :], vnew[:, HH * h + j, :], start=True, stop=True)
                        PE.done(last, ("s", h))

            @block.scalar
            def _(act):
                for c in range(T):
                    PE.wait(act, "sums", c)
                    AC.done(nc.scalar.activation(sc[:, 448:464], bank[2][:, 0:2 * H], ACT.Copy), "g")
                    AC.wait(act, "g", c)
                    AC.done(nc.scalar.activation(sc[:, 464:480], sc[:, 448:464], ACT.Exp), "e")
                    DV.wait(act, "rest", c)
                    AC.done(nc.scalar.activation(e_rest, e_rest, ACT.Exp), "rest")
                    DV.wait(act, "clip", c)
                    AC.done(nc.scalar.activation(decT, decT, ACT.Exp), "decay")
                    PE.wait(act, "qT", c)
                    for h in halves:
                        AC.done(nc.scalar.activation(qkbT[:, hs(h), 0, :], b4(3 + h), ACT.Copy), ("qT", h))
                    PE.wait(act, "kbT", c)
                    for h in halves:
                        AC.done(nc.scalar.activation(qkbT[:, hs(h), 1, :], b4(h), ACT.Copy), ("kbT", h))
                    two = lambda i: bank[i][:, 0:HU * P].rearrange("p (h n) -> p h n", h=HU)
                    us = lambda u: slice(HU * u, HU * u + HU)
                    for u in units:
                        PE.wait(act, ("t0", u), c)
                        AC.done(nc.scalar.activation(inv[:, us(u), :], two(4 + u), ACT.Copy), ("t0", u))
                    for l in LV:
                        for u in units:
                            PE.wait(act, ("lev", l, u), c)
                            AC.done(nc.scalar.activation(lev[:, us(u), :], two(u), ACT.Copy), ("lev", l, u))
                        if l < NL - 1:
                            for u in units:
                                PE.wait(act, ("turn", l, u), c)
                                AC.done(nc.scalar.activation(inv[:, us(u), :], two(u), ACT.Copy), ("turn", l, u))
                    for h in halves:
                        PE.wait(act, ("vn", h), c)
                        AC.done(nc.scalar.activation(vnew[:, hs(h), :], b4(2 + h), ACT.Copy), ("vn", h))

            @block.vector
            def _(dve):
                for c in range(T):
                    g_c, be_c = g_all[:, c * H:(c + 1) * H], beta_all[:, c * H:(c + 1) * H]
                    o_c = heads(vd_tok[:, c, :])
                    DV.done(nc.vector.tensor_tensor(lev, bcast(tri[:, :].unsqueeze(1), P, H, P), per_head(g_c), ALU.mult), "tg")
                    AC.wait(dve, "e", c)
                    DV.done(nc.vector.tensor_tensor(e_rest, gtot, gcol, ALU.subtract), "rest")
                    DV.done(nc.vector.tensor_tensor(b_eg, e_g, be_c, ALU.mult), "beg")
                    for h in halves:
                        DV.done(nc.vector.tensor_tensor(decT[:, hs(h), :], b4(h), per_head(gcol[:, hs(h)], HH), ALU.subtract), ("diff", h))
                    DV.wait(dve, ("diff", 1), c)
                    DV.done(nc.vector.tensor_scalar(decT, decT, 0.0, None, ALU.min), "clip")
                    PE.wait(dve, "kT", c)
                    for h in halves:
                        DV.done(nc.vector.tensor_copy(kT[:, hs(h), :], b4(5 + h)), ("kT", h))
                    PE.wait(dve, "scores", c)
                    PO.wait(dve, "causal", c)
                    for i in range(4):
                        s4 = bank[2 + i][:, :].rearrange("p (h i n) -> p h i n", h=2, i=2)
                        two = slice(2 * i, 2 * i + 2)
                        DV.done(nc.vector.tensor_tensor(qk[:, two, :], s4[:, :, 0, :], decT[:, two, :], ALU.mult), ("qk", i))
                        DV.done(nc.vector.tensor_tensor(negT[:, two, :], s4[:, :, 1, :], decT[:, two, :], ALU.mult), ("neg", i))
                    DV.wait(dve, ("neg", 3), c)
                    DV.done(nc.vector.scalar_tensor_tensor(out=negT, in0=negT, scalar=-1.0, in1=bcast(strict[:, :].unsqueeze(1), P, H, P),
                                                           op0=ALU.mult, op1=ALU.mult), "strict")
                    DV.wait(dve, "strict", c)
                    DV.done(nc.vector.tensor_tensor(inv_t, negT, bcast(level_mask[:, 0, :].unsqueeze(1), P, H, P), ALU.mult), "first")
                    DV.wait(dve, "first", c)
                    DV.done(nc.vector.tensor_tensor(inv_t, inv_t, bcast(ident[:, :].unsqueeze(1), P, H, P), ALU.add), "eye")
                    for l in LV:
                        for u in units:
                            PE.wait(dve, ("dinv", l, u), c)
                            DV.done(nc.vector.copy_predicated(
                                inv_t[:, HU * u:HU * u + HU, :], bcast(level_mask[:, l, :].bitcast(I32).unsqueeze(1), P, HU, P),
                                bank[4 + u][:, 0:HU * P].rearrange("p (h n) -> p h n", h=HU)), ("add", l, u))
                    for h in halves:
                        PE.wait(dve, ("ks", h), c)
                        DV.done(nc.vector.tensor_tensor(kb[:, hs(h), :], b4(h), per_head(b_eg[:, hs(h)], HH), ALU.mult), ("rk", h))
                        DV.wait(dve, ("rk", h), c)
                        PO.wait(dve, "vb", c)
                        DV.done(nc.vector.tensor_tensor(kb[:, hs(h), :], o_c[:, hs(h), :], kb[:, hs(h), :], ALU.subtract), ("r", h))
                    for h in halves:
                        PE.wait(dve, ("qs", h), c)
                        DV.wait(dve, ("r", h), c)
                        DV.done(nc.vector.tensor_tensor(o_c[:, hs(h), :], b4(6 + h), per_head(e_g[:, hs(h)], HH), ALU.mult), ("oq", h))
                        PE.wait(dve, ("o", h), c)
                        DV.wait(dve, ("oq", h), c)
                        DV.done(nc.vector.tensor_tensor(o_c[:, hs(h), :], o_c[:, hs(h), :], b4(4 + h), ALU.add), ("o", h))
                        PE.wait(dve, ("s", h), c)
                        DV.done(nc.vector.tensor_tensor(st_h[:, hs(h), :], st_h[:, hs(h), :], per_head(e_tot[:, hs(h)], HH), ALU.mult), ("sg", h))
                        DV.wait(dve, ("sg", h), c)
                        DV.done(nc.vector.tensor_tensor(st_h[:, hs(h), :], st_h[:, hs(h), :], b4(h), ALU.add), ("s", h))

            @block.gpsimd
            def _(pool):
                for c in range(T):
                    be_c = beta_all[:, c * H:(c + 1) * H]
                    k_c, v_c = heads(k_tok[:, c, :]), heads(vd_tok[:, c, :])
                    if c:
                        PE.wait(pool, ("s", 1), c - 1)
                    PO.done(nc.gpsimd.tensor_tensor(kb, k_c, per_head(be_c), ALU.mult), "kb")
                    PO.done(nc.gpsimd.tensor_tensor(v_c, v_c, per_head(be_c), ALU.mult), "vb")
                    AC.wait(pool, "rest", c)
                    PO.done(nc.gpsimd.tensor_tensor(kd, k_c, per_head(e_rest), ALU.mult), "kd")
                    AC.wait(pool, "decay", c)
                    PO.done(nc.gpsimd.affine_select(out=decT, in_=decT, compare_op=ALU.is_ge, fill=0.0, base=0,
                                                    pattern=[[0, H], [1, P]], channel_multiplier=-1), "causal")

            @block.sync
            def _(sp):
                load(sp, sc[:, 128:256], D["dn_norm_g"].partition_broadcast(P))
                wait_loads(sp)
                W.issue(sp)

        def rms_stage(items, eps, scratch, then=None, at=0):
            jobs = [(i, t) for i in range(len(items)) for t in range(T)]
            nj = len(jobs)
            dv = [("ssq", j) for j in range(nj)] + [("eps", i) for i in range(len(items))]
            pool_gain = 1
            afters = [len(items[i][4](t, dry=True)) if items[i][4] else 0 for i, t in jobs]
            for j in range(nj + pool_gain):
                dv += [("unit", j)] if j < nj else []
                if j >= pool_gain:
                    dv += [("after", j - pool_gain, k) for k in range(afters[j - pool_gain])]
            stage((), [("square", j) for j in range(nj)] + [(s_, i) for s_ in ("log", "inv") for i in range(len(items))],
                  dv, [("gain", j) for j in range(nj)])
            cols = []
            for x, n, w, gain, after in items:
                cols.append((at, at + T * n))
                at += T * n
            all_of = [small[:, lo:hi] for lo, hi in cols]
            st = [all_of[i][:, items[i][1] * t:items[i][1] * (t + 1)] for i, t in jobs]
            wide = max(n * w for x, n, w, gain, after in items)
            sq = [scratch[:, (j % 2) * wide:(j % 2) * wide + items[i][1] * items[i][2]].rearrange("p (n w) -> p n w", n=items[i][1])
                  for j, (i, t) in enumerate(jobs)]
            with nc.Block() as block:
                @block.scalar
                def _(act):
                    for j, (i, t) in enumerate(jobs):
                        if j >= 2:
                            DV.wait(act, ("ssq", j - 2))
                        AC.done(nc.scalar.activation(sq[j], items[i][0](t), ACT.Square), ("square", j))
                    for i, a in enumerate(all_of):
                        DV.wait(act, ("eps", i))
                        AC.done(nc.scalar.activation(a, a, ACT.Ln), ("log", i))
                    for i, a in enumerate(all_of):
                        AC.wait(act, ("log", i))
                        AC.done(nc.scalar.activation(a, a, ACT.Exp, scale=-0.5), ("inv", i))

                @block.vector
                def _(dve):
                    for j in range(nj):
                        AC.wait(dve, ("square", j))
                        DV.done(nc.vector.reduce_sum(st[j], sq[j], X_AXIS), ("ssq", j))
                    for i, a in enumerate(all_of):
                        DV.wait(dve, ("ssq", T * i + T - 1))
                        DV.done(nc.vector.tensor_scalar(a, a, 1.0 / items[i][2], eps, ALU.mult, ALU.add), ("eps", i))
                    for j in range(nj + pool_gain):
                        if j < nj:
                            i, t = jobs[j]
                            x, n, w = items[i][0:3]
                            AC.wait(dve, ("inv", i))
                            DV.done(nc.vector.tensor_tensor(x(t), x(t), bcast(st[j].unsqueeze(2), P, n, w), ALU.mult), ("unit", j))
                        if j >= pool_gain and afters[j - pool_gain]:
                            g = j - pool_gain
                            i, t = jobs[g]
                            PO.wait(dve, ("gain", g))
                            for k, f in enumerate(items[i][4](t)):
                                if k:
                                    DV.wait(dve, ("after", g, k - 1))
                                elif g and afters[g - 1]:
                                    DV.wait(dve, ("after", g - 1, afters[g - 1] - 1))
                                DV.done(f(), ("after", g, k))

                @block.gpsimd
                def _(pool):
                    for j, (i, t) in enumerate(jobs):
                        x, n, w, gain, after = items[i]
                        DV.wait(pool, ("unit", j))
                        PO.done(nc.gpsimd.tensor_tensor(x(t), x(t), bcast(gain.unsqueeze(1), P, n, w), ALU.mult), ("gain", j))

                @block.sync
                def _(sp):
                    if then:
                        then(sp)
                        wait_loads(sp)
                    W.issue(sp)

        z_tok = q_tok
        project(featT, KD, [BANK] * 2, "act",
                lambda n, t, b, mid: nc.scalar.activation(z_tok[:, t, span(n)], b[:, :], ACT.Silu), pieces=12)

        def times_z(t, dry=False):
            return [lambda: nc.vector.tensor_tensor(vd_tok[:, t, :], vd_tok[:, t, :], z_tok[:, t, :], ALU.mult)]

        def ln1_loads(sp):
            load(sp, buf[6][:, 0:DM], D["ln1_g"].partition_broadcast(P))
            load(sp, buf[6][:, DM:2 * DM], D["ln1_b"].partition_broadcast(P))
        rms_stage([(lambda t: heads(vd_tok[:, t, :]), H, P, sc[:, 128:256], times_z)], EPS, buf[3][:, 0:2 * DM], then=ln1_loads)
        oT = buf[1][:, :].rearrange("p (k s) -> p k s", k=KD)
        transpose_stage(vd_tok, oT)
        project(featT, KD, [BANK] * 2, "act",
                lambda n, t, b, mid: nc.scalar.activation(gate[:, t, span(n)], b[:, :], ACT.Sigmoid), pieces=12)

        def add_gated(n, t, b, mid):
            mid(nc.vector.tensor_tensor(buf[3][:, 0:BANK], b[:, :], gate[:, t, span(n)], ALU.mult))
            return nc.vector.tensor_tensor(y_tok[:, t, span(n)], y_tok[:, t, span(n)], buf[3][:, 0:BANK], ALU.add)
        project(oT, KD, [BANK] * 2, "dve", add_gated, mids=1)
        yT = buf[0][:, :].rearrange("p (k s) -> p k s", k=KD)
        transpose_stage(y_tok, yT)

        def add_resid(n, t, b, mid):
            return nc.vector.scalar_tensor_tensor(out=resid[:, t, span(n)], in0=resid[:, t, span(n)], scalar=ALPHA, in1=b[:, :],
                                                  op0=ALU.mult, op1=ALU.add)
        project(yT, KD, [BANK] * 2, "dve", add_resid)
        layer_norm(resid, buf[6][:, 0:DM], buf[6][:, DM:2 * DM], LN_EPS, 128)

        step1 = lambda name: Steps(sem(name))
        M_xT, M_gu, M_hT, M_down = (step1("moe_" + n) for n in ("x_turned", "gate_up_sum", "h_turned", "down_sum"))
        M_keep = {"act": step1("moe_x_kept_act"), "dve": step1("moe_x_kept_dve")}
        M_silu, M_h, M_hkept = step1("moe_silu"), step1("moe_h"), step1("moe_h_kept")
        M_y = {"act": step1("moe_y_kept_act"), "dve": step1("moe_y_kept_dve")}
        M_all = [M_xT, M_gu, M_hT, M_down, *M_keep.values(), M_silu, M_h, M_hkept, *M_y.values()]
        x_landed, y_stored = [sem(f"moe_x_landed{i}") for i in range(2)], [sem(f"moe_y_stored{i}") for i in range(2)]
        scattered, gathered = sem("rows_scattered"), [sem(f"rows_gathered{i}") for i in range(4)]
        E_in, E_pe, E_act, E_dve, E_out = (sem("extra_" + n) for n in ("landed", "pe", "act", "dve", "stored"))
        moe_n = [0]
        e_idx = small[:, 496:512]

        WORK = 7 * 4096
        MOD = WORK - 6 * DM
        sh1, sc1, g1row, sh2, sc2, g2row = (work[:, MOD + i * DM:MOD + (i + 1) * DM] for i in range(6))
        ada_sum = work[:, MOD - 6 * DM:MOD]
        norm = [work[:, i * DM:(i + 1) * DM] for i in range(2)]
        N_MOD = 6 * DM // BANK
        B_ADA = 6 * DM // 4
        b_ada = work[:, 2 * DM:2 * DM + B_ADA]

        def modulation_loads(sp, l):
            for stored in ada_stored:
                sp.wait_ge(stored, 16 * PIECES * (l + 1) // 2)
            load(sp, ada_sum, ada_part[l])
            load(sp, norm[0], D["mix_norm_2"][l:l + 1, :].partition_broadcast(P))
            load(sp, norm[1], D["ffn_norm_2"][l:l + 1, :].partition_broadcast(P))
            for i in range(4):
                load(sp, b_ada[32 * i:32 * i + 1, :], D["b_ada_2"][l:l + 1, i * B_ADA:(i + 1) * B_ADA])

        def moe(gate_w, up_w, down_w, group_w, group_b, expert_w, expert_b, x_tok, xT, finish, then=None, mod=None):
            nth = moe_n[0]
            moe_n[0] += 1
            r = buf[3]
            rw = r[:, 0:KD * (NG + NE)].rearrange("p (k n) -> p k n", k=KD)
            nrt = NG + NE
            rb = r[:, 160:160 + nrt]
            def f(at, n):
                return r[:, at:at + n]
            lg = f(192, T * nrt).rearrange("p (t n) -> p t n", t=T)
            gm, gsum, gp, mx1, mx2, low1, dif, w1, w2 = (f(272 + T * i, T) for i in range(9))
            eq, val, goh, gexp, ing, oh1, oh2, masked = (f(320 + 16 * i, 16).rearrange("p (t n) -> p t n", t=T) for i in range(8))
            O1, O2, O, prod, rowf, big = (f(448 + 64 * i, 64) for i in range(6))
            t16 = lambda a: a.rearrange("p (t n) -> p t n", t=T)
            t44 = lambda a: a.rearrange("p (t g j) -> p t g j", t=T, g=NG)
            cnt, nx, incl, xbase, tabA, tabB = (f(832 + 16 * i, 16) for i in range(6))
            rowsf, cmpx, eidf = f(928, 2 * T), f(944, N_EXTRA * NE), f(1072, N_EXTRA + 1)
            rows_i = ismall[:, 0:2 * T]
            ctl = ismall[:, 2 * T:2 * T + N_EXTRA + 1]
            per_tile = lambda a, n=NG: bcast(a.unsqueeze(2), P, T, n)
            idx4 = bcast(e_idx[:, 0:PER].unsqueeze(1), P, T, PER)
            N_DVE = 52
            stage(["logits", "ranks"], ["gexp", "r"], links("route", N_DVE))
            with nc.Block() as block:
                @block.sync
                def _(sp):
                    sp.wait_ge(zero_filled, 16 * 2 * (N_MAIN + N_EXTRA))
                    load(sp, rw[:, :, 0:NG], rows(group_w))
                    load(sp, rw[:, :, NG:nrt], rows(expert_w))
                    load(sp, rb[:, 0:NG], group_b.partition_broadcast(P))
                    load(sp, rb[:, NG:nrt], expert_b.partition_broadcast(P))
                all_loads = loads[0]

                @block.tensor
                def _(pe):
                    pe.wait_ge(loaded, all_loads)
                    for t in range(T):
                        for k in range(KD):
                            last = nc.tensor.matmul(bank[0][:, t * nrt:(t + 1) * nrt], xT[:, k, t * P:(t + 1) * P], rw[:, k, :],
                                                    start=(k == 0), stop=(k == KD - 1))
                    PE.done(last, "logits")
                    DV.wait(pe, ("route", 29))
                    for t in range(T):
                        for s in range(t + 1):
                            nc.tensor.matmul(bank[1][:, t * NE:(t + 1) * NE], (strict if s == t else ones)[:, :], O[:, s * NE:(s + 1) * NE],
                                             start=(s == 0), stop=(s == t))
                    for s in range(T):
                        last = nc.tensor.matmul(bank[1][:, T * NE:(T + 1) * NE], ones[:, :], O[:, s * NE:(s + 1) * NE], start=(s == 0), stop=(s == T - 1))
                    PE.done(last, "ranks")

                @block.scalar
                def _(act):
                    DV.wait(act, ("route", 6))
                    AC.done(nc.scalar.activation(gexp, gexp, ACT.Exp), "gexp")
                    DV.wait(act, ("route", 22))
                    AC.done(nc.scalar.activation(dif, dif, ACT.Exp), "r")

                @block.vector
                def _(dve):
                    link = chain(DV, dve, "route")
                    V = nc.vector

                    def first_of(x, m):
                        link(V.reduce_max(m, x, X_AXIS))
                        link(V.tensor_tensor(eq, x, per_tile(m), ALU.is_equal))
                        link(V.scalar_tensor_tensor(out=val, in0=eq, scalar=-64.0, in1=idx4, op0=ALU.mult, op1=ALU.add))
                        link(V.tensor_reduce(low1, val, X_AXIS, ALU.min))
                    dve.wait_ge(loaded, all_loads)
                    PE.wait(dve, "logits")
                    link(V.tensor_tensor(lg, bank[0][:, 0:T * nrt].rearrange("p (t n) -> p t n", t=T), bcast(rb.unsqueeze(1), P, T, nrt), ALU.add))
                    first_of(lg[:, :, 0:NG], gm)
                    link(V.tensor_tensor(goh, val, per_tile(low1), ALU.is_equal))
                    link(V.tensor_tensor(gexp, lg[:, :, 0:NG], per_tile(gm), ALU.subtract))
                    link(V.tensor_tensor(t44(prod), lg[:, :, NG:nrt].rearrange("p t (g j) -> p t g j", g=NG),
                                         bcast(goh.unsqueeze(3), P, T, NG, PER), ALU.mult))
                    link(V.reduce_sum(ing, prod.rearrange("p (t g j) -> p t j g", t=T, g=NG), X_AXIS))
                    AC.wait(dve, "gexp")
                    link(V.reduce_sum(gsum, gexp, X_AXIS))
                    link(V.reciprocal(gp, gsum))
                    first_of(ing, mx1)
                    link(V.tensor_tensor(oh1, val, per_tile(low1), ALU.is_equal))
                    link(V.scalar_tensor_tensor(out=masked, in0=oh1, scalar=-1e30, in1=ing, op0=ALU.mult, op1=ALU.add))
                    first_of(masked, mx2)
                    link(V.tensor_tensor(oh2, val, per_tile(low1), ALU.is_equal))
                    link(V.tensor_tensor(dif, mx2, mx1, ALU.subtract))
                    AC.wait(dve, "r")
                    link(V.tensor_scalar_add(mx1, dif, 1.0))
                    link(V.reciprocal(mx1, mx1))
                    link(V.tensor_tensor(w1, gp, mx1, ALU.mult))
                    link(V.tensor_tensor(w2, w1, dif, ALU.mult))
                    g4, j4 = bcast(goh.unsqueeze(3), P, T, NG, PER), lambda a: bcast(a.unsqueeze(2), P, T, NG, PER)
                    link(V.tensor_tensor(t44(O1), g4, j4(oh1), ALU.mult))
                    link(V.tensor_tensor(t44(O2), g4, j4(oh2), ALU.mult))
                    link(V.tensor_tensor(O, O1, O2, ALU.add))
                    PE.wait(dve, "ranks")
                    link(V.tensor_copy(cnt, bank[1][:, T * NE:(T + 1) * NE]))
                    link(V.tensor_scalar(nx, cnt, float(P), None, ALU.is_gt))
                    for m in range(2, T):
                        link(V.scalar_tensor_tensor(out=nx, in0=cnt, scalar=float(P * m), in1=nx, op0=ALU.is_gt, op1=ALU.add))
                    link(V.tensor_tensor_scan(incl, ones[:, 0:NE], nx, 0.0, ALU.mult, ALU.add))
                    link(V.tensor_tensor(xbase, incl, nx, ALU.subtract))
                    link(V.tensor_scalar(tabA, e_idx, float(P), None, ALU.mult))
                    link(V.tensor_scalar(tabB, xbase, float(P), float(P * (N_MAIN - 1)), ALU.mult, ALU.add))
                    link(V.tensor_tensor(tabB, tabB, tabA, ALU.subtract))
                    ranks = t16(bank[1][:, 0:T * NE])
                    link(V.tensor_scalar(t16(big), ranks, float(P), None, ALU.is_ge))
                    link(V.tensor_tensor(t16(big), t16(big), bcast(tabB.unsqueeze(1), P, T, NE), ALU.mult))
                    link(V.tensor_tensor(t16(big), t16(big), bcast(tabA.unsqueeze(1), P, T, NE), ALU.add))
                    link(V.tensor_tensor(t16(rowf), t16(big), ranks, ALU.add))
                    for i, oo in enumerate((O1, O2)):
                        link(V.tensor_tensor(prod, oo, rowf, ALU.mult))
                        link(V.reduce_sum(rowsf[:, i * T:(i + 1) * T], t16(prod), X_AXIS))
                    link(V.tensor_copy(rows_i, rowsf))
                    c3 = cmpx.rearrange("p (x n) -> p x n", x=N_EXTRA)
                    link(V.tensor_tensor(c3, bcast(incl.unsqueeze(1), P, N_EXTRA, NE), bcast(e_idx[:, 0:N_EXTRA].unsqueeze(2), P, N_EXTRA, NE), ALU.is_le))
                    link(V.reduce_sum(eidf[:, 0:N_EXTRA], c3, X_AXIS))
                    link(V.tensor_copy(eidf[:, N_EXTRA:N_EXTRA + 1], incl[:, NE - 1:NE]))
                    link(V.tensor_copy(ctl, eidf))

                @block.gpsimd
                def _(pool):
                    DV.wait(pool, ("route", N_DVE - 5))
                    for t in range(T):
                        for i in range(2):
                            nc.gpsimd.indirect_dma_start(
                                out=x_rows[:, :], out_offset=bass.IndirectOffsetOnAxis(ap=rows_i[:, i * T + t:i * T + t + 1], axis=0),
                                in_=x_tok[:, t, :], in_offset=None).then_inc(scattered, 16)
                    pool.wait_ge(scattered, 16 * 2 * T * (nth + 1))

            half = lambda a, n: [a[:, i * n:(i + 1) * n] for i in range(2)]
            xg, xgT = half(r[:, 2048:4096], DM), [a.rearrange("p (k n) -> p k n", k=KD) for a in half(buf[1][:, 0:2048], DM)]
            act_g, h_tok = half(buf[1][:, 2048:2560], FF), half(buf[1][:, 2560:3072], FF)
            hT = [a.rearrange("p (k n) -> p k n", k=KF) for a in half(buf[1][:, 3072:3072 + 2 * KF * P], KF * P)]
            yg = half(buf[2][:, 0:2048], DM)
            w_gu = [ring[i][:, :].rearrange("p (k n) -> p k n", k=KD) for i in range(2)]
            w_dn = [ring[2 + i][:, 0:KF * DM].rearrange("p (k n) -> p k n", k=KF) for i in range(2)]
            ids = W.take(2 * NE)
            stage()
            for m in M_all:
                m.begin(["e"], NE)
                m.at = m.due
            v = lambda m, e: m.value("e", 0) + e
            land = lambda chunk, pair: W.ready[chunk] + (W.ready[chunk + 4] - W.ready[chunk]) * pair
            xl = 16 * NE // 2 * nth
            gr, ur, dr = (w.rearrange("e (k p) n -> p e k n", p=P) for w in (gate_w, up_w, down_w))

            def rounds(eng, body, lo, hi):
                with eng.Fori(lo // 2, hi // 2) as pair:
                    for par in range(2):
                        body(2 * pair + par, par, pair)

            def turn_x(eng, e, par, pair):
                eng.wait_ge(x_landed[par], 16 * (pair + 1) + xl)
                for h in range(2):
                    for j in range(4):
                        k = 4 * h + j
                        last = nc.tensor.transpose(bank[h][:, j * P:(j + 1) * P], xg[par][:, k * P:(k + 1) * P], ident[:, :])
                last.then_inc(M_xT.sem, 1)

            def gate_up(e, par):
                for k in range(KD):
                    last = nc.tensor.matmul(bank[2 + par][:, :], xgT[par][:, k, :], w_gu[par][:, k, :], start=(k == 0), stop=(k == KD - 1))
                last.then_inc(M_gu.sem, 1)

            def turn_h(e, par):
                for k in range(KF):
                    last = nc.tensor.transpose(bank[4][:, k * P:(k + 1) * P], h_tok[par][:, k * P:(k + 1) * P], ident[:, :])
                last.then_inc(M_hT.sem, 1)

            def down(e, par):
                for h in range(2):
                    for k in range(KF):
                        last = nc.tensor.matmul(bank[5 + h][:, :], hT[par][:, k, :], w_dn[par][:, k, span(h)], start=(k == 0), stop=(k == KF - 1))
                last.then_inc(M_down.sem, 1)

            def keep_x(par, h):
                out, src = xgT[par][:, 4 * h:4 * h + 4, :], bank[h][:, :].rearrange("p (j n) -> p j n", j=4)
                return nc.vector.tensor_copy(out, src) if h else nc.scalar.activation(out, src, ACT.Copy)

            def silu(par):
                return nc.scalar.activation(act_g[par], bank[2 + par][:, 0:FF], ACT.Silu)

            def times_up(par):
                return nc.vector.tensor_tensor(h_tok[par], act_g[par], bank[2 + par][:, FF:2 * FF], ALU.mult)

            def keep_h(par):
                return nc.vector.tensor_copy(hT[par], bank[4][:, 0:KF * P].rearrange("p (k n) -> p k n", k=KF))

            def keep_y(par, h):
                out = yg[par][:, span(h)]
                return nc.vector.tensor_copy(out, bank[5 + h][:, :]) if h else nc.scalar.activation(out, bank[5][:, :], ACT.Copy)

            with nc.Block() as block:
                @block.tensor
                def _(pe):
                    def body(e, par, pair, first=False, second=False, last=False):
                        before = pair if par else pair - 1
                        pe.wait_ge(W.landed[par], land(ids[2 * par], pair))
                        for m in M_keep.values():
                            pe.wait_ge(m.sem, v(m, e))
                        gate_up(e, par)
                        if not last:
                            turn_x(pe, e + 1, 1 - par, pair + 1 if par else pair)
                        if not first:
                            pe.wait_ge(W.landed[2 + 1 - par], land(ids[2 * (1 - par) + 1], before))
                            pe.wait_ge(M_hkept.sem, v(M_hkept, e - 1))
                            if not second:
                                for m in M_y.values():
                                    pe.wait_ge(m.sem, v(m, e - 2))
                            down(e - 1, 1 - par)
                        pe.wait_ge(M_h.sem, v(M_h, e))
                        turn_h(e, par)
                    turn_x(pe, 0, 0, 0)
                    body(0, 0, 0, first=True)
                    body(1, 1, 0, second=True)
                    rounds(pe, body, 2, NE - 2)
                    body(NE - 2, 0, NE // 2 - 1)
                    body(NE - 1, 1, NE // 2 - 1, last=True)
                    W.wait_landed(pe, ids[2 * NE - 1])
                    pe.wait_ge(M_hkept.sem, v(M_hkept, NE - 1))
                    for m in M_y.values():
                        pe.wait_ge(m.sem, v(m, NE - 2))
                    down(NE - 1, 1)
                    for i in range(2 * NE):
                        m = M_down if i % 2 else M_gu
                        W.mark_used(ids[i], m.sem, v(m, i // 2))

                @block.scalar
                def _(act):
                    def keep_y_act(e, par, pair, early=False):
                        act.wait_ge(M_down.sem, v(M_down, e))
                        if not early:
                            act.wait_ge(y_stored[par], 16 * pair + xl)
                        keep_y(par, 0).then_inc(M_y["act"].sem, 1)

                    def store_y(e, par):
                        for m in M_y.values():
                            act.wait_ge(m.sem, v(m, e))
                        act.dma_start(y_rows[bass.ds(e * P, P), :], yg[par]).then_inc(y_stored[par], 16)

                    def keep_x_act(e, par):
                        act.wait_ge(M_xT.sem, v(M_xT, e))
                        keep_x(par, 0).then_inc(M_keep["act"].sem, 1)

                    def load_gate_up(e, par):
                        for i, w in enumerate((gr, ur)):
                            act.dma_start(ring[par][:, :].rearrange("p (k g n) -> p k g n", k=KD, g=2)[:, :, i, :],
                                          w[:, bass.ds(e, 1), :, :].rearrange("p e k n -> p (e k) n")).then_inc(W.landed[par], 16)

                    def load_down(e, par):
                        act.dma_start(w_dn[par], dr[:, bass.ds(e, 1), :, :].rearrange("p e k n -> p (e k) n")).then_inc(W.landed[2 + par], 16)

                    def body(e, par, pair, first=False, free=False, no_y=False, tail=False, last=False):
                        act.wait_ge(M_gu.sem, v(M_gu, e))
                        if not free:
                            act.wait_ge(M_h.sem, v(M_h, e - 2))
                        silu(par).then_inc(M_silu.sem, 1)
                        if not tail:
                            load_gate_up(e + 2, par)
                        if not last:
                            keep_x_act(e + 1, 1 - par)
                        if not first:
                            keep_y_act(e - 1, 1 - par, pair if par else pair - 1, early=no_y)
                            if not last:
                                load_down(e + 1, 1 - par)
                        if not first:
                            store_y(e - 1, 1 - par)
                    keep_x_act(0, 0)
                    body(0, 0, 0, first=True, free=True)
                    body(1, 1, 0, free=True, no_y=True)
                    body(2, 0, 1, no_y=True)
                    body(3, 1, 1)
                    rounds(act, body, 4, NE - 2)
                    body(NE - 2, 0, NE // 2 - 1, tail=True)
                    body(NE - 1, 1, NE // 2 - 1, tail=True, last=True)
                    keep_y_act(NE - 1, 1, NE // 2 - 1)
                    store_y(NE - 1, 1)
                    for i in range(2):
                        act.wait_ge(y_stored[i], 16 * NE // 2 * (nth + 1))

                @block.vector
                def _(dve):
                    def keep_y_dve(e, par, pair, early=False):
                        dve.wait_ge(M_down.sem, v(M_down, e))
                        if not early:
                            dve.wait_ge(y_stored[par], 16 * pair + xl)
                        keep_y(par, 1).then_inc(M_y["dve"].sem, 1)

                    def keep_x_dve(e, par):
                        dve.wait_ge(M_xT.sem, v(M_xT, e))
                        keep_x(par, 1).then_inc(M_keep["dve"].sem, 1)

                    def body(e, par, pair, first=False, early=False, last=False):
                        dve.wait_ge(M_silu.sem, v(M_silu, e))
                        times_up(par).then_inc(M_h.sem, 1)
                        if not last:
                            keep_x_dve(e + 1, 1 - par)
                        if not first:
                            keep_y_dve(e - 1, 1 - par, pair if par else pair - 1, early=early)
                        dve.wait_ge(M_hT.sem, v(M_hT, e))
                        keep_h(par).then_inc(M_hkept.sem, 1)
                    keep_x_dve(0, 0)
                    body(0, 0, 0, first=True)
                    body(1, 1, 0, early=True)
                    body(2, 0, 1, early=True)
                    body(3, 1, 1)
                    rounds(dve, body, 4, NE - 2)
                    body(NE - 2, 0, NE // 2 - 1)
                    body(NE - 1, 1, NE // 2 - 1, last=True)
                    keep_y_dve(NE - 1, 1, NE // 2 - 1)

                @block.gpsimd
                def _(pool):
                    def load_x(e, par):
                        pool.dma_start(xg[par], x_rows[bass.ds(e * P, P), :]).then_inc(x_landed[par], 16)

                    load_x(0, 0)
                    load_x(1, 1)

                    def body(e, par, pair):
                        pool.wait_ge(M_xT.sem, v(M_xT, e - 2))
                        load_x(e, par)
                    rounds(pool, body, 2, NE)

                @block.sync
                def _(sp):
                    W.issue(sp)
                    assert W.issued == ids[4]
                    if mod is not None:
                        modulation_loads(sp, mod)

                    W.issued += 2 * NE - 4
                mod_loads = loads[0]

            stage()
            with nc.Block() as block:
                def extra(eng, body):
                    n = eng.value_load(ctl[0:1, N_EXTRA:N_EXTRA + 1], min_val=0, max_val=N_EXTRA)
                    with eng.If(n > 0):
                        with eng.Fori(0, n) as x:
                            body(x)
                    with eng.Else():
                        eng.nop()

                @block.tensor
                def _(pe):
                    def body(x):
                        pe.wait_ge(E_in, 64 * x + 64)
                        for h in range(2):
                            for j in range(4):
                                k = 4 * h + j
                                last = nc.tensor.transpose(bank[h][:, j * P:(j + 1) * P], xg[0][:, k * P:(k + 1) * P], ident[:, :])
                        last.then_inc(E_pe, 1)
                        pe.wait_ge(E_act, 3 * x + 1)
                        pe.wait_ge(E_dve, 4 * x + 1)
                        for k in range(KD):
                            last = nc.tensor.matmul(bank[2][:, :], xgT[0][:, k, :], w_gu[0][:, k, :], start=(k == 0), stop=(k == KD - 1))
                        last.then_inc(E_pe, 1)
                        pe.wait_ge(E_dve, 4 * x + 2)
                        for k in range(KF):
                            last = nc.tensor.transpose(bank[4][:, k * P:(k + 1) * P], h_tok[0][:, k * P:(k + 1) * P], ident[:, :])
                        last.then_inc(E_pe, 1)
                        pe.wait_ge(E_dve, 4 * x + 3)
                        for h in range(2):
                            for k in range(KF):
                                last = nc.tensor.matmul(bank[5 + h][:, :], hT[0][:, k, :], w_dn[0][:, k, span(h)], start=(k == 0), stop=(k == KF - 1))
                        last.then_inc(E_pe, 1)
                    extra(pe, body)

                @block.scalar
                def _(act):
                    def body(x):
                        e = act.value_load(ctl[0:1, bass.ds(x, 1)], min_val=0, max_val=NE - 1)
                        row = bass.ds(x * P + N_MAIN * P, P)
                        act.dma_start(xg[0], x_rows[row, :]).then_inc(E_in, 16)
                        for i, w in enumerate((gr, ur)):
                            act.dma_start(ring[0][:, :].rearrange("p (k g n) -> p k g n", k=KD, g=2)[:, :, i, :],
                                          w[:, bass.ds(e, 1), :, :].rearrange("p e k n -> p (e k) n")).then_inc(E_in, 16)
                        act.dma_start(w_dn[0], dr[:, bass.ds(e, 1), :, :].rearrange("p e k n -> p (e k) n")).then_inc(E_in, 16)
                        act.wait_ge(E_pe, 4 * x + 1)
                        keep_x(0, 0).then_inc(E_act, 1)
                        act.wait_ge(E_pe, 4 * x + 2)
                        silu(0).then_inc(E_act, 1)
                        act.wait_ge(E_pe, 4 * x + 4)
                        keep_y(0, 0).then_inc(E_act, 1)
                        act.wait_ge(E_act, 3 * x + 3)
                        act.wait_ge(E_dve, 4 * x + 4)
                        act.dma_start(y_rows[row, :], yg[0]).then_inc(E_out, 16)
                        act.wait_ge(E_out, 16 * x + 16)
                    extra(act, body)

                @block.vector
                def _(dve):
                    def body(x):
                        dve.wait_ge(E_pe, 4 * x + 1)
                        keep_x(0, 1).then_inc(E_dve, 1)
                        dve.wait_ge(E_act, 3 * x + 2)
                        times_up(0).then_inc(E_dve, 1)
                        dve.wait_ge(E_pe, 4 * x + 3)
                        keep_h(0).then_inc(E_dve, 1)
                        dve.wait_ge(E_pe, 4 * x + 4)
                        keep_y(0, 1).then_inc(E_dve, 1)
                    extra(dve, body)

            g_buf = [buf[2][:, 2048:3072], buf[2][:, 3072:4096], buf[1][:, 0:1024], buf[1][:, 1024:2048]]
            fin = finish(0, g_buf[0], g_buf[1], w1[:, 0:1], w2[:, 0:1])
            sums = range(N_MOD if mod is not None else 0)
            LIVE = N_MOD - DM // BANK
            stage([("sum", n) for n in sums], [("row", n) for n in sums],
                  ([("bias", i) for i in range(4)] if sums else []) + [("f", t, i) for t in range(T) for i in range(len(fin))]
                  + ([("scale", 0), ("scale", 1)] if sums else []))
            with nc.Block() as block:
                @block.tensor
                def _(pe):
                    if sums:
                        pe.wait_ge(loaded, mod_loads)
                    for n in sums:
                        DV.wait(pe, ("bias", n * BANK // B_ADA))
                        if n >= N_BANKS:
                            AC.wait(pe, ("row", n - N_BANKS))
                        PE.done(nc.tensor.matmul(bank[n % N_BANKS][:, :], ones[:, :], ada_sum[:, span(n)], start=True, stop=True), ("sum", n))

                @block.scalar
                def _(act):
                    for n in sums:
                        if n == LIVE:
                            DV.wait(act, ("f", T - 1, len(fin) - 1))
                        PE.wait(act, ("sum", n))
                        AC.done(nc.scalar.activation(work[:, MOD + n * BANK:MOD + (n + 1) * BANK], bank[n % N_BANKS][:, :], ACT.Copy), ("row", n))

                @block.gpsimd
                def _(pool):
                    for s in (E_in, E_pe, E_act, E_dve, E_out):
                        pool.sem_clear(s)
                    for t in range(T):
                        if t >= 2:
                            DV.wait(pool, ("f", t - 2, len(fin) - 1))
                        for i in range(2):
                            g = 2 * (t % 2) + i
                            nc.gpsimd.indirect_dma_start(
                                out=g_buf[g], out_offset=None, in_=y_rows[:, :],
                                in_offset=bass.IndirectOffsetOnAxis(ap=rows_i[:, i * T + t:i * T + t + 1], axis=0)).then_inc(gathered[g], 16)

                @block.vector
                def _(dve):
                    if sums:
                        dve.wait_ge(loaded, mod_loads)
                        for i in range(4):
                            part = ada_sum[32 * i:32 * i + 1, i * B_ADA:(i + 1) * B_ADA]
                            DV.done(nc.vector.tensor_tensor(part, part, b_ada[32 * i:32 * i + 1, :], ALU.add), ("bias", i))
                    for t in range(T):
                        g = 2 * (t % 2)
                        for i in range(2):
                            dve.wait_ge(gathered[g + i], 16 * (T // 2 * nth + t // 2 + 1))
                        for i, ins in enumerate(finish(t, g_buf[g], g_buf[g + 1], w1[:, t:t + 1], w2[:, t:t + 1])):
                            if i:
                                DV.wait(dve, ("f", t, i - 1))
                            DV.done(ins(), ("f", t, i))
                    if sums:
                        AC.wait(dve, ("row", LIVE - 1))
                        for i, a in enumerate((sc1, sc2)):
                            DV.done(nc.vector.scalar_tensor_tensor(out=a, in0=a, scalar=1.0, in1=norm[i], op0=ALU.add, op1=ALU.mult), ("scale", i))

                @block.sync
                def _(sp):
                    if then:
                        if sums:
                            sp.wait_ge(loaded, mod_loads)
                        then(sp)
                        wait_loads(sp)
                    W.issue(sp)

        def ln2_loads(sp):
            load(sp, buf[3][:, 2 * DM:3 * DM], D["ln2_g"].partition_broadcast(P))
            load(sp, buf[3][:, 3 * DM:4 * DM], D["ln2_b"].partition_broadcast(P))

        def finish_a(t, g1, g2, a, b):
            x = resid[:, t, :]
            return [lambda: nc.vector.tensor_scalar(x, x, ALPHA, None, ALU.mult),
                    lambda: nc.vector.scalar_tensor_tensor(out=x, in0=g1, scalar=a, in1=x, op0=ALU.mult, op1=ALU.add),
                    lambda: nc.vector.scalar_tensor_tensor(out=x, in0=g2, scalar=b, in1=x, op0=ALU.mult, op1=ALU.add)]

        transpose_stage(resid, featT)
        moe(D["expert_w_gate"][0], D["expert_w_up"][0], D["expert_w_down"][0], D["router_group_w"][0], D["router_group_b"],
            D["router_expert_w"][0], D["router_expert_b"], resid, featT, finish_a, then=ln2_loads, mod=0)
        layer_norm(resid, buf[3][:, 2 * DM:3 * DM], buf[3][:, 3 * DM:4 * DM], LN_EPS, 128)

        NHB = D["fox_b_f_2"].shape[1]
        T4 = lambda a, n: a.rearrange("p (t n) -> p t n", t=T)

        h_tok2 = T4(work[:, 0:T * DM], DM)

        def modulated(scale, shift, dma=None):
            ssq, inv = small[:, 0:T], small[:, T:2 * T]
            squares = [work[:, (4 + i) * DM:(5 + i) * DM] for i in range(T)]
            tiles = range(T)

            def prep(eng_name, eng):
                if eng_name == "act":
                    for t in tiles:
                        AC.done(nc.scalar.activation(squares[t], resid[:, t, :], ACT.Square, accum_out=ssq[:, t:t + 1]), ("square", t))
                    DV.wait(eng, "eps")
                    AC.done(nc.scalar.activation(inv, inv, ACT.Ln), "log")
                    AC.wait(eng, "log")
                    AC.done(nc.scalar.activation(inv, inv, ACT.Exp, scale=-0.5), "inv")
                elif eng_name == "dve":
                    AC.wait(eng, ("square", T - 1))
                    DV.done(nc.vector.tensor_scalar(inv, ssq, 1.0 / DM, EPS, ALU.mult, ALU.add), "eps")
                    AC.wait(eng, "inv")
                    for t in tiles:
                        DV.done(nc.vector.scalar_tensor_tensor(out=h_tok2[:, t, :], in0=resid[:, t, :], scalar=inv[:, t:t + 1], in1=scale,
                                                               op0=ALU.mult, op1=ALU.mult), ("scaled", t))
                else:
                    for t in tiles:
                        DV.wait(eng, ("scaled", t))
                        PO.done(nc.gpsimd.tensor_tensor(h_tok2[:, t, :], h_tok2[:, t, :], shift, ALU.add), ("shifted", t))
            transpose_stage(h_tok2, featT, dict(act=[("square", t) for t in tiles] + ["log", "inv"], dve=["eps"] + [("scaled", t) for t in tiles],
                                                pool=[("shifted", t) for t in tiles]),
                            prep, ready=(PO, ("shifted",)), dma=dma)

        def attention(dk, q_at, k_at, v_at, qT_at, scale, cumT=None):
            wq = NHB * dk
            q, k = (T4(work[:, a:a + T * wq], wq) for a in (q_at, k_at))
            v = T4(work[:, v_at:v_at + T * DM], DM)
            G = NHB // 2
            dkp = max(dk, 96)
            DVH = DM // NHB
            scr = featT[:, :, :].rearrange("p k s -> p (k s)")
            sx = [scr[:, i * BANK:(i + 1) * BANK] for i in (0, 1, 2, 7)]
            pT = [scr[:, (3 + i) * BANK:(4 + i) * BANK].rearrange("p (s n) -> p s n", s=T) for i in range(2)]
            cb = [scr[:, (5 + i) * BANK:(6 + i) * BANK] for i in range(2)]
            mx, rs = small[:, 64:128], small[:, 128:192]
            for grp in range(2):
                hd = range(G)
                turned = [work[0:dkp, qT_at + i * G * S:qT_at + (i + 1) * G * S].rearrange("p (h s) -> p h s", h=G) for i in range(2)]
                stage([("turn", i, h) for h in hd for i in range(2)], [("kept", 0, h) for h in hd], [("kept", 1, h) for h in hd])
                with nc.Block() as block:
                    @block.tensor
                    def _(pe):
                        for h in hd:
                            for i, x in enumerate((q, k)):
                                if h >= 4:
                                    (AC, DV)[i].wait(pe, ("kept", i, h - 4))
                                c = (grp * G + h) * dk
                                for t in range(T):
                                    last = nc.tensor.transpose(bank[2 * (h % 4) + i][0:dk, t * P:(t + 1) * P], x[:, t, c:c + dk], ident[:, :])
                                PE.done(last, ("turn", i, h))

                    @block.scalar
                    def _(act):
                        for h in hd:
                            PE.wait(act, ("turn", 0, h))
                            AC.done(nc.scalar.activation(turned[0][0:dk, h, :], bank[2 * (h % 4)][0:dk, :], ACT.Copy), ("kept", 0, h))

                    @block.vector
                    def _(dve):
                        for h in hd:
                            PE.wait(dve, ("turn", 1, h))
                            DV.done(nc.vector.tensor_copy(turned[1][0:dk, h, :], bank[2 * (h % 4) + 1][0:dk, :]), ("kept", 1, h))

                    @block.gpsimd
                    def _(pool):
                        if dkp > dk and grp == 0:
                            for i in range(2):
                                nc.gpsimd.memset(turned[i][dk:dkp, :, :], 0.0)

                units = [(h, t) for h in hd for t in range(T)]
                cum_at = {max(0, T * h - 1): h for h in hd}
                N = len(units)
                pe_n, cum = [], cumT is not None
                for i in range(N + 4):
                    if i < N:
                        pe_n += [("C", units[i][0])] if cum and units[i][1] == 0 else []
                        pe_n += [("S", i)]
                    pe_n += [("turn", i - 3)] if 3 <= i < N + 3 else []
                    pe_n += [("pv", i - 4)] if i >= 4 else []
                ac_n, dv_n = [], []
                for i in range(N + 1):
                    if i < N:
                        ac_n += [("C", cum_at[i])] if cum and i in cum_at else []
                        ac_n += [("exp", i)]
                    if i:
                        ac_n += [("pT", i - 1)]
                for i in range(N + 4):
                    if i < N:
                        dv_n += [("scaled", i)]
                    if 1 <= i <= N:
                        dv_n += [("neg", i - 1)]
                    if i >= 4:
                        dv_n += [("inv", i - 4), ("o", i - 4)]
                stage(pe_n, ac_n, dv_n, [("masked", i) for i in range(N)])
                with nc.Block() as block:
                    @block.tensor
                    def _(pe):
                        for i in range(N + 4):
                            if i < N:
                                h, t = units[i]
                                if cum and t == 0:
                                    if h >= 2:
                                        AC.wait(pe, ("C", h - 2))
                                    hg = grp * G + h
                                    PE.done(nc.tensor.matmul(bank[6 + h % 2][:, :], bcast(ident[:, hg:hg + 1], P, P), cumT, start=True, stop=True), ("C", h))
                                if i >= 2:
                                    DV.wait(pe, ("scaled", i - 2))
                                PE.done(nc.tensor.matmul(bank[i % 2][:, 0:(t + 1) * P], turned[0][:, h, t * P:(t + 1) * P],
                                                         turned[1][:, h, 0:(t + 1) * P], start=True, stop=True), ("S", i))
                            if 3 <= i < N + 3:
                                j = i - 3
                                AC.wait(pe, ("exp", j))
                                if j >= 2:
                                    AC.wait(pe, ("pT", j - 2))
                                for s in range(units[j][1] + 1):
                                    last = nc.tensor.transpose(bank[2 + j % 2][:, s * P:(s + 1) * P], sx[j % 4][:, s * P:(s + 1) * P], ident[:, :])
                                PE.done(last, ("turn", j))
                            if i >= 4:
                                j = i - 4
                                h, t = units[j]
                                AC.wait(pe, ("pT", j))
                                if j >= 2:
                                    DV.wait(pe, ("o", j - 2))
                                c = (grp * G + h) * DVH
                                for s in range(t + 1):
                                    last = nc.tensor.matmul(bank[4 + j % 2][:, 0:DVH], pT[j % 2][:, s, :], v[:, s, c:c + DVH], start=(s == 0), stop=(s == t))
                                PE.done(last, ("pv", j))

                    @block.scalar
                    def _(act):
                        for i in range(N + 1):
                            if i < N:
                                if cum and i in cum_at:
                                    h = cum_at[i]
                                    PE.wait(act, ("C", h))
                                    if h >= 2:
                                        DV.wait(act, ("scaled", 4 * (h - 2) + 3))
                                    AC.done(nc.scalar.activation(cb[h % 2], bank[6 + h % 2][:, :], ACT.Copy), ("C", h))
                                DV.wait(act, ("neg", i))
                                e = sx[i % 4][:, 0:(units[i][1] + 1) * P]
                                AC.done(nc.scalar.activation(e, e, ACT.Exp, bias=mx[:, i:i + 1], accum_out=rs[:, i:i + 1]), ("exp", i))
                            if i:
                                j = i - 1
                                n = units[j][1] + 1
                                PE.wait(act, ("turn", j))
                                if j >= 2:
                                    PE.wait(act, ("pv", j - 2))
                                AC.done(nc.scalar.activation(pT[j % 2][:, 0:n, :], bank[2 + j % 2][:, 0:n * P].rearrange("p (s n) -> p s n", s=n), ACT.Copy), ("pT", j))

                    @block.vector
                    def _(dve):
                        for i in range(N + 4):
                            if i < N:
                                h, t = units[i]
                                n = (t + 1) * P
                                PE.wait(dve, ("S", i))
                                if i >= 4:
                                    PE.wait(dve, ("turn", i - 4))
                                if cum:
                                    AC.wait(dve, ("C", h))
                                    DV.done(nc.vector.scalar_tensor_tensor(out=sx[i % 4][:, 0:n], in0=bank[i % 2][:, 0:n], scalar=scale, in1=cb[h % 2][:, 0:n],
                                                                           op0=ALU.mult, op1=ALU.subtract), ("scaled", i))
                                else:
                                    DV.done(nc.vector.tensor_scalar(sx[i % 4][:, 0:n], bank[i % 2][:, 0:n], scale, None, ALU.mult), ("scaled", i))
                            if 1 <= i <= N:
                                j = i - 1
                                PO.wait(dve, ("masked", j))
                                DV.done(nc.vector.reduce_max(mx[:, j:j + 1], sx[j % 4][:, 0:(units[j][1] + 1) * P], X_AXIS, negate=True), ("neg", j))
                            if i >= 4:
                                j = i - 4
                                h, t = units[j]
                                AC.wait(dve, ("exp", j))
                                DV.done(nc.vector.reciprocal(rs[:, j:j + 1], rs[:, j:j + 1]), ("inv", j))
                                PE.wait(dve, ("pv", j))
                                DV.wait(dve, ("inv", j))
                                c = (grp * G + h) * DVH
                                DV.done(nc.vector.tensor_scalar(k[:, t, c:c + DVH], bank[4 + j % 2][:, 0:DVH], rs[:, j:j + 1], None, ALU.mult), ("o", j))

                    @block.gpsimd
                    def _(pool):
                        for i, (h, t) in enumerate(units):
                            DV.wait(pool, ("scaled", i))
                            d = sx[i % 4][:, t * P:(t + 1) * P]
                            PO.done(nc.gpsimd.affine_select(out=d, in_=d, compare_op=ALU.is_ge, fill=-3.0e38, base=0, pattern=[[-1, P]], channel_multiplier=1), ("masked", i))

            oT2 = work[:, qT_at:qT_at + KD * S].rearrange("p (k s) -> p k s", k=KD)
            transpose_stage(k[:, :, 0:DM], oT2)
            return oT2

        def add_mixed(n, t, b, mid):
            mid(nc.vector.tensor_tensor(work[:, 0:BANK], b[:, :], g1row[:, span(n)], ALU.mult))
            return nc.vector.tensor_tensor(resid[:, t, span(n)], resid[:, t, span(n)], work[:, 0:BANK], ALU.add)

        def finish_b(t, g1, g2, a, b):
            x = resid[:, t, :]
            return [lambda: nc.vector.tensor_scalar(g1, g1, a, None, ALU.mult),
                    lambda: nc.vector.scalar_tensor_tensor(out=g1, in0=g2, scalar=b, in1=g1, op0=ALU.mult, op1=ALU.add),
                    lambda: nc.vector.tensor_tensor(g1, g1, g2row, ALU.mult),
                    lambda: nc.vector.tensor_tensor(x, x, g1, ALU.add)]

        def experts_b(l):
            modulated(sc2, sh2)
            moe(D["moe_w_gate_2"][l], D["moe_w_up_2"][l], D["moe_w_down_2"][l], D["moe_w_grp_2"][l], D["moe_b_grp_2"][l:l + 1, :],
                D["moe_w_rt_2"][l], D["moe_b_rt_2"][l:l + 1, :], h_tok2, featT, finish_b, mod=l + 1 if l == 0 else None)

        FD = DM // NHB
        modulated(sc1, sh1)
        qkv_f = [T4(work[:, i * 4096:(i + 1) * 4096], DM) for i in range(3)]
        project(featT, KD, [BANK] * 6, "act",
                lambda n, t, b, mid: nc.scalar.activation(qkv_f[n // 2][:, t, span(n % 2)], b[:, :], ACT.Copy), pieces=2 * PIECES - 60)
        F0 = 5 * 4096
        cumT = work[:, F0:F0 + S]
        wf = work[:, F0 + 512:F0 + 512 + KD * NHB].rearrange("p (k n) -> p k n", k=KD)
        bf = work[:, F0 + 640:F0 + 640 + NHB]
        f_in, f_abs, f_log, f_cum = (work[:, F0 + 672 + i * 64:F0 + 736 + i * 64] for i in range(4))
        stage(["f", "cum", "cumT"], ["exp", "log", "cum", "cumT"], ["in", "neg", "abs", "low", "f"], ["zero"])
        with nc.Block() as block:
            @block.sync
            def _(sp):
                load(sp, wf, rows(D["fox_w_in_2"][0])[:, :, 3 * DM:3 * DM + NHB])
                load(sp, bf, D["fox_b_f_2"].partition_broadcast(P))
                load(sp, small[:, 256:256 + FD], D["fox_q_norm_2"].partition_broadcast(P))
                load(sp, small[:, 320:320 + FD], D["fox_k_norm_2"].partition_broadcast(P))
                wait_loads(sp)
                W.issue(sp)
            f_loads = loads[0]

            @block.tensor
            def _(pe):
                pe.wait_ge(loaded, f_loads)
                for t in range(T):
                    for k in range(KD):
                        last = nc.tensor.matmul(bank[0][:, t * NHB:(t + 1) * NHB], featT[:, k, t * P:(t + 1) * P], wf[:, k, :], start=(k == 0), stop=(k == KD - 1))
                PE.done(last, "f")
                DV.wait(pe, "f")
                for t in range(T):
                    for s in range(t + 1):
                        last = nc.tensor.matmul(bank[1][:, t * NHB:(t + 1) * NHB], (tri if s == t else ones)[:, :], f_log[:, s * NHB:(s + 1) * NHB],
                                                start=(s == 0), stop=(s == t))
                PE.done(last, "cum")
                AC.wait(pe, "cum")
                for t in range(T):
                    last = nc.tensor.transpose(bank[2][0:NHB, t * P:(t + 1) * P], f_cum[:, t * NHB:(t + 1) * NHB], ident[:, :])
                PE.done(last, "cumT")

            @block.vector
            def _(dve):
                dve.wait_ge(loaded, f_loads)
                PE.wait(dve, "f")
                DV.done(nc.vector.tensor_tensor(T4(f_in, NHB), T4(bank[0][:, 0:T * NHB], NHB), bcast(bf.unsqueeze(1), P, T, NHB), ALU.add), "in")
                DV.wait(dve, "in")
                DV.done(nc.vector.tensor_scalar(f_abs, f_in, -1.0, None, ALU.mult), "neg")
                DV.wait(dve, "neg")
                DV.done(nc.vector.tensor_tensor(f_abs, f_abs, f_in, ALU.min), "abs")
                DV.done(nc.vector.tensor_scalar(f_in, f_in, 0.0, None, ALU.min), "low")
                AC.wait(dve, "log")
                DV.wait(dve, "low")
                DV.done(nc.vector.tensor_tensor(f_log, f_in, f_abs, ALU.subtract), "f")

            @block.scalar
            def _(act):
                DV.wait(act, "abs")
                AC.done(nc.scalar.activation(f_abs, f_abs, ACT.Exp), "exp")
                AC.wait(act, "exp")
                AC.done(nc.scalar.activation(f_abs, f_abs, ACT.Ln, bias=1.0), "log")
                PE.wait(act, "cum")
                AC.done(nc.scalar.activation(f_cum, bank[1][:, 0:T * NHB], ACT.Copy), "cum")
                PE.wait(act, "cumT")
                PO.wait(act, "zero")
                AC.done(nc.scalar.activation(cumT[0:NHB, :], bank[2][0:NHB, :], ACT.Copy), "cumT")

            @block.gpsimd
            def _(pool):
                PO.done(nc.gpsimd.memset(cumT, 0.0), "zero")

        hd_view = lambda x, w: (lambda t: x[:, t, 0:NHB * w].rearrange("p (h n) -> p h n", h=NHB))
        rms_stage([(hd_view(qkv_f[i], FD), NHB, FD, small[:, 256 + 64 * i:256 + 64 * i + FD], None) for i in range(2)],
                  EPS, work[:, 4 * 4096:4 * 4096 + 2 * DM])
        oT2 = attention(FD, 0, 4096, 8192, 3 * 4096, FD ** -0.5, cumT)
        project(oT2, KD, [BANK] * 2, "dve", add_mixed, mids=1)
        experts_b(0)

        QR, KR = D["mla_q_lat_norm_2"].shape[1], D["mla_kv_lat_norm_2"].shape[1]
        QK = D["mla_q_norm_2"].shape[1]
        LAT = D["mla_w_in_2"].shape[2]
        ROPE = LAT - QR - KR
        NOPE, HALF = QK - ROPE, ROPE // 2
        modulated(sc1, sh1)
        V0, QT0 = 2 * T * NHB * QK, 2 * T * NHB * QK + 4096
        lat = T4(work[:, QT0:QT0 + T * LAT], LAT)
        project(featT, KD, [BANK, LAT - BANK], "act",
                lambda n, t, b, mid: nc.scalar.activation(lat[:, t, n * BANK:min((n + 1) * BANK, LAT)], b[:, 0:min(BANK, LAT - n * BANK)], ACT.Copy))
        gq, gkv = work[:, V0:V0 + QR], work[:, V0 + QR:V0 + QR + KR]

        def lat_loads(sp):
            load(sp, gq, D["mla_q_lat_norm_2"].partition_broadcast(P))
            load(sp, gkv, D["mla_kv_lat_norm_2"].partition_broadcast(P))
            load(sp, small[:, 192:192 + QK], D["mla_q_norm_2"].partition_broadcast(P))
            load(sp, small[:, 288:288 + QK], D["mla_k_norm_2"].partition_broadcast(P))
            load(sp, pos_rows, D["positions_2"].rearrange("b (t p) -> (b t) p", p=P))

        pos_rows = work[0:T, 0:P].bitcast(I32)
        posf = work[0:T, P:2 * P]
        TR = T * HALF
        ang, turns, res, freq, cos, sin = (work[:, V0 + 704 + i * TR:V0 + 704 + (i + 1) * TR] for i in range(6))
        TWO_PI = 6.283185307179586
        C1 = 6.28125
        C2 = float(int((TWO_PI - C1) * 2 ** 21)) / 2 ** 21
        C3 = TWO_PI - C1 - C2
        PI_F = 3.1415925
        ROUND = 12582912.0
        stage(["pos"], ["sin"], links("rope", 13) + ["cos_in"], links("freq", HALF))
        with nc.Block() as block:
            @block.sync
            def _(sp):
                lat_loads(sp)
                wait_loads(sp)
                W.issue(sp)
            pos_loads = loads[0]

            @block.gpsimd
            def _(pool):
                link = chain(PO, pool, "freq")
                for i in range(HALF):
                    link(nc.gpsimd.memset(freq[:, i:i + 1], 10000.0 ** (-i / HALF)))

            @block.tensor
            def _(pe):
                DV.wait(pe, ("rope", 0))
                PE.done(nc.tensor.transpose(bank[0][:, 0:T], posf, ident[0:T, 0:T]), "pos")

            @block.vector
            def _(dve):
                link = chain(DV, dve, "rope")
                V = nc.vector
                dve.wait_ge(loaded, pos_loads)
                link(V.tensor_copy(posf, pos_rows))
                PE.wait(dve, "pos")
                link(V.tensor_copy(small[:, 0:T], bank[0][:, 0:T]))
                PO.wait(dve, ("freq", HALF - 1))
                link(V.tensor_tensor(T4(ang, HALF), bcast(small[:, 0:T].unsqueeze(2), P, T, HALF), bcast(freq[:, 0:HALF].unsqueeze(1), P, T, HALF), ALU.mult))
                link(V.tensor_scalar(turns, ang, 1.0 / TWO_PI, None, ALU.mult))
                link(V.tensor_scalar(turns, turns, ROUND, None, ALU.add))
                link(V.tensor_scalar(turns, turns, ROUND, None, ALU.subtract))
                for c in (C1, C2, C3):
                    link(V.scalar_tensor_tensor(out=ang, in0=turns, scalar=-c, in1=ang, op0=ALU.mult, op1=ALU.add))
                link(V.tensor_scalar(res, ang, TWO_PI / 4, None, ALU.add))
                link(V.tensor_scalar(turns, res, PI_F, -TWO_PI, ALU.is_gt, ALU.mult))
                link(V.tensor_tensor(res, res, turns, ALU.add))
                link(V.tensor_scalar(ang, ang, PI_F, -PI_F, ALU.min, ALU.max))
                DV.done(V.tensor_scalar(res, res, PI_F, -PI_F, ALU.min, ALU.max), "cos_in")

            @block.scalar
            def _(act):
                DV.wait(act, "cos_in")
                nc.scalar.activation(sin, ang, ACT.Sin)
                AC.done(nc.scalar.activation(cos, res, ACT.Sin), "sin")

        rms_stage([(lambda t: lat[:, t, 0:QR].unsqueeze(1), 1, QR, gq, None),
                   (lambda t: lat[:, t, QR:QR + KR].unsqueeze(1), 1, KR, gkv, None)], EPS, work[:, 0:2 * QR])
        latT = featT
        transpose_stage(lat, latT, blocks=(QR + KR) // P)

        q_m, k_m = (T4(work[:, i * T * NHB * QK:(i + 1) * T * NHB * QK], NHB * QK) for i in range(2))
        v_m = T4(work[:, V0:V0 + 4096], DM)
        rt = [work[:, MOD + i * NHB * HALF:MOD + (i + 1) * NHB * HALF].rearrange("p (h n) -> p h n", h=NHB) for i in range(4)]
        trig = [work[:, MOD + 1024 + i * TR:MOD + 1024 + (i + 1) * TR] for i in range(2)]
        krope = work[:, MOD + 1152:MOD + 1152 + T * ROPE]
        stage((), (), ["cos", "sin", "krope"])
        with nc.Block() as block:
            @block.vector
            def _(dve):
                DV.done(nc.vector.tensor_copy(trig[0], cos), "cos")
                DV.done(nc.vector.tensor_copy(trig[1], sin), "sin")
                DV.done(nc.vector.tensor_copy(T4(krope, ROPE), lat[:, :, QR + KR:LAT]), "krope")

        def rope_of(x):
            def after(t, dry=False):
                v = x[:, t, :].rearrange("p (h n) -> p h n", h=NHB)
                x1, x2 = v[:, :, NOPE:NOPE + HALF], v[:, :, NOPE + HALF:QK]
                c, s = (bcast(T4(a, HALF)[:, t, :].unsqueeze(1), P, NHB, HALF) for a in trig)
                tt = lambda o, a, b, op: (lambda: nc.vector.tensor_tensor(o, a, b, op))
                return [tt(rt[0], x1, c, ALU.mult), tt(rt[1], x2, s, ALU.mult), tt(rt[2], x1, s, ALU.mult), tt(rt[3], x2, c, ALU.mult),
                        tt(x1, rt[0], rt[1], ALU.subtract), tt(x2, rt[2], rt[3], ALU.add)]
            return after
        project(latT, QR // P, [BANK] * (NHB * QK // BANK), "act",
                lambda n, t, b, mid: nc.scalar.activation(q_m[:, t, span(n)], b[:, :], ACT.Copy))

        HPB = BANK // P

        def keys_values(n, t, b, mid):
            kv = b[:, :].rearrange("p (h n) -> p h n", h=HPB)
            kd_ = k_m[:, t, :].rearrange("p (h n) -> p h n", h=NHB)[:, n * HPB:(n + 1) * HPB, 0:NOPE]
            mid(nc.scalar.activation(kd_, kv[:, :, 0:NOPE], ACT.Copy))
            vd_ = v_m[:, t, :].rearrange("p (h n) -> p h n", h=NHB)[:, n * HPB:(n + 1) * HPB, :]
            return nc.scalar.activation(vd_, kv[:, :, NOPE:P], ACT.Copy)
        project(latT[:, QR // P:(QR + KR) // P, :], KR // P, [BANK] * 4, "act", keys_values, mids=1)
        stage((), (), [("krope", t) for t in range(T)])
        with nc.Block() as block:
            @block.vector
            def _(dve):
                for t in range(T):
                    DV.done(nc.vector.tensor_copy(k_m[:, t, :].rearrange("p (h n) -> p h n", h=NHB)[:, :, NOPE:QK],
                                                  bcast(T4(krope, ROPE)[:, t, :].unsqueeze(1), P, NHB, ROPE)), ("krope", t))
        rms_stage([(hd_view(q_m, QK), NHB, QK, small[:, 192:192 + QK], rope_of(q_m)),
                   (hd_view(k_m, QK), NHB, QK, small[:, 288:288 + QK], rope_of(k_m))], EPS, work[:, QT0:QT0 + 2 * NHB * QK])
        oT3 = attention(QK, 0, T * NHB * QK, V0, QT0, QK ** -0.5)
        project(oT3, KD, [BANK] * 2, "dve", add_mixed, mids=1)
        experts_b(1)

        stage()
        with nc.Block() as block:
            @block.sync
            def _(sp):
                stored = sem("stored")
                sp.dma_start(OUT[0].rearrange("(t p) n -> p t n", p=P), resid[:, :, :]).then_inc(stored, 16)
                sp.wait_ge(stored, 16)


def kernel(**inputs):
    import numpy as np
    import concourse.bacc as bacc
    from concourse.bass_utils import run_bass_kernel_spmd

    nc = bacc.Bacc("TRN2", target_bir_lowering=False, num_devices=1)
    arrays, dram = {}, {}
    for name, value in inputs.items():
        arrays["in_" + name] = np.ascontiguousarray(value)
        dram[name] = nc.dram_tensor("in_" + name, arrays["in_" + name].shape, mybir.dt.from_np(arrays["in_" + name].dtype),
                                    kind="ExternalInput").ap()
    out = nc.dram_tensor("out", inputs["x"].shape, F32, kind="ExternalOutput").ap()
    build(nc, dram, out)
    result = run_bass_kernel_spmd(nc, [arrays], core_ids=[0])
    return result.results[0]["out"]
```
